# Optimizing a Trainium2 kernel written in Bass

```python
import jax
import jax.numpy as jnp
from jax import lax
import numpy as np
import jax, jax.numpy as jnp

D_MODEL = 1024
BATCH = 1
SEQ = 256
DEPTH = 1

NORM_EPS = 1e-6
D_FF = 2816

ATTN_HEAD_DIM = 64
ATTN_HEADS_PER_GROUP = 4
ATTN_GROUPS = ((128, 1), (512, 4), (2048, 16))
N_ATTN_GROUPS = 3
ATTN_WIDTH = N_ATTN_GROUPS * ATTN_HEADS_PER_GROUP * ATTN_HEAD_DIM
ATTN_OUT_WIDTH = ATTN_HEADS_PER_GROUP * ATTN_HEAD_DIM
ROPE_THETA = 500000.0
ROPE_DIM = ATTN_HEAD_DIM // 4

RWKV_HEAD_DIM = 64
RWKV_WIDTH = D_MODEL
RWKV_HEADS = RWKV_WIDTH // RWKV_HEAD_DIM
DECAY_LORA = 64
ICLR_LORA = 64
GATE_LORA = 160
RWKV_GN_EPS = 64e-5
RWKV_STREAM = 3 * RWKV_WIDTH + DECAY_LORA + ICLR_LORA + GATE_LORA

IN_COLS = 3 * ATTN_WIDTH + RWKV_STREAM + 2 * D_MODEL


def rms_norm(x, gain):
    xf = x.astype(jnp.float32)
    y = xf * lax.rsqrt(jnp.mean(xf * xf, axis=-1, keepdims=True) + NORM_EPS)
    return (y * gain.astype(jnp.float32)).astype(x.dtype)

def swiglu(h, w_gate, w_up, w_down):
    return (jax.nn.silu(h @ w_gate) * (h @ w_up)) @ w_down

def partial_rope(x, positions):
    half = ROPE_DIM // 2
    inv_freq = jnp.power(ROPE_THETA, -jnp.arange(half, dtype=jnp.float32) * (2.0 / ROPE_DIM))
    ang = positions.astype(jnp.float32)[:, None] * inv_freq[None, :]
    cos = jnp.cos(ang)[None, :, None, :]
    sin = jnp.sin(ang)[None, :, None, :]
    xr = x[..., :ROPE_DIM].astype(jnp.float32)
    x1, x2 = xr[..., :half], xr[..., half:]
    rot = jnp.concatenate([x1 * cos - x2 * sin, x2 * cos + x1 * sin], axis=-1).astype(x.dtype)
    return jnp.concatenate([rot, x[..., ROPE_DIM:]], axis=-1)

def dilated_group(q, k, v, window, dilation):
    B, S, H, Dh = q.shape
    n = window // dilation
    L = S // dilation
    nb = -(-L // n)
    Lp = nb * n

    def to_sub(t):
        t = t.reshape(B, L, dilation, H, Dh).transpose(0, 2, 3, 1, 4)
        t = jnp.pad(t, ((0, 0), (0, 0), (0, 0), (0, Lp - L), (0, 0)))
        return t.reshape(B, dilation, H, nb, n, Dh)

    def with_prev(t):
        prev = jnp.pad(t, ((0, 0), (0, 0), (0, 0), (1, 0), (0, 0), (0, 0)))[:, :, :, :-1]
        return jnp.concatenate([prev, t], axis=4)

    def from_sub(t):
        t = t.reshape(B, dilation, H, Lp, t.shape[-1])[:, :, :, :L]
        return t.transpose(0, 3, 1, 2, 4).reshape(B, S, H, t.shape[-1])

    qb = to_sub(q)
    kw = with_prev(to_sub(k))
    vw = with_prev(to_sub(v))
    s = jnp.einsum('brhiqd,brhikd->brhiqk', qb, kw, preferred_element_type=jnp.float32)
    qi = jnp.arange(n)[:, None]
    ki = jnp.arange(2 * n)[None, :]
    rel = qi + n - ki
    band = (rel >= 0) & (rel <= n)
    blk = jnp.arange(nb)[:, None, None]
    valid = band[None] & ((blk > 0) | (ki[None] >= n))
    s = jnp.where(valid, s, -jnp.inf)
    m = jnp.max(s, axis=-1)
    p = jnp.exp(s - m[..., None])
    l = jnp.sum(p, axis=-1)
    acc = jnp.einsum('brhiqk,brhikd->brhiqd', p, vw.astype(jnp.float32))
    return from_sub(acc), from_sub(m[..., None])[..., 0], from_sub(l[..., None])[..., 0]

def dilated_attention(qkv, positions):
    B, S, _ = qkv.shape
    G, Hg, Dh = N_ATTN_GROUPS, ATTN_HEADS_PER_GROUP, ATTN_HEAD_DIM
    q, k, v = jnp.split(qkv, 3, axis=-1)
    q = partial_rope(q.reshape(B, S, G * Hg, Dh), positions) * (Dh ** -0.5)
    k = partial_rope(k.reshape(B, S, G * Hg, Dh), positions)
    v = v.reshape(B, S, G * Hg, Dh)
    accs, ms, ls = [], [], []
    for g, (window, dilation) in enumerate(ATTN_GROUPS):
        sl = slice(g * Hg, (g + 1) * Hg)
        acc, m, l = dilated_group(q[:, :, sl], k[:, :, sl], v[:, :, sl], window, dilation)
        accs.append(acc)
        ms.append(m)
        ls.append(l)
    m_all = jnp.stack(ms)
    c = jnp.exp(m_all - jnp.max(m_all, axis=0))
    num = jnp.sum(c[..., None] * jnp.stack(accs), axis=0)
    den = jnp.sum(c * jnp.stack(ls), axis=0)
    out = (num / den[..., None]).astype(qkv.dtype)
    return out.reshape(B, S, Hg * Dh)

def token_shift(z, mu):
    prev = jnp.pad(z, ((0, 0), (1, 0), (0, 0)))[:, :-1]
    return z + (prev - z) * mu

def wkv7_scan(r, w, k, v, a, b):
    B, S, H, N = r.shape

    def step(state, inp):
        r_t, w_t, k_t, v_t, a_t, b_t = inp
        sa = jnp.einsum('bhvk,bhk->bhv', state, a_t)
        state = (state * w_t[:, :, None, :] + sa[..., None] * b_t[:, :, None, :]
                 + v_t[..., None] * k_t[:, :, None, :])
        return state, jnp.einsum('bhvk,bhk->bhv', state, r_t)

    xs = tuple(jnp.moveaxis(t.astype(jnp.float32), 1, 0) for t in (r, w, k, v, a, b))
    _, ys = lax.scan(step, jnp.zeros((B, H, N, N), jnp.float32), xs)
    return jnp.moveaxis(ys, 0, 1)

def rwkv7_time_mix(z, w0, w2, a0, a2, g2, k_k, k_a, r_k, ln_w, ln_b, w_out):
    B, S, _ = z.shape
    RW, H, N = RWKV_WIDTH, RWKV_HEADS, RWKV_HEAD_DIM
    o1, o2, o3 = RW, 2 * RW, 3 * RW
    o4, o5 = o3 + DECAY_LORA, o3 + DECAY_LORA + ICLR_LORA
    r, k, v = z[..., :o1], z[..., o1:o2], z[..., o2:o3]
    zw, za, zg = z[..., o3:o4], z[..., o4:o5], z[..., o5:]
    logw = -jax.nn.softplus(-(w0 + jnp.tanh(zw) @ w2)) - 0.5
    decay = jnp.exp(-jnp.exp(logw.astype(jnp.float32)))
    a = jax.nn.sigmoid(a0 + za @ a2)
    g = jax.nn.sigmoid(zg) @ g2
    kk = (k * k_k).astype(jnp.float32).reshape(B, S, H, N)
    kk = kk / jnp.maximum(jnp.sqrt(jnp.sum(kk * kk, axis=-1, keepdims=True)), 1e-12)
    k = k * (1.0 + (a - 1.0) * k_a)
    rh = r.reshape(B, S, H, N).astype(jnp.float32)
    kh = k.reshape(B, S, H, N).astype(jnp.float32)
    vh = v.reshape(B, S, H, N).astype(jnp.float32)
    ah = a.reshape(B, S, H, N).astype(jnp.float32)
    y = wkv7_scan(rh, decay.reshape(B, S, H, N), kh, vh, -kk, kk * ah)
    mu = jnp.mean(y, axis=-1, keepdims=True)
    var = jnp.mean(jnp.square(y - mu), axis=-1, keepdims=True)
    yn = ((y - mu) * lax.rsqrt(var + RWKV_GN_EPS)).reshape(B, S, RW)
    yn = yn * ln_w.astype(jnp.float32) + ln_b.astype(jnp.float32)
    bonus = (jnp.sum(rh * kh * r_k.astype(jnp.float32), axis=-1, keepdims=True) * vh).reshape(B, S, RW)
    return ((yn + bonus) * g.astype(jnp.float32)).astype(z.dtype) @ w_out

def hybrid_mixer(h, positions, w_in, gate_bias, attn_w_up, rwkv_mu, rwkv_w0, rwkv_w2, rwkv_a0,
                 rwkv_a2, rwkv_g2, rwkv_k_k, rwkv_k_a, rwkv_r_k, rwkv_ln_w, rwkv_ln_b,
                 rwkv_w_out, w_o):
    proj = h @ w_in
    aw, rs = 3 * ATTN_WIDTH, RWKV_STREAM
    gates = jax.nn.sigmoid(proj[..., aw + rs:] + gate_bias)
    y_attn = dilated_attention(proj[..., :aw], positions) @ attn_w_up
    y_rwkv = rwkv7_time_mix(token_shift(proj[..., aw:aw + rs], rwkv_mu), rwkv_w0, rwkv_w2,
                            rwkv_a0, rwkv_a2, rwkv_g2, rwkv_k_k, rwkv_k_a, rwkv_r_k,
                            rwkv_ln_w, rwkv_ln_b, rwkv_w_out)
    merged = gates[..., :D_MODEL] * y_attn + gates[..., D_MODEL:] * y_rwkv
    return merged @ w_o

def first_inputs(seed: int = 0) -> dict:
    key = jax.random.key(seed)
    ks = iter(jax.random.split(key, 40))
    f32 = jnp.float32

    def nrm(shape, scale):
        return jax.random.normal(next(ks), shape, f32) * scale

    def gain(shape):
        return 1.0 + 0.05 * jax.random.normal(next(ks), shape, f32)

    L, D, F = DEPTH, D_MODEL, D_FF
    RW, H, N = RWKV_WIDTH, RWKV_HEADS, RWKV_HEAD_DIM
    return {
        'x': nrm((BATCH, SEQ, D), 1.0),
        'ffn1_norm': gain((L, D)),
        'ffn1_w_gate': nrm((L, D, F), D ** -0.5),
        'ffn1_w_up': nrm((L, D, F), D ** -0.5),
        'ffn1_w_down': nrm((L, F, D), F ** -0.5),
        'mix_norm': gain((L, D)),
        'w_in': nrm((L, D, IN_COLS), D ** -0.5),
        'gate_bias': nrm((L, 2 * D), 0.1),
        'attn_w_up': nrm((L, ATTN_OUT_WIDTH, D), ATTN_OUT_WIDTH ** -0.5),
        'rwkv_mu': jax.random.uniform(next(ks), (L, RWKV_STREAM), f32),
        'rwkv_w0': jax.random.uniform(next(ks), (L, RW), f32, -6.0, -1.0),
        'rwkv_w2': nrm((L, DECAY_LORA, RW), 0.1 * DECAY_LORA ** -0.5),
        'rwkv_a0': nrm((L, RW), 0.1),
        'rwkv_a2': nrm((L, ICLR_LORA, RW), 0.1 * ICLR_LORA ** -0.5),
        'rwkv_g2': nrm((L, GATE_LORA, RW), GATE_LORA ** -0.5),
        'rwkv_k_k': 0.85 + 0.05 * jax.random.normal(next(ks), (L, RW), f32),
        'rwkv_k_a': gain((L, RW)),
        'rwkv_r_k': nrm((L, H, N), 0.1),
        'rwkv_ln_w': gain((L, RW)),
        'rwkv_ln_b': nrm((L, RW), 0.02),
        'rwkv_w_out': nrm((L, RW, D), RW ** -0.5),
        'w_o': nrm((L, D, D), D ** -0.5),
        'ffn2_norm': gain((L, D)),
        'ffn2_w_gate': nrm((L, D, F), D ** -0.5),
        'ffn2_w_up': nrm((L, D, F), D ** -0.5),
        'ffn2_w_down': nrm((L, F, D), F ** -0.5),
        'final_norm': gain((D,)),
    }

def first_block(x, ffn1_norm, ffn1_w_gate, ffn1_w_up, ffn1_w_down, mix_norm, w_in, gate_bias,
              attn_w_up, rwkv_mu, rwkv_w0, rwkv_w2, rwkv_a0, rwkv_a2, rwkv_g2, rwkv_k_k,
              rwkv_k_a, rwkv_r_k, rwkv_ln_w, rwkv_ln_b, rwkv_w_out, w_o, ffn2_norm,
              ffn2_w_gate, ffn2_w_up, ffn2_w_down, final_norm):
    positions = jnp.arange(x.shape[1], dtype=jnp.int32)
    for layer in range(DEPTH):
        x = x + 0.5 * swiglu(rms_norm(x, ffn1_norm[layer]), ffn1_w_gate[layer],
                             ffn1_w_up[layer], ffn1_w_down[layer])
        x = x + hybrid_mixer(rms_norm(x, mix_norm[layer]), positions, w_in[layer],
                             gate_bias[layer], attn_w_up[layer], rwkv_mu[layer],
                             rwkv_w0[layer], rwkv_w2[layer], rwkv_a0[layer], rwkv_a2[layer],
                             rwkv_g2[layer], rwkv_k_k[layer], rwkv_k_a[layer],
                             rwkv_r_k[layer], rwkv_ln_w[layer], rwkv_ln_b[layer],
                             rwkv_w_out[layer], w_o[layer])
        x = x + 0.5 * swiglu(rms_norm(x, ffn2_norm[layer]), ffn2_w_gate[layer],
                             ffn2_w_up[layer], ffn2_w_down[layer])
    return rms_norm(x, final_norm)


DEPTH_2 = 2

CHUNK = 64
Q_BLOCK = 128
HEAD_DIM = 64
D_MIX = D_MODEL
A_HEADS = 6
A_LEFT_CHUNKS = 8
A_REL_MAX = 128
A_NUM_REL = CHUNK + A_REL_MAX
B_HEADS = 5
IDX_HEADS = 8
IDX_DIM = 32
TOPK_MAX = 256
C_HEADS = 5
C_Q_RANK = 384
C_KV_RANK = 256
C_NOPE = 64
C_ROPE = 32
C_V = 64
ROPE_THETA_2 = 10000.0
EPS = 1e-6
NEG = -1e30

A_W = A_HEADS * HEAD_DIM
B_W = B_HEADS * HEAD_DIM
C_W = C_HEADS * C_V
IN_SIZES = (A_W, A_W, A_W, B_W, B_W, B_W, IDX_HEADS * IDX_DIM, IDX_DIM, IDX_HEADS,
            C_Q_RANK, C_KV_RANK, C_ROPE)
D_IN = 3 * A_W + 3 * B_W + IDX_HEADS * IDX_DIM + IDX_DIM + IDX_HEADS + C_Q_RANK + C_KV_RANK + C_ROPE


def rmsnorm(x, g):
    x32 = x.astype(jnp.float32)
    y = x32 * lax.rsqrt(jnp.mean(x32 * x32, axis=-1, keepdims=True) + EPS)
    return (y * g.astype(jnp.float32)).astype(x.dtype)

def rope(x, pos):
    d = x.shape[-1]
    inv = ROPE_THETA_2 ** (-jnp.arange(0, d, 2, dtype=jnp.float32) / d)
    ang = pos.astype(jnp.float32)[:, None] * inv[None, :]
    cos = jnp.cos(ang)[:, None, :]
    sin = jnp.sin(ang)[:, None, :]
    x32 = x.astype(jnp.float32)
    x1, x2 = x32[..., : d // 2], x32[..., d // 2:]
    return jnp.concatenate([x1 * cos - x2 * sin, x1 * sin + x2 * cos], axis=-1).astype(x.dtype)

def swiglu_2(x, w_gate, w_up, w_down):
    return (jax.nn.silu(x @ w_gate) * (x @ w_up)) @ w_down

def sweep_query_blocks(fn, bsz, seq):
    out = lax.map(fn, jnp.arange(seq // Q_BLOCK) * Q_BLOCK)
    return jnp.moveaxis(out, 0, 1).reshape(bsz, seq, -1)

def chunk_relpos_attention(q, k, v, rel_bias):
    bsz, seq, h, d = q.shape
    nc = seq // CHUNK
    nb = A_LEFT_CHUNKS + 1
    pad = A_LEFT_CHUNKS * CHUNK
    qc = q.reshape(bsz, nc, CHUNK, h, d)
    kp = jnp.pad(k, ((0, 0), (pad, 0), (0, 0), (0, 0))).reshape(bsz, nc + A_LEFT_CHUNKS, CHUNK, h, d)
    vp = jnp.pad(v, ((0, 0), (pad, 0), (0, 0), (0, 0))).reshape(bsz, nc + A_LEFT_CHUNKS, CHUNK, h, d)
    kb = jnp.stack([kp[:, j:j + nc] for j in range(nb)], axis=2).reshape(bsz, nc, nb * CHUNK, h, d)
    vb = jnp.stack([vp[:, j:j + nc] for j in range(nb)], axis=2).reshape(bsz, nc, nb * CHUNK, h, d)
    s = jnp.einsum('bcqhd,bckhd->bhcqk', qc, kb).astype(jnp.float32) * (d ** -0.5)
    qi = jnp.arange(CHUNK)[:, None]
    ki = jnp.arange(nb * CHUNK)[None, :]
    rel = pad + qi - ki
    ridx = jnp.clip(rel, -(CHUNK - 1), A_REL_MAX) + (CHUNK - 1)
    bias = rel_bias.astype(jnp.float32)[:, ridx]
    valid = (jnp.arange(nc)[:, None] + ki // CHUNK - A_LEFT_CHUNKS) >= 0
    s = jnp.where(valid[None, None, :, None, :], s + bias[None, :, None], NEG)
    p = jax.nn.softmax(s, axis=-1).astype(v.dtype)
    o = jnp.einsum('bhcqk,bckhd->bcqhd', p, vb)
    return o.reshape(bsz, seq, h * d)

def dsa_attention(q, k, v, q_idx, k_idx, w_idx):
    bsz, seq, h, d = q.shape
    topk = min(TOPK_MAX, seq // 4)
    kchunk = jnp.arange(seq) // CHUNK
    gather = jax.vmap(lambda kk, ii: kk[ii])

    def block(q0):
        tc = (q0 + jnp.arange(Q_BLOCK)) // CHUNK
        qi = lax.dynamic_slice_in_dim(q_idx, q0, Q_BLOCK, axis=1)
        wi = lax.dynamic_slice_in_dim(w_idx, q0, Q_BLOCK, axis=1).astype(jnp.float32) * (IDX_HEADS ** -0.5)
        qb = lax.dynamic_slice_in_dim(q, q0, Q_BLOCK, axis=1)
        dots = jnp.einsum('bqhd,bsd->bqhs', qi, k_idx).astype(jnp.float32) * (IDX_DIM ** -0.5)
        score = jnp.einsum('bqh,bqhs->bqs', wi, jax.nn.relu(dots))
        adm = kchunk[None, :] <= tc[:, None]
        score = jnp.where(adm[None], score, NEG)
        _, idx = lax.top_k(score, topk)
        ksel = gather(k, idx)
        vsel = gather(v, idx)
        valid = (idx // CHUNK) <= tc[None, :, None]
        s = jnp.einsum('bqhd,bqkhd->bhqk', qb, ksel).astype(jnp.float32) * (d ** -0.5)
        s = jnp.where(valid[:, None], s, NEG)
        p = jax.nn.softmax(s, axis=-1).astype(v.dtype)
        return jnp.einsum('bhqk,bqkhd->bqhd', p, vsel)

    return sweep_query_blocks(block, bsz, seq)

def mla_attention(c_q, c_kv, k_rope, q_norm, kv_norm, w_uq, w_ukv, pos):
    bsz, seq, _ = c_q.shape
    q = (rmsnorm(c_q, q_norm) @ w_uq).reshape(bsz, seq, C_HEADS, C_NOPE + C_ROPE)
    qn, qr = q[..., :C_NOPE], rope(q[..., C_NOPE:], pos)
    kv = (rmsnorm(c_kv, kv_norm) @ w_ukv).reshape(bsz, seq, C_HEADS, C_NOPE + C_V)
    kn, v = kv[..., :C_NOPE], kv[..., C_NOPE:]
    kr = rope(k_rope[:, :, None, :], pos)[:, :, 0, :]
    kchunk = pos // CHUNK
    scale = (C_NOPE + C_ROPE) ** -0.5

    def block(q0):
        tc = (q0 + jnp.arange(Q_BLOCK)) // CHUNK
        qnb = lax.dynamic_slice_in_dim(qn, q0, Q_BLOCK, axis=1)
        qrb = lax.dynamic_slice_in_dim(qr, q0, Q_BLOCK, axis=1)
        s = (jnp.einsum('bqhd,bshd->bhqs', qnb, kn) + jnp.einsum('bqhr,bsr->bhqs', qrb, kr)).astype(jnp.float32) * scale
        s = jnp.where((kchunk[None, :] <= tc[:, None])[None, None], s, NEG)
        p = jax.nn.softmax(s, axis=-1).astype(v.dtype)
        return jnp.einsum('bhqs,bshd->bqhd', p, v)

    return sweep_query_blocks(block, bsz, seq)

def split_columns(h):
    parts, off = [], 0
    for size in IN_SIZES:
        parts.append(h[..., off:off + size])
        off += size
    return parts

def hybrid_layer(x, pos, ffn1_norm, ffn1_w_gate, ffn1_w_up, ffn1_w_down, mix_norm, w_in, a_rel_bias,
                 c_q_norm, c_kv_norm, c_w_uq, c_w_ukv, w_out, ffn2_norm, ffn2_w_gate, ffn2_w_up, ffn2_w_down):
    bsz, seq, _ = x.shape
    x = x + 0.5 * swiglu_2(rmsnorm(x, ffn1_norm), ffn1_w_gate, ffn1_w_up, ffn1_w_down)
    h = rmsnorm(x, mix_norm) @ w_in
    (a_q, a_k, a_v, b_q, b_k, b_v, i_q, i_k, i_w, c_q, c_kv, c_kr) = split_columns(h)
    hd4 = lambda t, nh: t.reshape(bsz, seq, nh, -1)
    o_a = chunk_relpos_attention(hd4(a_q, A_HEADS), hd4(a_k, A_HEADS), hd4(a_v, A_HEADS), a_rel_bias)
    o_b = dsa_attention(rope(hd4(b_q, B_HEADS), pos), rope(hd4(b_k, B_HEADS), pos), hd4(b_v, B_HEADS),
                        rope(hd4(i_q, IDX_HEADS), pos), rope(i_k[:, :, None, :], pos)[:, :, 0, :], i_w)
    o_c = mla_attention(c_q, c_kv, c_kr, c_q_norm, c_kv_norm, c_w_uq, c_w_ukv, pos)
    x = x + jnp.concatenate([o_a, o_b, o_c], axis=-1) @ w_out
    x = x + 0.5 * swiglu_2(rmsnorm(x, ffn2_norm), ffn2_w_gate, ffn2_w_up, ffn2_w_down)
    return x

def second_inputs(seed: int = 0) -> dict:
    key = jax.random.key(seed)
    ks = jax.random.split(key, 20)
    f32 = jnp.float32

    def nrm(k, shape, scale):
        return jax.random.normal(k, shape, f32) * scale

    def gain(k, n):
        return 1.0 + 0.02 * jax.random.normal(k, (DEPTH_2, n), f32)

    return {
        "x": jax.random.normal(ks[0], (BATCH, SEQ, D_MODEL), f32),
        "ffn1_norm": gain(ks[1], D_MODEL),
        "ffn1_w_gate": nrm(ks[2], (DEPTH_2, D_MODEL, D_FF), D_MODEL ** -0.5),
        "ffn1_w_up": nrm(ks[3], (DEPTH_2, D_MODEL, D_FF), D_MODEL ** -0.5),
        "ffn1_w_down": nrm(ks[4], (DEPTH_2, D_FF, D_MODEL), D_FF ** -0.5),
        "mix_norm": gain(ks[5], D_MODEL),
        "w_in": nrm(ks[6], (DEPTH_2, D_MODEL, D_IN), D_MODEL ** -0.5),
        "a_rel_bias": nrm(ks[7], (DEPTH_2, A_HEADS, A_NUM_REL), 0.1),
        "c_q_norm": gain(ks[8], C_Q_RANK),
        "c_kv_norm": gain(ks[9], C_KV_RANK),
        "c_w_uq": nrm(ks[10], (DEPTH_2, C_Q_RANK, C_HEADS * (C_NOPE + C_ROPE)), C_Q_RANK ** -0.5),
        "c_w_ukv": nrm(ks[11], (DEPTH_2, C_KV_RANK, C_HEADS * (C_NOPE + C_V)), C_KV_RANK ** -0.5),
        "w_out": nrm(ks[12], (DEPTH_2, D_MIX, D_MODEL), D_MIX ** -0.5),
        "ffn2_norm": gain(ks[13], D_MODEL),
        "ffn2_w_gate": nrm(ks[14], (DEPTH_2, D_MODEL, D_FF), D_MODEL ** -0.5),
        "ffn2_w_up": nrm(ks[15], (DEPTH_2, D_MODEL, D_FF), D_MODEL ** -0.5),
        "ffn2_w_down": nrm(ks[16], (DEPTH_2, D_FF, D_MODEL), D_FF ** -0.5),
        "final_norm": 1.0 + 0.02 * jax.random.normal(ks[17], (D_MODEL,), f32),
    }

def second_block(x, ffn1_norm, ffn1_w_gate, ffn1_w_up, ffn1_w_down, mix_norm, w_in, a_rel_bias,
              c_q_norm, c_kv_norm, c_w_uq, c_w_ukv, w_out, ffn2_norm, ffn2_w_gate, ffn2_w_up,
              ffn2_w_down, final_norm):
    pos = jnp.arange(x.shape[1], dtype=jnp.int32)
    for l in range(DEPTH_2):
        x = hybrid_layer(x, pos, ffn1_norm[l], ffn1_w_gate[l], ffn1_w_up[l], ffn1_w_down[l], mix_norm[l],
                         w_in[l], a_rel_bias[l], c_q_norm[l], c_kv_norm[l], c_w_uq[l], c_w_ukv[l], w_out[l],
                         ffn2_norm[l], ffn2_w_gate[l], ffn2_w_up[l], ffn2_w_down[l])
    return rmsnorm(x, final_norm)


def setup_inputs(seed=0):
    out = dict(first_inputs(seed))
    for name, value in second_inputs(seed + 1).items():
        if name != "x":
            out[name + "_2"] = value
    return out


def reference(
    x, ffn1_norm, ffn1_w_gate, ffn1_w_up, ffn1_w_down, mix_norm, w_in, gate_bias, attn_w_up,
    rwkv_mu, rwkv_w0, rwkv_w2, rwkv_a0, rwkv_a2, rwkv_g2, rwkv_k_k, rwkv_k_a, rwkv_r_k,
    rwkv_ln_w, rwkv_ln_b, rwkv_w_out, w_o, ffn2_norm, ffn2_w_gate, ffn2_w_up, ffn2_w_down,
    final_norm, ffn1_norm_2, ffn1_w_gate_2, ffn1_w_up_2, ffn1_w_down_2, mix_norm_2, w_in_2,
    a_rel_bias_2, c_q_norm_2, c_kv_norm_2, c_w_uq_2, c_w_ukv_2, w_out_2, ffn2_norm_2,
    ffn2_w_gate_2, ffn2_w_up_2, ffn2_w_down_2, final_norm_2,
):
    x = first_block(
        x, ffn1_norm, ffn1_w_gate, ffn1_w_up, ffn1_w_down, mix_norm, w_in, gate_bias, attn_w_up,
        rwkv_mu, rwkv_w0, rwkv_w2, rwkv_a0, rwkv_a2, rwkv_g2, rwkv_k_k, rwkv_k_a, rwkv_r_k,
        rwkv_ln_w, rwkv_ln_b, rwkv_w_out, w_o, ffn2_norm, ffn2_w_gate, ffn2_w_up, ffn2_w_down,
        final_norm,
    )
    return second_block(
        x, ffn1_norm_2, ffn1_w_gate_2, ffn1_w_up_2, ffn1_w_down_2, mix_norm_2, w_in_2,
        a_rel_bias_2, c_q_norm_2, c_kv_norm_2, c_w_uq_2, c_w_ukv_2, w_out_2, ffn2_norm_2,
        ffn2_w_gate_2, ffn2_w_up_2, ffn2_w_down_2, final_norm_2,
    )


_drawn_inputs = setup_inputs


def setup_inputs(seed=0):
    import zlib

    import numpy as np

    out = dict(_drawn_inputs(seed))
    spreads = {}
    factors = {'rwkv_w2': 8.0,
     'rwkv_ln_b': 3.312,
     'ffn1_norm_2': 2.746,
     'a_rel_bias_2': 3.902,
     'c_q_norm_2': 8.0,
     'c_kv_norm_2': 8.0,
     'ffn2_norm_2': 4.004,
     'final_norm_2': 2.843}
    for name, (base, spread) in spreads.items():
        noise = np.random.default_rng([zlib.crc32(name.encode()), seed]).standard_normal(out[name].shape)
        drawn = base * np.exp(spread * noise) if base else spread * noise
        out[name] = jnp.asarray(drawn.astype(out[name].dtype))
    for name, factor in factors.items():
        out[name] = (out[name] * factor).astype(out[name].dtype)
    return out
```

```python
from contextlib import ExitStack
import math

import numpy as np

import concourse.bass as bass
from concourse import mybir

F32 = mybir.dt.float32
F32R = mybir.dt.float32r
ALU = mybir.AluOpType
ACT = mybir.ActivationFunctionType
AX = mybir.AxisListType.X

D = 1024
FF = 2816
NM = FF // 128
NIN2 = 3080
NEG = -1e30
DECAY = -math.exp(-0.5)
CW = 2048


def plan(stages):
    out = []

    def ffn(w):
        for m in range(NM + 1):
            if m < NM:
                out.append((w, "gu", m, 2048))
            if m >= 2 and m % 2 == 0:
                out.append((w, "down", m // 2 - 1, 2048))

    for s in stages:
        if s[0] == "ffn":
            ffn(s[1])
        elif s[0] == "mix1":
            out.append(("mix1", "lora", 0, 2048))
            out.append(("mix1", "lora", 1, 1024))
            for j in range(4):
                out += [("mix1", "qkv", 2 * j, 2048), ("mix1", "qkv", 2 * j + 1, 2048)]
            out.append(("mix1", "qkv", 8, 2048))
            for j in range(8):
                out.append(("mix1", "gate", j, 2048))
            out.append(("mix1", "up", 0, 2048))
            for g in range(4):
                for q in "kvr":
                    out.append(("mix1", q, g, 2048))
            for j in range(4):
                out.append(("mix1", "wout", j, 2048))
            for j in range(4):
                out.append(("mix1", "wo", j, 2048))
        elif s[0] == "mix2":
            l = s[1]
            out.append((l, "in2", 12, 64))
            for j in (0, 1, 2, 3, 4, 5, 6, 7, 8, 9, 10, 11):
                out.append((l, "in2", j, 2048))
            out.append((l, "uq", 0, 1440))
            out.append((l, "ukv", 0, 1280))
            for j in range(4):
                out.append((l, "wout2", j, 2048))
    return out


def const_table():
    p = np.arange(128)
    cols = {}
    parts = []
    at = 0

    def put(name, a):
        nonlocal at
        a = np.asarray(a, np.float32).reshape(128, -1)
        cols[name] = (at, a.shape[1])
        parts.append(a)
        at += a.shape[1]

    put("ident", np.eye(128))
    put("anti", np.eye(128)[:, ::-1])
    put("hsel", (p[:, None] // 64 == np.arange(2)[None, :]))
    s = p[:, None] % 64
    t = np.arange(64)[None, :]
    put("mar", np.stack([s < t, s <= t], 1))
    put("mlow", t < s)
    put("i64", t == s)

    def lower(k):
        return (s >> (k + 1) == t >> (k + 1)) & ((s >> k) % 2 == 1) & ((t >> k) % 2 == 0)

    def upper(k):
        return (s >> (k + 1) == t >> (k + 1)) & ((s >> k) % 2 == 0) & ((t >> k) % 2 == 1)

    put("m0", lower(0))
    put("m0t", upper(0))
    bd = p[:, None] // 64 == p[None, :] // 64
    for k in range(1, 6):
        put(f"mt{k}", np.tile(upper(k), (1, 2)) & bd)
    put("bd", bd)
    put("half", np.full((128, 2), -0.5))
    f = np.float32

    def tables(theta, d):
        half = d // 2
        inv = np.power(f(theta), -(np.arange(half, dtype=f) * f(2.0 / d))).astype(f)
        ang = (np.arange(256, dtype=f)[:, None] * inv[None, :]).astype(f)
        sh = lambda a: a.reshape(2, 128, half).transpose(1, 0, 2)
        return sh(np.cos(ang)), sh(np.sin(ang))

    for name, th, d in (("r16", 500000.0, 16), ("r64", 10000.0, 64), ("r32", 10000.0, 32)):
        c, sn = tables(th, d)
        put(name + "c", c)
        put(name + "s", sn)
    base = at
    for tt in range(2):
        tq = (128 * tt + p)[:, None]
        sk = np.arange(128 * (tt + 1))[None, :]
        ok = [(sk <= tq) & (tq - sk <= 128), (sk <= tq) & ((tq - sk) % 4 == 0), (sk <= tq) & ((tq - sk) % 16 == 0)]
        put(f"dil{tt}", np.where(np.stack(ok, 1), 0.0, NEG))
    return cols, np.concatenate(parts, 1), base


def col_layout():
    names = [("ffn1_norm", 8), ("mix_norm", 8), ("ffn2_norm", 8), ("mu", 27), ("w0", 8), ("a0", 8), ("kk", 8),
             ("ka", 8), ("rk", 8)]
    for l in range(2):
        names += [(f"ffn1_norm_2{l}", 8), (f"mix_norm_2{l}", 8), (f"ffn2_norm_2{l}", 8), (f"cq{l}", 3), (f"ckv{l}", 2)]
    at, out = 0, {}
    for n, w in names:
        out[n] = (at, w)
        at += w
    return out, at


class Call:

    def matmul(self, *a, **k):
        return lambda e: e.matmul(*a, **k)

    def transpose(self, *a, **k):
        return lambda e: e.transpose(*a, **k)

    def activation(self, *a, **k):
        return lambda e: e.activation(*a, **k)

    def tensor_tensor(self, *a, **k):
        return lambda e: e.tensor_tensor(*a, **k)

    def tensor_scalar(self, *a, **k):
        return lambda e: e.tensor_scalar(*a, **k)

    def scalar_tensor_tensor(self, *a, **k):
        return lambda e: e.scalar_tensor_tensor(*a, **k)

    def tensor_reduce(self, *a, **k):
        return lambda e: e.tensor_reduce(*a, **k)

    def tensor_copy(self, *a, **k):
        return lambda e: e.tensor_copy(*a, **k)

    def memset(self, *a, **k):
        return lambda e: e.memset(*a, **k)

    def reciprocal(self, *a, **k):
        return lambda e: e.reciprocal(*a, **k)

    def tensor_tensor_scan(self, *a, **k):
        return lambda e: e.tensor_tensor_scan(*a, **k)

    def max(self, *a, **k):
        return lambda e: e.max(*a, **k)

    def match_replace(self, *a, **k):
        return lambda e: e.match_replace(*a, **k)


CALL = Call()


class Prog:

    def __init__(self, nc, ctx):
        self.nc, self.ctx = nc, ctx
        self.q = {e: [] for e in ("pe", "act", "dve", "pool", "sp")}
        self.sem = {e: ctx.enter_context(nc.semaphore(f"s_{e}")) for e in ("pe", "act", "dve", "pool")}
        self.n = {e: 0 for e in self.sem}
        self.seen = {}
        self.nsem = 0

    def wait(self, eng, toks):
        for t in toks:
            if t is None:
                continue
            if isinstance(t, list):
                self.wait(eng, t)
                continue
            s, v = t
            key = (eng, id(s))
            if self.seen.get(key, 0) < v:
                self.seen[key] = v
                self.q[eng].append(lambda e, s=s, v=v: e.wait_ge(s, v))

    def last(self, eng):
        return (self.sem[eng], self.n[eng]) if self.n[eng] else None

    def op(self, eng, fn, *toks, dep=True, sig=True):
        fn = fn(CALL)
        self.wait(eng, toks)
        if dep and eng != "pe":
            self.wait(eng, [self.last(eng)])
        if not sig:
            self.q[eng].append(fn)
            return None
        s = self.sem[eng]
        self.q[eng].append(lambda e: fn(e).then_inc(s, 1))
        self.n[eng] += 1
        return (s, self.n[eng])

    def pe(self, fn, *t, sig=False):
        return self.op("pe", fn, *t, sig=sig)

    def act(self, fn, *t, dep=True):
        return self.op("act", fn, *t, dep=dep)

    def dve(self, fn, *t, dep=True):
        return self.op("dve", fn, *t, dep=dep)

    def pool(self, fn, *t, dep=True):
        return self.op("pool", fn, *t, dep=dep)

    def new_sem(self):
        self.nsem += 1
        return [self.ctx.enter_context(self.nc.semaphore(f"d{self.nsem}")), 0]

    def dma(self, dst, src, sem, *toks, eng="sp"):
        self.wait(eng, toks)
        sem[1] += 16
        s = sem[0]
        self.q[eng].append(lambda e: e.dma_start(dst, src).then_inc(s, 16))
        return (s, sem[1])


class Ring:

    def __init__(self, aps):
        self.free = [(a, []) for a in aps]

    def get(self):
        assert self.free, "no slot free"
        return self.free.pop(0)

    def put(self, ap, toks):
        self.free.append((ap, list(toks)))


def interleave(main, side, ratio=1):
    side_on = True
    for _ in main:
        for _ in range(ratio):
            if side_on and next(side, 0) == 0:
                side_on = False
    for _ in side:
        pass


def staggered(gens, depth):
    gens = iter(gens)
    live = []
    while True:
        if len(live) < depth:
            g = next(gens, None)
            if g is not None:
                live.append(g)
        if not live:
            return
        for g in list(live):
            if next(g, 0) == 0:
                live.remove(g)
        yield 1


def build(nc, stages, x_in, wall, consts, cols, rows, lorap, ebias, out):
    ctab, carr, cbase = const_table()
    NCON = carr.shape[1]
    clay, NCOL = col_layout()
    with ExitStack() as ctx:
        p = Prog(nc, ctx)

        def sb(name, shape, dt=F32):
            return ctx.enter_context(nc.sbuf_tensor(name, shape, dt))

        X = sb("X", [128, 2, 1024])
        raw = [sb(f"raw{i}", [128, CW]) for i in range(3)]
        whi = [sb(f"whi{i}", [128, CW], F32R) for i in range(2)]
        wlo = [sb(f"wlo{i}", [128, CW], F32R) for i in range(2)]
        xh, xl = sb("xh", [128, 8, 256], F32R), sb("xl", [128, 8, 256], F32R)
        yh, yl = sb("yh", [128, 8, 256], F32R), sb("yl", [128, 8, 256], F32R)
        C = sb("C", [128, cbase])
        COL = sb("COL", [128, NCOL])
        small = sb("small", [128, 256])
        GATE = sb("GATE", [128, 2, 2048])
        NA = 22300
        arena = sb("arena", [128, NA])
        PS = ctx.enter_context(nc.psum_tensor("PS", [128, 8, 512], F32))
        bank = [PS[:, i, :] for i in range(8)]
        R = Ring(bank[0:4])
        A = Ring(bank[4:8])

        def con(name):
            a, w = ctab[name]
            return C[:, a:a + w]

        def col(name, j):
            a, _ = clay[name]
            return COL[:, a + j:a + j + 1]

        class Space:
            def __init__(self, at=0):
                self.at = at

            def take(self, *shape):
                n = int(np.prod(shape))
                a = arena[:, self.at:self.at + n]
                self.at += n
                assert self.at <= NA, self.at
                if len(shape) == 1:
                    return a
                names = "abcde"[:len(shape)]
                return a.rearrange(f"p ({' '.join(names)}) -> p {' '.join(names)}",
                                   **{n_: s_ for n_, s_ in zip(names, shape)})

        ident = con("ident")
        sem_c, sem_x, sem_col = p.new_sem(), p.new_sem(), p.new_sem()
        t_x = p.dma(X[:], x_in.rearrange("(t p) d -> p t d", p=128), sem_x)
        t_c = p.dma(C[:], consts[:, 0:cbase], sem_c)
        t_col = p.dma(COL[:], cols, sem_col)

        chunks = plan(stages)
        offs = np.cumsum([0] + [128 * c[3] for c in chunks])
        raw_sem = [p.new_sem() for _ in range(3)]
        RAWN, SPL = 3, 2
        st = {"dma": 0, "split": 0, "use": 0}
        land, split_tok, use_tok, info = {}, {}, {}, {}

        def feed_dma():
            i = st["dma"]
            if i >= len(chunks):
                return
            w = chunks[i][3]
            src = wall[int(offs[i]):int(offs[i + 1])].rearrange("(p w) -> p w", p=128)
            land[i] = p.dma(raw[i % RAWN][:, 0:w], src, raw_sem[i % RAWN],
                            split_tok[i - RAWN] if i >= RAWN else [])
            st["dma"] += 1

        def feed_split():
            i = st["split"]
            if i >= len(chunks):
                return
            w = chunks[i][3]
            free = use_tok[i - SPL] if i >= SPL else None
            r = raw[i % RAWN][:, 0:w]
            hi, lo = whi[i % SPL][:, 0:w], wlo[i % SPL][:, 0:w]
            a = p.act(lambda e: e.activation(hi, r, ACT.Copy), land[i], free, dep=False)
            d = p.dve(lambda e: e.tensor_tensor(lo, r, hi.bitcast(F32), ALU.subtract), land[i], a, free, dep=False)
            split_tok[i] = [a, d]
            st["split"] += 1
            feed_dma()

        for _ in range(RAWN):
            feed_dma()
        feed_split()

        def take(key):
            i = st["use"]
            assert chunks[i][:3] == key, (chunks[i], key)
            w = chunks[i][3]
            while st["split"] <= i:
                feed_split()
            return whi[i % SPL][:, 0:w], wlo[i % SPL][:, 0:w], split_tok[i]

        def done(tok):
            use_tok[st["use"]] = tok
            st["use"] += 1
            if st["split"] <= st["use"]:
                feed_split()

        def mm3(o, wa, wb, xa, xb, first, last, toks, sig=False):
            p.pe(lambda e: e.matmul(o, wa, xa, start=first, stop=False), *toks)
            p.pe(lambda e: e.matmul(o, wa, xb, start=False, stop=False))
            return p.pe(lambda e: e.matmul(o, wb, xa, start=False, stop=last), sig=sig)

        def transpose(o, i, *toks, sig=False, id_=None):
            k = i.shape[0]
            idn = ident if id_ is None else id_
            return p.pe(lambda e: e.transpose(o, i, idn[0:k, 0:k]), *toks, sig=sig)

        def rstd(src, n, width, eps, toks):
            a = p.pool(lambda e: e.tensor_scalar(src, src, 1.0 / width, eps, ALU.mult, ALU.add), toks)
            h = con("half")[:, 0:1]
            hb = h.to_broadcast([128, n])
            return p.pool(lambda e: e.tensor_tensor(src, src, hb, ALU.pow), a, t_c)

        def sumsq(src2, width, scratch, toks):
            ts = []
            for tt in range(2):
                s_, o_, acc = src2[:, tt, :], scratch[:, tt, :], small[:, tt:tt + 1]
                ts.append(p.act(lambda e, s_=s_, o_=o_, acc=acc: e.activation(o_, s_, ACT.Square, accum_out=acc),
                                toks))
            return rstd(small[:, 0:2], 2, width, 1e-6, ts)

        def to_channels(src2, n, gain, hi, lo, toks, k0=0):
            out = []
            for k in range(0, n, 2):
                b, free = R.get()
                ks = list(range(k, min(n, k + 2)))
                for kk in ks:
                    for tt in range(2):
                        o = b[:, (kk - k) * 256 + tt * 128:(kk - k) * 256 + tt * 128 + 128]
                        i = src2[:, tt, kk * 128:(kk + 1) * 128]
                        t = transpose(o, i, toks, free, t_c, sig=(kk == ks[-1] and tt == 1))
                a, ls = None, []
                for kk in ks:
                    o, i = hi[:, k0 + kk, :], b[:, (kk - k) * 256:(kk - k) * 256 + 256]
                    if gain:
                        g = col(gain, kk)
                        a = p.act(lambda e, o=o, i=i, g=g: e.activation(o, i, ACT.Copy, scale=g), t, t_col,
                                  dep=False)
                    else:
                        a = p.act(lambda e, o=o, i=i: e.activation(o, i, ACT.Copy), t, dep=False)
                for kk in ks:
                    o, h, i = lo[:, k0 + kk, :], hi[:, k0 + kk, :].bitcast(F32), b[:, (kk - k) * 256:(kk - k) * 256 + 256]
                    if gain:
                        g = col(gain, kk)
                        d = p.dve(lambda e, o=o, i=i, g=g, h=h: e.scalar_tensor_tensor(o, i, g, h, ALU.mult, ALU.subtract),
                                  a, t_col, dep=False)
                    else:
                        d = p.dve(lambda e, o=o, i=i, h=h: e.tensor_tensor(o, i, h, ALU.subtract), a, dep=False)
                R.put(b, [d])
                out += [a, d]
            return out

        def norm_channels(gain, xtok, free):
            xn = Space().take(2, 1024)
            r = sumsq(X, 1024, xn, [xtok, free])
            ts = []
            for tt in range(2):
                o, i, s_ = xn[:, tt, :], X[:, tt, :], small[:, tt:tt + 1]
                if tt == 0:
                    ts.append(p.act(lambda e, o=o, i=i, s_=s_: e.activation(o, i, ACT.Copy, scale=s_), r))
                else:
                    ts.append(p.dve(lambda e, o=o, i=i, s_=s_: e.tensor_scalar(o, i, s_, None, ALU.mult), r, ts))
            return to_channels(xn, 8, gain, xh, xl, ts)

        def down_like(key_fn, n, lhs, toks_fn, banks, frees, kper=2):
            for j in range(n):
                hi, lo, w = take(key_fn(j))
                h3 = hi.rearrange("p (k n) -> p k n", k=kper)
                l3 = lo.rearrange("p (k n) -> p k n", k=kper)
                for kk in range(kper):
                    k = j * kper + kk
                    for tt in range(2):
                        a, b = lhs(k, tt)
                        for nn in range(2):
                            o = banks[2 * tt + nn]
                            first, last = k == 0, k == n * kper - 1
                            wh_, wl_ = h3[:, kk, nn * 512:nn * 512 + 512], l3[:, kk, nn * 512:nn * 512 + 512]
                            t = mm3(o, a, b, wh_, wl_, first, last, [w, toks_fn(k), frees if k == 0 else None],
                                    sig=(kk == kper - 1 and tt == 1 and nn == 1))
                done(t)
                yield t

        def residual(banks, scale, tok):
            for tt in range(2):
                for nn in range(2):
                    o = X[:, tt, nn * 512:nn * 512 + 512]
                    b = banks[2 * tt + nn]
                    d = p.dve(lambda e, o=o, b=b: e.scalar_tensor_tensor(o, b, scale, o, ALU.mult, ALU.add), tok,
                              dep=(tt == 0 and nn == 0))
                    A.put(b, [d])
            return d

        def ffn(which, gain, xtok):
            xt = norm_channels(gain, xtok, None)
            sg = [small_buf(i) for i in range(2)]
            hring = Ring([(yh[:, i, :], yl[:, i, :]) for i in range(5)])
            sgr = Ring(sg)
            got = [A.get() for _ in range(4)]
            banks, frees = [b for b, _ in got], [f for _, f in got]
            hs = {}

            def gu(m):
                hi, lo, w = take((which, "gu", m))
                b, free = R.get()
                for g in range(2):
                    for k in range(8):
                        c0 = (g * 8 + k) * 128
                        t = mm3(b[:, g * 256:(g + 1) * 256], hi[:, c0:c0 + 128], lo[:, c0:c0 + 128], xh[:, k, :],
                                xl[:, k, :], k == 0, k == 7, [w, xt, free], sig=(k == 7))
                done(t)
                s_, sf = sgr.get()
                a = p.act(lambda e: e.activation(s_, b[:, 0:256], ACT.Silu), t, sf, dep=False)
                d = p.dve(lambda e: e.tensor_tensor(s_, s_, b[:, 256:512], ALU.mult), a, dep=False)
                R.put(b, [d])
                (hh, hl), hf = hring.get()
                a = p.act(lambda e: e.activation(hh, s_, ACT.Copy), d, hf, dep=False)
                d = p.dve(lambda e: e.tensor_tensor(hl, s_, hh.bitcast(F32), ALU.subtract), a, hf, dep=False)
                sgr.put(s_, [a, d])
                hs[m] = (hh, hl, [a, d])

            def lhs(k, tt):
                hh, hl, _ = hs[k]
                return hh[:, tt * 128:(tt + 1) * 128], hl[:, tt * 128:(tt + 1) * 128]

            dn = down_like(lambda j: (which, "down", j), NM // 2, lhs, lambda k: hs[k][2], banks, frees)
            for m in range(NM + 1):
                if m < NM:
                    gu(m)
                if m >= 2 and m % 2 == 0:
                    t = next(dn)
                    for k in (m - 2, m - 1):
                        hring.put(hs[k][:2], [t])
            return residual(banks, 0.5, t)

        smb = [arena[:, 20000 + 256 * i:20256 + 256 * i] for i in range(2)]

        def small_buf(i):
            return smb[i]

        def soften(S, n, toks, nm, den):
            d = p.dve(lambda e: e.tensor_reduce(nm, S, AX, ALU.max, negate=True), toks)
            a = p.act(lambda e: e.activation(S, S, ACT.Exp, bias=nm, accum_out=den), d)
            return a, p.dve(lambda e: e.reciprocal(den, den), a)

        def turn_and_weigh(S, blocks, values, PT, ptfree, a, rden, o, extra, ofree):
            ts = []
            for b0 in range(0, blocks, 4):
                b, free = R.get()
                nb = min(4, blocks - b0)
                for i in range(nb):
                    t = transpose(b[:, i * 128:(i + 1) * 128], S[:, (b0 + i) * 128:(b0 + i + 1) * 128], a, free,
                                  t_c, sig=(i == nb - 1))
                dst = PT[:, b0 * 128:(b0 + nb) * 128]
                c = p.act(lambda e, dst=dst, b=b, nb=nb: e.activation(dst, b[:, 0:nb * 128], ACT.Copy), t, ptfree,
                          dep=False)
                R.put(b, [c])
                ts.append(c)
            yield 1
            b, free = R.get()
            dv = o.shape[1]
            for i in range(blocks):
                t = p.pe(lambda e, i=i: e.matmul(b[:, 0:dv], PT[:, i * 128:(i + 1) * 128], values[i],
                                                 start=(i == 0), stop=(i == blocks - 1)), ts, free, extra,
                         sig=(i == blocks - 1))
            d = p.dve(lambda e: e.tensor_scalar(o, b[:, 0:dv], rden, None, ALU.mult), t, ofree)
            R.put(b, [d])
            self_done.append((t, d))

        self_done = []

        def rope(src, dst, tt, nh, hd, off, half, name, tmp, toks):
            c = con(name + "c")[:, tt * half:(tt + 1) * half].unsqueeze(1).to_broadcast([128, nh, half])
            s_ = con(name + "s")[:, tt * half:(tt + 1) * half].unsqueeze(1).to_broadcast([128, nh, half])
            sv = src.rearrange("p (h d) -> p h d", d=hd)
            dv_ = dst.rearrange("p (h d) -> p h d", d=hd)
            x1, x2 = sv[:, :, off:off + half], sv[:, :, off + half:off + 2 * half]
            o1, o2 = dv_[:, :, off:off + half], dv_[:, :, off + half:off + 2 * half]
            n = nh * half
            tv = [tmp[:, i * n:(i + 1) * n].rearrange("p (h d) -> p h d", d=half) for i in range(4)]
            p.dve(lambda e: e.tensor_tensor(tv[0], x1, c, ALU.mult), toks, t_c)
            p.dve(lambda e: e.tensor_tensor(tv[1], x2, s_, ALU.mult), dep=False)
            p.dve(lambda e: e.tensor_tensor(tv[2], x2, c, ALU.mult), dep=False)
            p.dve(lambda e: e.tensor_tensor(tv[3], x1, s_, ALU.mult), dep=False)
            p.dve(lambda e: e.tensor_tensor(o1, tv[0], tv[1], ALU.subtract))
            return p.dve(lambda e: e.tensor_tensor(o2, tv[2], tv[3], ALU.add), dep=False)

        def proj_b(keys, dsts, xt, evac):
            got = [A.get() for _ in range(2)]
            nk = 8 // len(keys)
            w = 0
            for j, key in enumerate(keys):
                hi, lo, wt = take(key)
                w = hi.shape[1] // nk
                for kk in range(nk):
                    k = j * nk + kk
                    for tt in range(2):
                        b, free = got[tt]
                        t = mm3(b[:, 0:w], xh[:, k, tt * 128:(tt + 1) * 128], xl[:, k, tt * 128:(tt + 1) * 128],
                                hi[:, kk * w:(kk + 1) * w], lo[:, kk * w:(kk + 1) * w], k == 0, k == 7,
                                [wt, xt, free if k == 0 else None], sig=(kk == nk - 1 and tt == 1))
                done(t)
                if j < len(keys) - 1:
                    yield 1
            for tt in range(2):
                b, _ = got[tt]
                A.put(b, [evac(tt, b[:, 0:w], t)])
            yield 1

        def mix1(xtok):
            xt = norm_channels("mix_norm", xtok, None)
            after_norm = [p.last("pe"), p.last("act"), p.last("dve")]
            sp = Space()
            zl = sp.take(3, 256)
            rbase = sp.at
            QKV = sp.take(2, 2304)
            DM = [sp.take(384), sp.take(768)]
            GB = sp.take(2048)
            qT = sp.take(6, 256)
            kz = sp.take(12, 256)
            Sb = [sp.take(768) for _ in range(3)]
            PTb = [sp.take(768) for _ in range(2)]
            AO = sp.take(2, 256)
            rt = sp.take(4 * 24 * 8)
            z = sp.take(2, 257)
            ztmp = sp.take(2, 256)
            sem = p.new_sem()
            for tt in range(2):
                a_, w_ = ctab[f"dil{tt}"]
                t_dm = p.dma(DM[tt], consts[:, a_:a_ + w_], sem, after_norm, eng="pool")
            sem = p.new_sem()
            t_gb = p.dma(GB, rows[0:1, 0:2048].to_broadcast([128, 2048]), sem, after_norm, eng="pool")
            zk = p.pool(lambda e: e.memset(kz, 0.0), after_norm)
            z0 = p.pool(lambda e: e.memset(z[:, :, 0:1], 0.0))

            def shift(key, n, w, dst, mus, zz, zt, zfree, rows_=128):
                hi, lo, wt = take(key)
                b, free = A.get()
                for j in range(n):
                    for k in range(8):
                        c0 = k * n * w + j * w
                        t = mm3(b[0:w, j * 256:(j + 1) * 256], hi[:, c0:c0 + w], lo[:, c0:c0 + w], xh[:, k, :],
                                xl[:, k, :], k == 0, k == 7, [wt, xt, free], sig=(k == 7))
                done(t)
                bb = b.rearrange("p (n t) -> p n t", n=2)[0:w, 0:n, :]
                c = p.act(lambda e: e.activation(zz[0:w, 0:n, 1:257], bb, ACT.Copy), t, zfree, z0, dep=False)
                A.put(b, [c])
                d = p.dve(lambda e: e.tensor_tensor(zt[0:w, 0:n, :], zz[0:w, 0:n, 0:256], zz[0:w, 0:n, 1:257],
                                                    ALU.subtract), c)
                for j in range(n):
                    m_ = col("mu", mus[j])[0:w]
                    d = p.dve(lambda e, j=j, m_=m_: e.scalar_tensor_tensor(
                        dst[0:w, j, :], zt[0:w, j, :], m_, zz[0:w, j, 1:257], ALU.mult, ALU.add), t_col,
                        dep=(j == 0))
                return d

            d = shift(("mix1", "lora", 0), 2, 128, zl, [0, 1], z, ztmp, None)
            d = shift(("mix1", "lora", 1), 1, 128, zl[:, 2:3, :], [2], z, ztmp, d)
            p.act(lambda e: e.activation(zl[0:64, 0, :], zl[0:64, 0, :], ACT.Tanh), d)
            p.act(lambda e: e.activation(zl[:, 1, :], zl[:, 1, :], ACT.Tanh, scale=0.5), d, dep=False)
            a = p.act(lambda e: e.activation(zl[:, 2, :], zl[:, 2, :], ACT.Tanh, scale=0.5), d, dep=False)
            p.dve(lambda e: e.tensor_scalar(zl[:, 1, :], zl[:, 1, :], 0.5, 0.5, ALU.mult, ALU.add), a)
            t_zl = p.dve(lambda e: e.tensor_scalar(zl[:, 2, :], zl[:, 2, :], 0.5, 0.5, ALU.mult, ALU.add),
                         dep=False)

            def qkv_chunks():
                for j in range(5):
                    keys = [("mix1", "qkv", 2 * j), ("mix1", "qkv", 2 * j + 1)] if j < 4 else [("mix1", "qkv", 8)]

                    def evac(tt, b, t, j=j):
                        o = QKV[:, tt, j * 512:j * 512 + b.shape[1]]
                        return p.act(lambda e: e.activation(o, b, ACT.Copy), t, after_norm, dep=False)
                    yield from proj_b(keys, None, xt, evac)

            for _ in qkv_chunks():
                pass
            tq = p.last("act")
            r_ = []
            for tt in range(2):
                r_.append(rope(QKV[:, tt, 0:1536], QKV[:, tt, 0:1536], tt, 24, 64, 0, 8, "r16", rt, [tq]))

            def gates():
                for j in range(4):
                    def evac(tt, b, t, j=j):
                        o = GATE[:, tt, j * 512:(j + 1) * 512]
                        gb = GB[:, j * 512:(j + 1) * 512]
                        d = p.dve(lambda e: e.tensor_tensor(o, b, gb, ALU.add), t, t_gb, dep=False)
                        a = p.act(lambda e: e.activation(o, o, ACT.Tanh, scale=0.5), d, dep=False)
                        p.pool(lambda e: e.tensor_scalar(o, o, 0.5, 0.5, ALU.mult, ALU.add), a, dep=False)
                        return d
                    yield from proj_b([("mix1", "gate", 2 * j), ("mix1", "gate", 2 * j + 1)], None, xt, evac)

            def attention():
                kv = []
                for j in range(12):
                    b, free = R.get()
                    for tt in range(2):
                        t = transpose(b[:, tt * 128:(tt + 1) * 128], QKV[:, tt, j * 128:(j + 1) * 128], r_, free, t_c,
                                      sig=(tt == 1))
                    if j < 6:
                        c = p.act(lambda e, j=j, b=b: e.activation(qT[:, j, :], b[:, 0:256], ACT.Copy), t, dep=False)
                    else:
                        for q in range(2):
                            o = kz[64 * q:64 * q + 64, 2 * (j - 6) + q, :]
                            i_ = b[64 * q:64 * q + 64, 0:256]
                            c = p.act(lambda e, o=o, i_=i_: e.activation(o, i_, ACT.Copy), t, zk, dep=False)
                    R.put(b, [c])
                    kv.append(c)
                    if j % 3 == 2:
                        yield 1
                Sr, Pr = Ring(Sb), Ring(PTb)
                stat = Ring([small[:, 8 + 2 * i:10 + 2 * i] for i in range(4)])

                def unit(hh, tt):
                    S, sfree = Sr.get()
                    sv_, stf = stat.get()
                    nm, den = sv_[:, 0:1], sv_[:, 1:2]
                    W = 128 * (tt + 1)
                    groups = [[0, 1, 2]] if tt == 0 else [[0, 1], [2]]
                    ds = []
                    for gs in groups:
                        b, free = R.get()
                        for i, g in enumerate(gs):
                            q = qT[:, 2 * g + hh // 2, tt * 128:(tt + 1) * 128]
                            k_ = kz[:, 4 * g + hh, 0:W]
                            o = b[:, i * W:(i + 1) * W]
                            t = p.pe(lambda e, o=o, q=q, k_=k_: e.matmul(o, q, k_, start=True, stop=True), kv, free,
                                     sig=(i == len(gs) - 1))
                        n = len(gs) * W
                        o = S[:, gs[0] * W:gs[0] * W + n]
                        m_ = DM[tt][:, gs[0] * W:gs[0] * W + n]
                        d = p.dve(lambda e, o=o, b=b, m_=m_, n=n: e.scalar_tensor_tensor(
                            o, b[:, 0:n], 0.125, m_, ALU.mult, ALU.add), t, sfree, stf, t_dm, dep=False)
                        R.put(b, [d])
                        ds.append(d)
                    a, rd = soften(S[:, 0:3 * W], 3 * W, ds, nm, den)
                    yield 1
                    PT, pf = Pr.get()
                    vals = [QKV[:, s_, 1536 + (4 * g + hh) * 64:1536 + (4 * g + hh) * 64 + 64]
                            for g in range(3) for s_ in range(tt + 1)]
                    yield from turn_and_weigh(S, 3 * (tt + 1), vals, PT, pf, a, den,
                                              AO[:, tt, hh * 64:(hh + 1) * 64], tq, None)
                    t, d = self_done.pop()
                    Sr.put(S, [t])
                    Pr.put(PT, [t])
                    stat.put(sv_, [d])
                    yield 1

                yield from staggered((unit(hh, tt) for hh in range(4) for tt in range(2)), 2)

            interleave(gates(), attention(), 2)
            ao = p.last("dve")
            tc_ = to_channels(AO, 2, None, yh, yl, [ao])
            got = [A.get() for _ in range(4)]
            banks, frees = [b for b, _ in got], [f for _, f in got]
            for t in down_like(lambda j: ("mix1", "up", 0), 1,
                               lambda k, tt: (yh[:, k, tt * 128:(tt + 1) * 128], yl[:, k, tt * 128:(tt + 1) * 128]),
                               lambda k: tc_, banks, frees):
                pass
            tg = p.last("pool")
            for tt in range(2):
                for nn in range(2):
                    o = GATE[:, tt, nn * 512:nn * 512 + 512]
                    b = banks[2 * tt + nn]
                    d = p.dve(lambda e, o=o, b=b: e.tensor_tensor(o, o, b, ALU.mult), t, tg, dep=False)
                    A.put(b, [d])
            attn_done = [p.last("pe"), p.last("act"), p.last("dve"), p.last("pool")]
            rwkv(rbase, zl, t_zl, xt, shift, attn_done)
            got = [A.get() for _ in range(4)]
            banks, frees = [b for b, _ in got], [f for _, f in got]
            ty = [p.last("act"), p.last("dve")]
            for t in down_like(lambda j: ("mix1", "wout", j), 4,
                               lambda k, tt: (yh[:, k, tt * 128:(tt + 1) * 128], yl[:, k, tt * 128:(tt + 1) * 128]),
                               lambda k: ty, banks, frees):
                pass
            for tt in range(2):
                for nn in range(2):
                    o = GATE[:, tt, 1024 + nn * 512:1024 + nn * 512 + 512]
                    g0 = GATE[:, tt, nn * 512:nn * 512 + 512]
                    b = banks[2 * tt + nn]
                    d = p.dve(lambda e, o=o, b=b: e.tensor_tensor(o, o, b, ALU.mult), t)
                    A.put(b, [d])
                    d = p.dve(lambda e, o=o, g0=g0: e.tensor_tensor(g0, g0, o, ALU.add), d)
            tm = to_channels(GATE[:, :, 0:1024], 8, None, yh, yl, [d, t])
            got = [A.get() for _ in range(4)]
            banks, frees = [b for b, _ in got], [f for _, f in got]
            for t in down_like(lambda j: ("mix1", "wo", j), 4,
                               lambda k, tt: (yh[:, k, tt * 128:(tt + 1) * 128], yl[:, k, tt * 128:(tt + 1) * 128]),
                               lambda k: tm, banks, frees):
                pass
            return residual(banks, 1.0, t)

        def rwkv(base, zl, t_zl, xt, shift, start):
            sp = Space(base)
            kzv = {q: sp.take(2, 256) for q in "kvr"}
            z = [sp.take(2, 257) for _ in range(2)]
            zt = [sp.take(2, 256) for _ in range(2)]
            LW, LG = sp.take(256), sp.take(2, 256)
            LN = sp.take(2, 256)
            wd, aa, kk, kp, rn = [sp.take(2, 256) for _ in range(5)]
            Pi, Px, iP, w1 = [sp.take(2, 256) for _ in range(4)]
            bt, kt = sp.take(2, 256), sp.take(2, 256)
            ARz = sp.take(4, 4, 2, 64)
            Vt, Bt, Kt = [sp.take(2, 256) for _ in range(3)]
            Vz = sp.take(4, 256)
            TB, TK = sp.take(8, 128), sp.take(8, 128)
            eight = lambda t_: t_.rearrange("p a b -> p (a b)").rearrange("p (u k) -> p u k", u=8)
            L, Dm, DT, Xc = eight(aa), eight(wd), eight(kk), eight(kp)
            DTb, Xb, Lb = [sp.take(8, 128) for _ in range(3)]
            Gz, Uz = sp.take(2, 256), sp.take(2, 256)
            ST = sp.take(2, 64)
            Yt, sq = Px, iP
            st_ = sp.take(64)
            for t_ in (ARz, Vz, Gz, Uz, w1):
                z0 = p.pool(lambda e, t_=t_: e.memset(t_, 0.0), start)
            for t_ in z:
                z0 = p.pool(lambda e, t_=t_: e.memset(t_[:, :, 0:1], 0.0))
            semL = p.new_sem()
            BD = con("bd").unsqueeze(1).to_broadcast([128, 8, 128])

            def three(t_):
                return t_.rearrange("p a b -> p (a b)")

            def wide(o, i, *toks, eng=None):
                i4 = i.unsqueeze(2).to_broadcast([128, 8, 2, 64])
                o4 = o.rearrange("p u (c k) -> p u c k", c=2)
                b4 = con("bd").rearrange("p (c k) -> p c k", c=2).unsqueeze(1).to_broadcast([128, 8, 2, 64])
                return (eng or p.dve)(lambda e: e.tensor_tensor(o4, i4, b4, ALU.mult), *toks)

            def group(g, prev):
                tl = p.dma(LW, lorap[0, :, g * 256:(g + 1) * 256], semL, prev, eng="pool")
                tl = p.dma(LG, lorap[1:3, :, g * 256:(g + 1) * 256].rearrange("a p n -> p a n"), semL, eng="pool")
                tl = p.dma(LN, rows[1:3, g * 256:(g + 1) * 256].unsqueeze(0).to_broadcast([128, 2, 256]), semL, eng="pool")
                tz = {}
                for i, q in enumerate("kvr"):
                    tz[q] = shift(("mix1", q, g), 2, 128, kzv[q], [3 + 8 * i + 2 * g, 4 + 8 * i + 2 * g],
                                  z[i % 2], zt[i % 2], prev + [z0] + ([tz["k"]] if i == 2 else []))
                    yield 1
                k3, v3, r3 = kzv["k"], kzv["v"], kzv["r"]
                b1, f1 = R.get()
                b2, f2 = R.get()
                for j in range(2):
                    o1, o2 = b1[:, j * 256:(j + 1) * 256], b2[:, j * 256:(j + 1) * 256]
                    l1, l2 = LW[0:64, j * 128:(j + 1) * 128], LW[64:128, j * 128:(j + 1) * 128]
                    p.pe(lambda e, o1=o1, l1=l1: e.matmul(o1, l1, zl[0:64, 0, :], start=True, stop=True), t_zl, tl, f1)
                    t1 = p.pe(lambda e, o2=o2, l2=l2: e.matmul(o2, l2, zl[64:128, 0, :], start=True, stop=True), f2,
                              sig=True)
                for j in range(2):
                    for b, dst, nm in ((b1, wd, "w0"), (b2, aa, "a0")):
                        o, i_ = dst[:, j, :], b[:, j * 256:(j + 1) * 256]
                        c_ = col(nm, 2 * g + j)
                        a = p.dve(lambda e, o=o, i_=i_, c_=c_: e.tensor_scalar(o, i_, c_, 0.5, ALU.add, ALU.mult),
                                  t1, t_col, prev, dep=False)
                R.put(b1, [a])
                R.put(b2, [a])
                p.act(lambda e: e.activation(wd, wd, ACT.Tanh), a)
                a = p.act(lambda e: e.activation(aa, aa, ACT.Tanh), a, dep=False)
                p.dve(lambda e: e.tensor_scalar(wd, wd, 0.5, 0.5, ALU.mult, ALU.add), a)
                d = p.dve(lambda e: e.tensor_scalar(aa, aa, 0.5, 0.5, ALU.mult, ALU.add), dep=False)
                ew = p.act(lambda e: e.activation(wd, wd, ACT.Exp, scale=DECAY), d)
                for j in range(2):
                    o, i_, c_ = kk[:, j, :], k3[:, j, :], col("kk", 2 * g + j)
                    d = p.dve(lambda e, o=o, i_=i_, c_=c_: e.tensor_scalar(o, i_, c_, None, ALU.mult), tz["k"], prev,
                              t_col, dep=False)
                a = p.act(lambda e: e.activation(rn, kk, ACT.Square), d, prev)
                b, f = R.get()
                for tt in range(2):
                    for j in range(2):
                        o = b[:, tt * 4 + j * 2:tt * 4 + j * 2 + 2]
                        t = p.pe(lambda e: e.matmul(o, rn[:, j, tt * 128:(tt + 1) * 128], con("hsel"), start=True,
                                                    stop=True), a, f, sig=(tt == 1 and j == 1))
                yield 1
                nrm = st_[:, 16:24]
                d = p.dve(lambda e: e.tensor_scalar(nrm, b[:, 0:8], 1e-24, None, ALU.max), t)
                R.put(b, [d])
                hb = con("half")[:, 0:1].to_broadcast([128, 8])
                pw = p.pool(lambda e: e.tensor_tensor(nrm, nrm, hb, ALU.pow), d)
                wide4 = three(rn).rearrange("p (u k) -> p u k", k=64)
                nb4 = nrm.unsqueeze(2).to_broadcast([128, 8, 64])
                sp_ = p.pool(lambda e: e.tensor_copy(wide4, nb4), pw)
                brn, f = R.get()
                for tt in range(2):
                    for j in range(2):
                        trn = transpose(brn[:, j * 256 + tt * 128:j * 256 + tt * 128 + 128],
                                        three(rn)[:, tt * 256 + j * 128:tt * 256 + j * 128 + 128], sp_, f,
                                        sig=(tt == 1 and j == 1))
                for j in range(2):
                    o, i_, c_ = kp[:, j, :], aa[:, j, :], col("ka", 2 * g + j)
                    p.dve(lambda e, o=o, i_=i_, c_=c_: e.tensor_scalar(o, i_, 1.0, c_, ALU.subtract, ALU.mult))
                p.dve(lambda e: e.scalar_tensor_tensor(three(kp), three(kp), 1.0, three(k3), ALU.add, ALU.mult))
                wv = three(wd).rearrange("p (c t) -> p c t", t=64)
                w1v = three(w1).rearrange("p (c t) -> p c t", t=64)
                p.dve(lambda e: e.tensor_copy(w1v[:, :, 0:1], wv[:, :, 0:1]), ew, z0)
                p.dve(lambda e: e.memset(wv[:, :, 0:1], 0.0))
                p.dve(lambda e: e.tensor_tensor_scan(three(Pi), three(wd), three(w1), 0.0, ALU.mult, ALU.add))
                Piv = three(Pi).rearrange("p (c t) -> p c t", t=64)
                Pxv = three(Px).rearrange("p (c t) -> p c t", t=64)
                p.dve(lambda e: e.tensor_copy(Pxv[:, :, 1:64], Piv[:, :, 0:63]))
                p.dve(lambda e: e.memset(Pxv[:, :, 0:1], 1.0), dep=False)
                p.dve(lambda e: e.reciprocal(iP, Pi), dep=False)
                p.dve(lambda e: e.tensor_tensor(three(kt), three(kp), three(iP), ALU.mult))
                d = p.dve(lambda e: e.tensor_tensor(three(kk), three(kk), brn, ALU.mult), trn)
                R.put(brn, [d])
                p.dve(lambda e: e.tensor_tensor(three(bt), three(kk), three(aa), ALU.mult))
                p.dve(lambda e: e.tensor_tensor(three(bt), three(bt), three(iP), ALU.mult))
                for hh in range(4):
                    j, q = hh // 2, hh % 2
                    s_ = slice(64 * q, 64 * q + 64)
                    cv = lambda t_: t_[s_, j, :].rearrange("p (c t) -> p c t", t=64)
                    oa, orr = ARz[s_, hh, :, 0, :], ARz[s_, hh, :, 1, :]
                    ka_, px_, r_, pi_ = cv(kk), cv(Px), cv(r3), cv(Pi)
                    p.dve(lambda e, oa=oa, ka_=ka_, px_=px_: e.scalar_tensor_tensor(
                        oa, ka_, -1.0, px_, ALU.mult, ALU.mult), z0, dep=(hh == 0))
                    tar = p.dve(lambda e, orr=orr, r_=r_, pi_=pi_: e.tensor_tensor(orr, r_, pi_, ALU.mult), tz["r"],
                                dep=False)
                for j in range(2):
                    o, i_, c_, k_ = rn[:, j, :], r3[:, j, :], col("rk", 2 * g + j), kp[:, j, :]
                    d = p.dve(lambda e, o=o, i_=i_, c_=c_, k_=k_: e.scalar_tensor_tensor(
                        o, i_, c_, k_, ALU.mult, ALU.mult))
                yield 1
                tt_ = {}
                for nm, src, dst in (("v", v3, Vt), ("b", bt, Bt), ("k", kt, Kt)):
                    b, f = R.get()
                    for tt in range(2):
                        for j in range(2):
                            t = transpose(b[:, tt * 256 + j * 128:tt * 256 + j * 128 + 128],
                                          src[:, j, tt * 128:(tt + 1) * 128], tar, tz["v"], f, t_c,
                                          sig=(tt == 1 and j == 1))
                    a = p.act(lambda e, dst=dst, b=b: e.activation(three(dst), b, ACT.Copy), t, prev, dep=False)
                    R.put(b, [a])
                    tt_[nm] = a
                for c in range(4):
                    s_ = slice(64 * (c % 2), 64 * (c % 2) + 64)
                    vz = p.pool(lambda e, c=c, s_=s_: e.tensor_copy(Vz[s_, c, :], Vt[s_, c // 2, :]), tt_["v"], prev,
                                z0, dep=False)
                outs = {}
                for nm, src, dst in (("b", bt, TB), ("k", kt, TK)):
                    for half in range(2):
                        b, f = R.get()
                        for i in range(4):
                            u = half * 4 + i
                            hh, tt = u // 2, u % 2
                            for q in range(2):
                                c = 2 * tt + q
                                o = b[64 * q:64 * q + 64, i * 128:(i + 1) * 128]
                                l_ = src[:, hh // 2, c * 64:(c + 1) * 64]
                                r_ = ARz[:, hh, c, :, :].rearrange("p a t -> p (a t)")
                                t = p.pe(lambda e, o=o, l_=l_, r_=r_: e.matmul(o, l_, r_, start=True, stop=True), f,
                                         tar, sig=(i == 3 and q == 1))
                        o = dst[:, half * 4:half * 4 + 4, :]
                        m_ = con("mar").unsqueeze(1).to_broadcast([128, 4, 128])
                        bv = b.rearrange("p (u k) -> p u k", u=4)
                        d = p.dve(lambda e, o=o, bv=bv, m_=m_: e.tensor_tensor(o, bv, m_, ALU.mult), t, prev,
                                  dep=False)
                        R.put(b, [d])
                        outs[nm] = d
                b, f = R.get()
                for u in range(8):
                    hh, tt = u // 2, u % 2
                    for q in range(2):
                        c = 2 * tt + q
                        o = b[64 * q:64 * q + 64, u * 64:(u + 1) * 64]
                        l_ = ARz[:, hh, c, 0, :]
                        r_ = bt[:, hh // 2, c * 64:(c + 1) * 64]
                        t = p.pe(lambda e, o=o, l_=l_, r_=r_: e.matmul(o, l_, r_, start=True, stop=True), f,
                                 sig=(u == 7 and q == 1))
                bv = b.rearrange("p (u k) -> p u k", u=8)
                ml = con("mlow").unsqueeze(1).to_broadcast([128, 8, 64])
                d = p.dve(lambda e: e.tensor_tensor(L, bv, ml, ALU.mult), t, prev)
                R.put(b, [d])
                yield 1
                LT = TB[:, :, 0:64]
                bc = lambda n: con(n).unsqueeze(1).to_broadcast([128, 8, 64])
                p.dve(lambda e: e.tensor_tensor(Dm, L, bc("m0"), ALU.mult))
                p.dve(lambda e: e.tensor_tensor(Dm, Dm, bc("i64"), ALU.add))
                p.dve(lambda e: e.tensor_tensor(DT, LT, bc("m0t"), ALU.mult))
                d = p.dve(lambda e: e.tensor_tensor(DT, DT, bc("i64"), ALU.add))
                db = wide(DTb, DT, d)
                for k in range(1, 6):
                    i4 = LT.unsqueeze(2).to_broadcast([128, 8, 2, 64])
                    o4 = Lb.rearrange("p u (c k) -> p u c k", c=2)
                    b4 = con(f"mt{k}").rearrange("p (c k) -> p c k", c=2).unsqueeze(1).to_broadcast([128, 8, 2, 64])
                    lb = p.dve(lambda e, o4=o4, i4=i4, b4=b4: e.tensor_tensor(o4, i4, b4, ALU.mult), p.last("pe"))
                    b, f = R.get()
                    for u in range(8):
                        t = p.pe(lambda e, u=u, b=b: e.matmul(b[:, u * 64:(u + 1) * 64], Lb[:, u, :], Dm[:, u, :],
                                                              start=True, stop=True), f, lb, d, sig=(u == 7))
                    bv = b.rearrange("p (u k) -> p u k", u=8)
                    xb = wide(Xb, bv, t)
                    xc = None
                    if k < 5:
                        xc = p.act(lambda e, bv=bv: e.activation(Xc, bv, ACT.Copy), xb, dep=False)
                    R.put(b, [xb, xc])
                    yield 1
                    if k < 5:
                        b, f = R.get()
                        for u in range(8):
                            t = p.pe(lambda e, u=u, b=b: e.matmul(b[:, u * 64:(u + 1) * 64], DTb[:, u, :],
                                                                  Xc[:, u, :], start=True, stop=True), f, db, xc,
                                     sig=(u == 7))
                        bv = b.rearrange("p (u k) -> p u k", u=8)
                        d = p.dve(lambda e, bv=bv: e.tensor_tensor(Dm, Dm, bv, ALU.add), t)
                        R.put(b, [d])
                    b, f = R.get()
                    for u in range(8):
                        t = p.pe(lambda e, u=u, b=b: e.matmul(b[:, u * 64:(u + 1) * 64], Xb[:, u, :], DT[:, u, :],
                                                              start=True, stop=True), f, xb, sig=(u == 7))
                    bv = b.rearrange("p (u k) -> p u k", u=8)
                    d = p.dve(lambda e, bv=bv: e.tensor_tensor(DT, DT, bv, ALU.add), t)
                    R.put(b, [d])
                    if k < 5:
                        db = wide(DTb, DT, d)
                    yield 1
                t_inv = d
                s_tok = None
                for c in range(4):
                    tt, q = c // 2, c % 2
                    ps = slice(64 * q, 64 * q + 64)
                    if q == 0:
                        yb, yf = R.get()
                    b, f = R.get()
                    for hh in range(4):
                        o = b[ps, hh * 64:(hh + 1) * 64]
                        u = hh * 2 + tt
                        if c:
                            p.pe(lambda e, o=o, hh=hh, c=c: e.matmul(o, ARz[:, hh, c, 0, :], ST[:, hh // 2, :],
                                                                     start=True, stop=False), f, s_tok)
                        t = p.pe(lambda e, o=o, hh=hh, c=c, u=u: e.matmul(
                            o, TK[:, u, 0:64], Vz[:, c, hh * 64:(hh + 1) * 64], start=(c == 0), stop=True), f, vz,
                            outs["k"], sig=(hh == 3))
                    gd = p.dve(lambda e, b=b, ps=ps, q=q: e.tensor_copy(Gz[ps, q, :], b[ps, 0:256]), t, z0)
                    R.put(b, [gd])
                    yield 1
                    b, f = R.get()
                    for hh in range(4):
                        o = b[ps, hh * 64:(hh + 1) * 64]
                        u = hh * 2 + tt
                        t = p.pe(lambda e, o=o, hh=hh, u=u, q=q: e.matmul(
                            o, DT[:, u, :], Gz[:, q, hh * 64:(hh + 1) * 64], start=True, stop=True), f, gd, t_inv,
                            sig=(hh == 3))
                    ud = p.dve(lambda e, b=b, ps=ps, q=q: e.tensor_copy(Uz[ps, q, :], b[ps, 0:256]), t)
                    R.put(b, [ud])
                    for hh in range(4):
                        o = yb[ps, hh * 64:(hh + 1) * 64]
                        u = hh * 2 + tt
                        if c:
                            p.pe(lambda e, o=o, hh=hh, c=c: e.matmul(o, ARz[:, hh, c, 1, :], ST[:, hh // 2, :],
                                                                     start=(hh == 0), stop=False,
                                                                     skip_group_check=True), yf)
                        p.pe(lambda e, o=o, hh=hh, c=c, u=u: e.matmul(
                            o, TK[:, u, 64:128], Vz[:, c, hh * 64:(hh + 1) * 64], start=(c == 0 and hh == 0),
                            stop=False, skip_group_check=True), yf)
                    yield 1
                    b = None
                    if c < 3:
                        b, f = R.get()
                        for hh in range(4):
                            o = b[64 * (hh % 2):64 * (hh % 2) + 64, (hh // 2) * 64:(hh // 2) * 64 + 64]
                            p.pe(lambda e, o=o, hh=hh, tt=tt, q=q: e.matmul(
                                o, Bt[:, tt, hh * 64:(hh + 1) * 64], Uz[:, q, hh * 64:(hh + 1) * 64], start=True,
                                stop=False), f, ud, tt_["b"])
                            t = p.pe(lambda e, o=o, hh=hh, tt=tt, c=c: e.matmul(
                                o, Kt[:, tt, hh * 64:(hh + 1) * 64], Vz[:, c, hh * 64:(hh + 1) * 64], start=False,
                                stop=True), tt_["k"], sig=(hh == 3))
                    t_st = t
                    for hh in range(4):
                        o = yb[ps, hh * 64:(hh + 1) * 64]
                        u = hh * 2 + tt
                        t = p.pe(lambda e, o=o, hh=hh, u=u, q=q: e.matmul(
                            o, TB[:, u, 64:128], Uz[:, q, hh * 64:(hh + 1) * 64], start=False, stop=True,
                            skip_group_check=True), ud, sig=(hh == 3))
                    if c < 3:
                        bv = b[:, 0:128].rearrange("p (j k) -> p j k", j=2)
                        pc = Pi[:, :, c * 64 + 63:c * 64 + 64].to_broadcast([128, 2, 64])
                        if c:
                            p.dve(lambda e, bv=bv: e.tensor_tensor(ST, ST, bv, ALU.add), t, t_st)
                            s_tok = p.dve(lambda e, pc=pc: e.tensor_tensor(ST, ST, pc, ALU.mult))
                        else:
                            s_tok = p.dve(lambda e, bv=bv, pc=pc: e.tensor_tensor(ST, bv, pc, ALU.mult), t, t_st)
                        R.put(b, [s_tok])
                    if q == 1:
                        yd = p.dve(lambda e, yb=yb, tt=tt: e.tensor_copy(Yt[:, tt, :], yb[:, 0:256]), t)
                        R.put(yb, [yd])
                    yield 1
                y4 = three(Yt).rearrange("p (u v) -> p u v", v=64)
                s4 = three(sq).rearrange("p (u v) -> p u v", v=64)
                mean, var = st_[:, 0:8], st_[:, 8:16]
                mb = mean.unsqueeze(2).to_broadcast([128, 8, 64])
                vb = var.unsqueeze(2).to_broadcast([128, 8, 64])
                p.dve(lambda e: e.tensor_reduce(mean, y4, AX, ALU.add))
                p.dve(lambda e: e.tensor_scalar(mean, mean, 1.0 / 64, None, ALU.mult))
                d = p.dve(lambda e: e.tensor_tensor(y4, y4, mb, ALU.subtract))
                a = p.act(lambda e: e.activation(s4, y4, ACT.Square), d)
                d = p.dve(lambda e: e.tensor_reduce(var, s4, AX, ALU.add), a)
                p.pool(lambda e: e.tensor_scalar(var, var, 1.0 / 64, 64e-5, ALU.mult, ALU.add), d)
                h8 = con("half")[:, 0:1].to_broadcast([128, 8])
                pw = p.pool(lambda e: e.tensor_tensor(var, var, h8, ALU.pow))
                b1, f1 = R.get()
                for tt in range(2):
                    o = b1[:, tt * 256:(tt + 1) * 256]
                    p.pe(lambda e, o=o, tt=tt: e.matmul(o, zl[:, 1, tt * 128:(tt + 1) * 128], LG[:, 0, :], start=True,
                                                        stop=False), f1, tl)
                    t1 = p.pe(lambda e, o=o, tt=tt: e.matmul(o, zl[:, 2, tt * 128:(tt + 1) * 128], LG[:, 1, :],
                                                             start=False, stop=True), sig=True)
                b2, f2 = R.get()
                for tt in range(2):
                    for j in range(2):
                        o = b2[:, tt * 4 + j * 2:tt * 4 + j * 2 + 2]
                        t2 = p.pe(lambda e, o=o, tt=tt, j=j: e.matmul(
                            o, rn[:, j, tt * 128:(tt + 1) * 128], con("hsel"), start=True, stop=True), f2,
                            sig=True)
                yield 1
                p.dve(lambda e: e.tensor_tensor(y4, y4, vb, ALU.mult), pw)
                lw = LN[:, 0:1, :].to_broadcast([128, 2, 256])
                lb_ = LN[:, 1:2, :].to_broadcast([128, 2, 256])
                p.dve(lambda e: e.tensor_tensor(Yt, Yt, lw, ALU.mult), tl)
                p.dve(lambda e: e.tensor_tensor(Yt, Yt, lb_, ALU.add))
                bs = b2[:, 0:8].unsqueeze(2).to_broadcast([128, 8, 64])
                v4 = three(Vt).rearrange("p (u v) -> p u v", v=64)
                d2 = p.dve(lambda e: e.tensor_tensor(s4, v4, bs, ALU.mult), t2)
                R.put(b2, [d2])
                p.dve(lambda e: e.tensor_tensor(Yt, Yt, sq, ALU.add))
                d = p.dve(lambda e: e.tensor_tensor(three(Yt), three(Yt), b1, ALU.mult), t1)
                R.put(b1, [d])
                to_channels(Yt, 2, None, yh, yl, [d], k0=2 * g)
                yield 1

            prev = [z0]
            for g in range(4):
                for _ in group(g, prev):
                    pass
                prev = [p.last("pe"), p.last("act"), p.last("dve"), p.last("pool")]

        def mix2(l, xtok):
            xt = norm_channels(f"mix_norm_2{l}", xtok, None)
            after = [p.last("pe"), p.last("act"), p.last("dve")]
            sp = Space()
            PJ = sp.take(2, NIN2)
            EB = sp.take(6, 256)
            AK = sp.take(6, 256)
            BK = sp.take(5, 256)
            CK = sp.take(5, 256)
            IK = sp.take(4, 256)
            AQ, BQ, CQ, IQ = sp.take(3, 256), sp.take(3, 256), sp.take(5, 256), sp.take(2, 256)
            QF = sp.take(2, 480)
            KVF = sp.take(2, 640)
            KF = sp.take(2, 480)
            IKr = sp.take(2, 512)
            sc2 = sp.take(2, 384)
            rt = GATE[:, 0, 0:2048]
            OUT = rt.rearrange("p (t d) -> p t d", t=2)
            IXW = GATE[:, 1, 0:2048]
            MB = [sp.take(128), sp.take(256)]
            SC = sp.take(256)
            work = SC
            sflat, iflat = sc2.rearrange("p a b -> p (a b)"), IKr.rearrange("p a b -> p (a b)")
            Sb = [sflat[:, 256 * i:256 * i + 256] for i in range(3)]
            PTb = [iflat[:, 256 * i:256 * i + 256] for i in range(3)]
            CM = [sp.take(128), sp.take(256)]
            sem = p.new_sem()
            t_eb = p.dma(EB, bass.AP(ebias.tensor, ebias[l, 0, 0:1].offset, [[1, 128], [384, 6], [1, 256]]), sem, after, eng="pool")
            zz = [p.pool(lambda e, t_=t_: e.memset(t_, 0.0), after) for t_ in (AK, BK, IKr, CM[0], CM[1])]
            zz.append(p.pool(lambda e: e.memset(CM[0][0:64, 64:128], NEG)))
            zz.append(p.pool(lambda e: e.memset(CM[1][0:64, 192:256], NEG)))
            ev = []

            def proj():
                for j in (6, 0, 1, 2, 3, 4, 5):
                    keys = [(l, "in2", 12)] if j == 6 else [(l, "in2", 2 * j), (l, "in2", 2 * j + 1)]

                    def evac(tt, b, t, j=j):
                        o = PJ[:, tt, j * 512:j * 512 + b.shape[1]]
                        a = p.act(lambda e: e.activation(o, b, ACT.Copy), t, after, dep=False)
                        ev.append(a)
                        return a
                    yield from proj_b(keys, None, xt, evac)

            for _ in proj():
                pass
            tp = [p.last("act")]

            lat = []
            for j, (c0, w, nm, k0) in enumerate(((2408, 384, f"cq{l}", 0), (2792, 256, f"ckv{l}", 3))):
                s2 = sc2[:, :, 0:w]
                r = sumsq(PJ[:, :, c0:c0 + w], w, s2, tp)
                for tt in range(2):
                    o, i_, s_ = s2[:, tt, :], PJ[:, tt, c0:c0 + w], small[:, tt:tt + 1]
                    a = p.act(lambda e, o=o, i_=i_, s_=s_: e.activation(o, i_, ACT.Copy, scale=s_), r)
                to_channels(s2, w // 128, nm, yh, yl, [a], k0=k0)
                lat = [p.last("act"), p.last("dve"), p.last("pe")]
            t = None
            for nm, nk, k0, w, dst in (("uq", 3, 0, 480, QF), ("ukv", 2, 3, 640, KVF)):
                hi, lo, wt = take((l, nm, 0))
                for tt in range(2):
                    for c0 in range(0, w, 320):
                        cw = min(320, w - c0)
                        b, f = R.get()
                        for k in range(nk):
                            lh, ll = yh[:, k0 + k, tt * 128:(tt + 1) * 128], yl[:, k0 + k, tt * 128:(tt + 1) * 128]
                            t = mm3(b[:, 0:cw], lh, ll, hi[:, k * w + c0:k * w + c0 + cw],
                                    lo[:, k * w + c0:k * w + c0 + cw], k == 0, k == nk - 1, [wt, lat, f],
                                    sig=(k == nk - 1))
                        o = dst[:, tt, c0:c0 + cw]
                        a = p.act(lambda e, o=o, b=b, cw=cw: e.activation(o, b[:, 0:cw], ACT.Copy), t, after,
                                  dep=False)
                        R.put(b, [a])
                done(t)
            tl = [p.last("act")]
            for tt in range(2):
                P_ = PJ[:, tt, :]
                rope(P_[:, 1152:1792], P_[:, 1152:1792], tt, 10, 64, 0, 32, "r64", rt, tp)
                rope(P_[:, 2112:2400], P_[:, 2112:2400], tt, 9, 32, 0, 16, "r32", rt, tp)
                rope(P_[:, 3048:3080], P_[:, 3048:3080], tt, 1, 32, 0, 16, "r32", rt, tp)
                tr = rope(QF[:, tt, :], QF[:, tt, :], tt, 5, 96, 64, 16, "r32", rt, tl)
                kf = KF[:, tt, :].rearrange("p (h d) -> p h d", d=96)
                kn = KVF[:, tt, :].rearrange("p (h d) -> p h d", d=128)[:, :, 0:64]
                kr = P_[:, 3048:3080].unsqueeze(1).to_broadcast([128, 5, 32])
                p.pool(lambda e, kf=kf, kn=kn: e.tensor_copy(kf[:, :, 0:64], kn), tl, after)
                p.pool(lambda e, kf=kf, kr=kr: e.tensor_copy(kf[:, :, 64:96], kr), tr)
                for j in range(4):
                    o = IKr[:, tt, j * 128 + 32 * j:j * 128 + 32 * j + 32]
                    tk = p.pool(lambda e, o=o, i_=P_[:, 2368:2400]: e.tensor_copy(o, i_), tr)
            ready = [tr, tk, tp, tl]

            def turned(src, w, parts):
                b, f = R.get()
                for tt in range(2):
                    t = transpose(b[0:w, tt * 128:(tt + 1) * 128], src(tt), ready, f, t_c, sig=(tt == 1))
                c = None
                for dst, r0, n in parts:
                    c = p.act(lambda e, dst=dst, r0=r0, n=n: e.activation(dst[r0:r0 + n], b[r0:r0 + n, 0:256],
                                                                          ACT.Copy), t, zz, after, dep=False)
                R.put(b, [c])
                return c

            for j in range(2):
                turned(lambda tt, j=j: PJ[:, tt, 2112 + 128 * j:2240 + 128 * j], 128, [(IQ[:, j, :], 0, 128)])
            for j in range(4):
                ti = turned(lambda tt, j=j: IKr[:, tt, 128 * j:128 * j + 128], 128, [(IK[:, j, :], 0, 128)])

            def heads():
                for j in range(3):
                    turned(lambda tt, j=j: PJ[:, tt, 128 * j:128 * j + 128], 128, [(AQ[:, j, :], 0, 128)])
                    turned(lambda tt, j=j: PJ[:, tt, 384 + 128 * j:512 + 128 * j], 128,
                           [(AK[:, 2 * j, :], 0, 64), (AK[:, 2 * j + 1, :], 64, 64)])
                    yield 1
                for j in range(5):
                    turned(lambda tt, j=j: QF[:, tt, 96 * j:96 * j + 96], 96, [(CQ[:, j, :], 0, 96)])
                    turned(lambda tt, j=j: KF[:, tt, 96 * j:96 * j + 96], 96, [(CK[:, j, :], 0, 96)])
                    yield 1
                for j in range(3):
                    w = 128 if j < 2 else 64
                    turned(lambda tt, j=j, w=w: PJ[:, tt, 1152 + 128 * j:1152 + 128 * j + w], w,
                           [(BQ[:, j, :], 0, w)])
                    turned(lambda tt, j=j, w=w: PJ[:, tt, 1472 + 128 * j:1472 + 128 * j + w], w,
                           [(BK[:, 2 * j, :], 0, 64)] + ([(BK[:, 2 * j + 1, :], 64, 64)] if w == 128 else []))
                    yield 1

            mtok = {}

            def index(tt):
                W = 128 * (tt + 1)
                sl = slice(tt * 128, (tt + 1) * 128)
                iv = IXW[:, 0:8 * W].rearrange("p (h w) -> p h w", h=8)
                nb = 512 // W
                for h0 in range(0, 8, nb):
                    b, f = R.get()
                    for i in range(nb):
                        h = h0 + i
                        o = b[:, i * W:(i + 1) * W]
                        q, k_ = IQ[:, h // 4, sl], IK[:, h % 4, 0:W]
                        t = p.pe(lambda e, o=o, q=q, k_=k_: e.matmul(o, q, k_, start=True, stop=True), f, ti,
                                 sig=(i == nb - 1))
                    o = IXW[:, h0 * W:h0 * W + 512]
                    a = p.act(lambda e, o=o, b=b: e.activation(o, b, ACT.Relu, scale=32 ** -0.5), t, p.last("dve"),
                              dep=False)
                    R.put(b, [a])
                    yield 1
                iw = PJ[:, tt, 2400:2408]
                ws = small[:, 32:40]
                p.dve(lambda e: e.tensor_scalar(ws, iw, 8 ** -0.5, None, ALU.mult), tp)
                wb = ws.unsqueeze(2).to_broadcast([128, 8, W])
                p.dve(lambda e: e.tensor_tensor(iv, iv, wb, ALU.mult), a)
                p.dve(lambda e: e.tensor_tensor(iv[:, 0:4, :], iv[:, 0:4, :], iv[:, 4:8, :], ALU.add))
                p.dve(lambda e: e.tensor_tensor(iv[:, 0:2, :], iv[:, 0:2, :], iv[:, 2:4, :], ALU.add))
                s_, w_ = SC[:, 0:W], work[:, 0:W]
                p.dve(lambda e: e.tensor_tensor(s_, iv[:, 0, :], iv[:, 1, :], ALU.add))
                p.dve(lambda e: e.memset(SC[0:64, W - 64:W], NEG))
                yield 1
                m8 = small[:, 40:48]
                for r in range(8):
                    p.dve(lambda e: e.max(m8, s_))
                    p.dve(lambda e: e.match_replace(s_, m8, s_, -3e38))
                    if r % 2:
                        yield 1
                p.dve(lambda e: e.tensor_scalar(w_, s_, -2e38, NEG, ALU.is_ge, ALU.mult))
                mb = MB[tt]
                cm = CM[tt]
                mtok[tt] = p.dve(lambda e: e.tensor_tensor(mb, w_, cm, ALU.add), zz)
                yield 1

            Sr, Pr = Ring(Sb), Ring(PTb)
            stat = Ring([small[:, 8 + 2 * i:10 + 2 * i] for i in range(4)])

            def unit(kind, h, tt):
                S, sfree = Sr.get()
                sv_, stf = stat.get()
                nm, den = sv_[:, 0:1], sv_[:, 1:2]
                W = 128 * (tt + 1)
                sl = slice(tt * 128, (tt + 1) * 128)
                b, f = R.get()
                sw = S[:, 0:W]
                tk_ = p.last("act") if (kind, h) not in kt_ else kt_[(kind, h)]
                if kind == "a":
                    p.pe(lambda e: e.matmul(b[:, 0:W], AQ[:, h // 2, sl], AK[:, h, 0:W], start=True, stop=True),
                         f, tk_)
                    for kt2 in range(tt + 1):
                        lh = EB[:, h, 128 * (tt - kt2):128 * (tt - kt2) + 128]
                        t = p.pe(lambda e, kt2=kt2, lh=lh: e.matmul(
                            b[:, 256 + kt2 * 128:384 + kt2 * 128], lh, con("anti"), start=True, stop=True), t_eb,
                            sig=(kt2 == tt))
                    cm = CM[tt]
                    d0 = p.dve(lambda e: e.scalar_tensor_tensor(sw, b[:, 0:W], 0.125, cm, ALU.mult, ALU.add), t,
                               sfree, stf, zz, dep=False)
                    d = p.dve(lambda e: e.tensor_tensor(sw, sw, b[:, 256:256 + W], ALU.add), d0)
                    v = [PJ[:, s_, 768 + h * 64:768 + (h + 1) * 64] for s_ in range(tt + 1)]
                    oc = h * 64
                elif kind == "b":
                    t = p.pe(lambda e: e.matmul(b[:, 0:W], BQ[0:bk(h), h // 2, sl], BK[0:bk(h), h, 0:W], start=True,
                                                stop=True), f, tk_, sig=True)
                    mb = MB[tt]
                    d = p.dve(lambda e: e.scalar_tensor_tensor(sw, b[:, 0:W], 0.125, mb, ALU.mult, ALU.add), t,
                              sfree, stf, mtok[tt], dep=False)
                    v = [PJ[:, s_, 1792 + h * 64:1792 + (h + 1) * 64] for s_ in range(tt + 1)]
                    oc = 384 + h * 64
                else:
                    t = p.pe(lambda e: e.matmul(b[:, 0:W], CQ[0:96, h, sl], CK[0:96, h, 0:W], start=True, stop=True),
                             f, tk_, sig=True)
                    cm = CM[tt]
                    d = p.dve(lambda e: e.scalar_tensor_tensor(sw, b[:, 0:W], 96 ** -0.5, cm, ALU.mult, ALU.add), t,
                              sfree, stf, zz, dep=False)
                    v = [KVF[:, s_, h * 128 + 64:h * 128 + 128] for s_ in range(tt + 1)]
                    oc = 704 + h * 64
                R.put(b, [d])
                a, rd = soften(sw, W, [d], nm, den)
                yield 1
                PT, pf = Pr.get()
                yield from turn_and_weigh(S, tt + 1, v, PT, pf, a, den, OUT[:, tt, oc:oc + 64], [tp, tl], after)
                t, d = self_done.pop()
                Sr.put(S, [t])
                Pr.put(PT, [t])
                stat.put(sv_, [d])
                yield 1

            kt_ = {}

            def bk(h):
                return 64 if h == 4 else 128

            for _ in heads():
                pass
            units = [(k, h, tt) for k, n in (("a", 6), ("c", 5)) for h in range(n) for tt in range(2)]

            def idx_all():
                yield from index(0)
                yield from index(1)
            interleave(staggered((unit(*u) for u in units), 2), idx_all(), 1)
            for _ in staggered((unit("b", h, tt) for tt in range(2) for h in range(5)), 2):
                pass
            to_ = to_channels(OUT, 8, None, xh, xl, [p.last("dve"), p.last("pe")])
            got = [A.get() for _ in range(4)]
            banks, frees = [b for b, _ in got], [f for _, f in got]
            for t in down_like(lambda j: (l, "wout2", j), 4,
                               lambda k, tt: (xh[:, k, tt * 128:(tt + 1) * 128], xl[:, k, tt * 128:(tt + 1) * 128]),
                               lambda k: to_, banks, frees):
                pass
            return residual(banks, 1.0, t)

        def final(row, xtok, inplace=True):
            sp = Space()
            xn = sp.take(2, 1024)
            gr = sp.take(1024)
            g = p.dma(gr, rows[row:row + 1, 0:1024].to_broadcast([128, 1024]), p.new_sem(), xtok, eng="pool")
            r = sumsq(X, 1024, xn, [xtok])
            d = None
            for tt in range(2):
                o, s_ = X[:, tt, :], small[:, tt:tt + 1]
                d = p.dve(lambda e, o=o, s_=s_: e.scalar_tensor_tensor(o, o, s_, gr, ALU.mult, ALU.mult), r, g,
                          dep=False)
            return [d, xtok] if isinstance(xtok, tuple) else [d]

        xtok = [t_x]
        for s in stages:
            if s[0] == "ffn":
                xtok = [ffn(s[1], s[2], xtok)]
            elif s[0] == "mix1":
                xtok = [mix1(xtok)]
            elif s[0] == "mix2":
                xtok = [mix2(s[1], xtok)]
            else:
                xtok = final(s[1], xtok)
        s_out = p.new_sem()
        t = p.dma(out.rearrange("(t p) d -> p t d", p=128), X[:], s_out, xtok)
        p.wait("sp", [t])

        block = ctx.enter_context(nc.Block())

        @block.sync
        def _(e):
            for f in p.q["sp"]:
                f(e)

        @block.tensor
        def _(e):
            for f in p.q["pe"]:
                f(e)

        @block.scalar
        def _(e):
            for f in p.q["act"]:
                f(e)

        @block.vector
        def _(e):
            for f in p.q["dve"]:
                f(e)

        @block.gpsimd
        def _(e):
            for f in p.q["pool"]:
                f(e)


STAGES = [("ffn", "f1", "ffn1_norm"), ("mix1",), ("ffn", "f2", "ffn2_norm"), ("final", 3),
          ("ffn", "f3", "ffn1_norm_20"), ("mix2", 0), ("ffn", "f4", "ffn2_norm_20"),
          ("ffn", "f5", "ffn1_norm_21"), ("mix2", 1), ("ffn", "f6", "ffn2_norm_21"), ("final", 4)]


def kernel(**inputs):
    import concourse.bacc as bacc
    from concourse.bass_utils import run_bass_kernel_spmd

    I = {k: np.asarray(v) for k, v in inputs.items()}
    w_in = I["w_in"][0]
    ffns = {"f1": ("ffn1", "", 0), "f2": ("ffn2", "", 0), "f3": ("ffn1", "_2", 0), "f4": ("ffn2", "_2", 0),
            "f5": ("ffn1", "_2", 1), "f6": ("ffn2", "_2", 1)}
    AW, RS = 2304, 3360

    def rows_of(w):
        return w.reshape(w.shape[0] // 128, 128, w.shape[1]).transpose(1, 0, 2)

    def block(c):
        who, what, j, w = c
        if what in ("gu", "down"):
            n, sfx, l = ffns[who]
            if what == "gu":
                a = [rows_of(I[f"{n}_w_{g}{sfx}"][l][:, j * 128:(j + 1) * 128]) for g in ("gate", "up")]
                return np.stack(a, 1)
            return rows_of(I[f"{n}_w_down{sfx}"][l][j * 256:(j + 1) * 256])
        if who == "mix1":
            if what == "lora":
                c0 = AW + 3072 + 256 * j
                if j == 1:
                    return rows_of(np.pad(w_in[:, c0:c0 + 32], ((0, 0), (0, 96))))
                return rows_of(w_in[:, c0:c0 + 256])
            if what == "qkv":
                if j == 8:
                    return rows_of(w_in[:, 2048:2304])
                return rows_of(w_in[(j % 2) * 512:(j % 2) * 512 + 512, (j // 2) * 512:(j // 2) * 512 + 512])
            if what == "gate":
                c0 = AW + RS + (j // 2) * 512
                return rows_of(w_in[(j % 2) * 512:(j % 2) * 512 + 512, c0:c0 + 512])
            if what == "up":
                return rows_of(I["attn_w_up"][0])
            if what in "kvr":
                c0 = AW + {"r": 0, "k": 1024, "v": 2048}[what] + 256 * j
                return rows_of(w_in[:, c0:c0 + 256])
            return rows_of(I["rwkv_w_out" if what == "wout" else "w_o"][0][j * 256:(j + 1) * 256])
        if what == "in2":
            wi = I["w_in_2"][who]
            if j == 12:
                return rows_of(wi[:, 3072:3080])
            return rows_of(wi[(j % 2) * 512:(j % 2) * 512 + 512, (j // 2) * 512:(j // 2) * 512 + 512])
        if what == "uq":
            return rows_of(I["c_w_uq_2"][who])
        if what == "ukv":
            return rows_of(I["c_w_ukv_2"][who])
        return rows_of(I["w_out_2"][who][j * 256:(j + 1) * 256])

    chunks = plan(STAGES)
    wall = np.empty(sum(128 * c[3] for c in chunks), np.float32)
    at = 0
    for c in chunks:
        n = 128 * c[3]
        wall[at:at + n].reshape(128, -1)[:] = block(c).reshape(128, -1)
        at += n

    clay, NCOL = col_layout()
    cols = np.zeros((128, NCOL), np.float32)

    def put(name, v, at=0):
        a, w = clay[name]
        n = v.size // 128
        cols[:, a + at:a + at + n] = v.reshape(n, 128).T

    for n in ("ffn1_norm", "mix_norm", "ffn2_norm"):
        put(n, I[n][0])
        for l in range(2):
            put(f"{n}_2{l}", I[n + "_2"][l])
    mu = I["rwkv_mu"][0]
    put("mu", mu[3072:3328], 0)
    cols[0:32, clay["mu"][0] + 2] = mu[3328:3360]
    for i, o in enumerate((1024, 2048, 0)):
        put("mu", mu[o:o + 1024], 3 + 8 * i)
    for n, k in (("w0", "rwkv_w0"), ("a0", "rwkv_a0"), ("kk", "rwkv_k_k"), ("ka", "rwkv_k_a"), ("rk", "rwkv_r_k")):
        put(n, I[k][0].reshape(-1))
    for l in range(2):
        put(f"cq{l}", I["c_q_norm_2"][l])
        put(f"ckv{l}", I["c_kv_norm_2"][l])
    rows = np.zeros((5, 2048), np.float32)
    rows[0] = I["gate_bias"][0]
    rows[1, :1024], rows[2, :1024] = I["rwkv_ln_w"][0], I["rwkv_ln_b"][0]
    rows[3, :1024], rows[4, :1024] = I["final_norm"], I["final_norm_2"]
    lorap = np.zeros((3, 128, 1024), np.float32)
    lorap[0, :64], lorap[0, 64:] = I["rwkv_w2"][0], I["rwkv_a2"][0]
    lorap[1], lorap[2, :32] = I["rwkv_g2"][0][:128], I["rwkv_g2"][0][128:]
    ebias = I["a_rel_bias_2"][:, :, np.clip(np.arange(384) - 127, -63, 128) + 63]

    arrays = {"x": np.ascontiguousarray(I["x"][0]), "wall": wall, "consts": const_table()[1], "cols": cols,
              "rows": rows, "lorap": lorap, "ebias": np.ascontiguousarray(ebias)}
    nc = bacc.Bacc("TRN2", target_bir_lowering=False, num_devices=1)
    aps = [nc.dram_tensor(n, a.shape, mybir.dt.from_np(a.dtype), kind="ExternalInput").ap() for n, a in arrays.items()]
    o = nc.dram_tensor("out", (256, 1024), F32, kind="ExternalOutput").ap()
    build(nc, STAGES, *aps, o)
    r = run_bass_kernel_spmd(nc, [arrays], core_ids=[0])
    return r.results[0]["out"].reshape(1, 256, 1024)
```

```python
from contextlib import ExitStack
import math

import numpy as np

import concourse.bass as bass
from concourse import mybir

F32 = mybir.dt.float32
F32R = mybir.dt.float32r
ALU = mybir.AluOpType
ACT = mybir.ActivationFunctionType
AX = mybir.AxisListType.X

D = 1024
FF = 2816
NM = FF // 128
NIN2 = 3080
NEG = -1e30
DECAY = -math.exp(-0.5)
CW = 2048


def plan(stages):
    out = []

    def ffn(w):
        for m in range(NM + 1):
            if m < NM:
                out.append((w, "gu", m, 2048))
            if m >= 2 and m % 2 == 0:
                out.append((w, "down", m // 2 - 1, 2048))

    for s in stages:
        if s[0] == "ffn":
            ffn(s[1])
        elif s[0] == "mix1":
            out.append(("mix1", "lora", 0, 2048))
            out.append(("mix1", "lora", 1, 1024))
            for j in range(4):
                out += [("mix1", "qkv", 2 * j, 2048), ("mix1", "qkv", 2 * j + 1, 2048)]
            out.append(("mix1", "qkv", 8, 2048))
            for j in range(8):
                out.append(("mix1", "gate", j, 2048))
            out.append(("mix1", "up", 0, 2048))
            for g in range(4):
                for q in "kvr":
                    out.append(("mix1", q, g, 2048))
            for j in range(4):
                out.append(("mix1", "wout", j, 2048))
            for j in range(4):
                out.append(("mix1", "wo", j, 2048))
        elif s[0] == "mix2":
            l = s[1]
            out.append((l, "in2", 12, 64))
            for j in (0, 1, 2, 3, 4, 5, 6, 7, 8, 9, 10, 11):
                out.append((l, "in2", j, 2048))
            out.append((l, "uq", 0, 1440))
            out.append((l, "ukv", 0, 1280))
            for j in range(4):
                out.append((l, "wout2", j, 2048))
    return out


def const_table():
    p = np.arange(128)
    cols = {}
    parts = []
    at = 0

    def put(name, a):
        nonlocal at
        a = np.asarray(a, np.float32).reshape(128, -1)
        cols[name] = (at, a.shape[1])
        parts.append(a)
        at += a.shape[1]

    put("ident", np.eye(128))
    put("anti", np.eye(128)[:, ::-1])
    put("hsel", (p[:, None] // 64 == np.arange(2)[None, :]))
    s = p[:, None] % 64
    t = np.arange(64)[None, :]
    put("mar", np.stack([s < t, s <= t], 1))
    put("mlow", t < s)
    put("i64", t == s)

    def lower(k):
        return (s >> (k + 1) == t >> (k + 1)) & ((s >> k) % 2 == 1) & ((t >> k) % 2 == 0)

    def upper(k):
        return (s >> (k + 1) == t >> (k + 1)) & ((s >> k) % 2 == 0) & ((t >> k) % 2 == 1)

    put("m0", lower(0))
    put("m0t", upper(0))
    for k in range(1, 6):
        put(f"m{k}", lower(k))
    put("half", np.full((128, 2), -0.5))
    f = np.float32

    def tables(theta, d):
        half = d // 2
        inv = np.power(f(theta), -(np.arange(half, dtype=f) * f(2.0 / d))).astype(f)
        ang = (np.arange(256, dtype=f)[:, None] * inv[None, :]).astype(f)
        sh = lambda a: a.reshape(2, 128, half).transpose(1, 0, 2)
        return sh(np.cos(ang)), sh(np.sin(ang))

    for name, th, d in (("r16", 500000.0, 16), ("r64", 10000.0, 64), ("r32", 10000.0, 32)):
        c, sn = tables(th, d)
        put(name + "c", c)
        put(name + "s", sn)
    base = at
    for tt in range(2):
        tq = (128 * tt + p)[:, None]
        sk = np.arange(128 * (tt + 1))[None, :]
        ok = [(sk <= tq) & (tq - sk <= 128), (sk <= tq) & ((tq - sk) % 4 == 0), (sk <= tq) & ((tq - sk) % 16 == 0)]
        put(f"dil{tt}", np.where(np.stack(ok, 1), 0.0, NEG))
    return cols, np.concatenate(parts, 1), base


def col_layout():
    names = [("ffn1_norm", 8), ("mix_norm", 8), ("ffn2_norm", 8), ("mu", 27), ("w0", 8), ("a0", 8), ("kk", 8),
             ("ka", 8), ("rk", 8)]
    for l in range(2):
        names += [(f"ffn1_norm_2{l}", 8), (f"mix_norm_2{l}", 8), (f"ffn2_norm_2{l}", 8), (f"cq{l}", 3), (f"ckv{l}", 2)]
    at, out = 0, {}
    for n, w in names:
        out[n] = (at, w)
        at += w
    return out, at


class Call:

    def matmul(self, *a, **k):
        return lambda e: e.matmul(*a, **k)

    def transpose(self, *a, **k):
        return lambda e: e.transpose(*a, **k)

    def activation(self, *a, **k):
        return lambda e: e.activation(*a, **k)

    def tensor_tensor(self, *a, **k):
        return lambda e: e.tensor_tensor(*a, **k)

    def tensor_scalar(self, *a, **k):
        return lambda e: e.tensor_scalar(*a, **k)

    def scalar_tensor_tensor(self, *a, **k):
        return lambda e: e.scalar_tensor_tensor(*a, **k)

    def tensor_reduce(self, *a, **k):
        return lambda e: e.tensor_reduce(*a, **k)

    def tensor_copy(self, *a, **k):
        return lambda e: e.tensor_copy(*a, **k)

    def memset(self, *a, **k):
        return lambda e: e.memset(*a, **k)

    def reciprocal(self, *a, **k):
        return lambda e: e.reciprocal(*a, **k)

    def tensor_tensor_scan(self, *a, **k):
        return lambda e: e.tensor_tensor_scan(*a, **k)

    def max(self, *a, **k):
        return lambda e: e.max(*a, **k)

    def match_replace(self, *a, **k):
        return lambda e: e.match_replace(*a, **k)


CALL = Call()


class Prog:

    def __init__(self, nc, ctx):
        self.nc, self.ctx = nc, ctx
        self.q = {e: [] for e in ("pe", "act", "dve", "pool", "sp")}
        self.sem = {e: ctx.enter_context(nc.semaphore(f"s_{e}")) for e in ("pe", "act", "dve", "pool")}
        self.n = {e: 0 for e in self.sem}
        self.seen = {}
        self.nsem = 0

    def wait(self, eng, toks):
        for t in toks:
            if t is None:
                continue
            if not (len(t) == 2 and isinstance(t[1], int)):
                self.wait(eng, t)
                continue
            s, v = t
            key = (eng, id(s))
            if self.seen.get(key, 0) < v:
                self.seen[key] = v
                self.q[eng].append(lambda e, s=s, v=v: e.wait_ge(s, v))

    def last(self, eng):
        return (self.sem[eng], self.n[eng]) if self.n[eng] else None

    def op(self, eng, fn, *toks, dep=True, sig=True):
        fn = fn(CALL)
        self.wait(eng, toks)
        if dep and eng != "pe":
            self.wait(eng, [self.last(eng)])
        if not sig:
            self.q[eng].append(fn)
            return None
        s = self.sem[eng]
        self.q[eng].append(lambda e: fn(e).then_inc(s, 1))
        self.n[eng] += 1
        return (s, self.n[eng])

    def pe(self, fn, *t, sig=False):
        return self.op("pe", fn, *t, sig=sig)

    def act(self, fn, *t, dep=True):
        return self.op("act", fn, *t, dep=dep)

    def dve(self, fn, *t, dep=True):
        return self.op("dve", fn, *t, dep=dep)

    def pool(self, fn, *t, dep=True):
        return self.op("pool", fn, *t, dep=dep)

    def new_sem(self):
        self.nsem += 1
        return [self.ctx.enter_context(self.nc.semaphore(f"d{self.nsem}")), 0]

    def dma(self, dst, src, sem, *toks, eng="sp"):
        self.wait(eng, toks)
        sem[1] += 16
        s = sem[0]
        self.q[eng].append(lambda e: e.dma_start(dst, src).then_inc(s, 16))
        return (s, sem[1])


class Ring:

    def __init__(self, aps):
        self.free = [(a, []) for a in aps]

    def get(self):
        assert self.free, "no slot free"
        return self.free.pop(0)

    def put(self, ap, toks):
        self.free.append((ap, list(toks)))


def interleave(main, side, ratio=1):
    side_on = True
    for _ in main:
        for _ in range(ratio):
            if side_on and next(side, 0) == 0:
                side_on = False
    for _ in side:
        pass


def staggered(gens, depth):
    gens = iter(gens)
    live = []
    while True:
        if len(live) < depth:
            g = next(gens, None)
            if g is not None:
                live.append(g)
        if not live:
            return
        for g in list(live):
            if next(g, 0) == 0:
                live.remove(g)
        yield 1


def build(nc, stages, x_in, wall, consts, cols, rows, lorap, ebias, out):
    ctab, carr, cbase = const_table()
    NCON = carr.shape[1]
    clay, NCOL = col_layout()
    with ExitStack() as ctx:
        p = Prog(nc, ctx)

        def sb(name, shape, dt=F32):
            return ctx.enter_context(nc.sbuf_tensor(name, shape, dt))

        X = sb("X", [128, 2, 1024])
        raw = [sb(f"raw{i}", [128, CW]) for i in range(3)]
        whi = [sb(f"whi{i}", [128, CW], F32R) for i in range(2)]
        wlo = [sb(f"wlo{i}", [128, CW], F32R) for i in range(2)]
        xh, xl = sb("xh", [128, 8, 256], F32R), sb("xl", [128, 8, 256], F32R)
        yh, yl = sb("yh", [128, 8, 256], F32R), sb("yl", [128, 8, 256], F32R)
        C = sb("C", [128, cbase])
        COL = sb("COL", [128, NCOL])
        small = sb("small", [128, 256])
        GATE = sb("GATE", [128, 2, 2048])
        NA = 22300
        arena = sb("arena", [128, NA])
        PS = ctx.enter_context(nc.psum_tensor("PS", [128, 8, 512], F32))
        bank = [PS[:, i, :] for i in range(8)]
        R = A = Ring(bank)

        def con(name):
            a, w = ctab[name]
            return C[:, a:a + w]

        def col(name, j):
            a, _ = clay[name]
            return COL[:, a + j:a + j + 1]

        class Space:
            def __init__(self, at=0):
                self.at = at

            def take(self, *shape):
                n = int(np.prod(shape))
                a = arena[:, self.at:self.at + n]
                self.at += n
                assert self.at <= NA, self.at
                if len(shape) == 1:
                    return a
                names = "abcde"[:len(shape)]
                return a.rearrange(f"p ({' '.join(names)}) -> p {' '.join(names)}",
                                   **{n_: s_ for n_, s_ in zip(names, shape)})

        ident = con("ident")
        sem_c, sem_x, sem_col = p.new_sem(), p.new_sem(), p.new_sem()
        t_x = p.dma(X[:], x_in.rearrange("(t p) d -> p t d", p=128), sem_x)
        t_c = p.dma(C[:], consts[:, 0:cbase], sem_c)
        t_col = p.dma(COL[:], cols, sem_col)

        chunks = plan(stages)
        offs = np.cumsum([0] + [128 * c[3] for c in chunks])
        raw_sem = [p.new_sem() for _ in range(3)]
        RAWN, SPL = 3, 2
        st = {"dma": 0, "split": 0, "use": 0}
        land, split_tok, use_tok, info = {}, {}, {}, {}

        def feed_dma():
            i = st["dma"]
            if i >= len(chunks):
                return
            w = chunks[i][3]
            src = wall[int(offs[i]):int(offs[i + 1])].rearrange("(p w) -> p w", p=128)
            land[i] = p.dma(raw[i % RAWN][:, 0:w], src, raw_sem[i % RAWN],
                            split_tok[i - RAWN] if i >= RAWN else [])
            st["dma"] += 1

        def feed_split():
            i = st["split"]
            if i >= len(chunks):
                return
            w = chunks[i][3]
            free = use_tok[i - SPL] if i >= SPL else None
            r = raw[i % RAWN][:, 0:w]
            hi, lo = whi[i % SPL][:, 0:w], wlo[i % SPL][:, 0:w]
            a = p.act(lambda e: e.activation(hi, r, ACT.Copy), land[i], free, dep=False)
            d = p.dve(lambda e: e.tensor_tensor(lo, r, hi.bitcast(F32), ALU.subtract), land[i], a, free, dep=False)
            split_tok[i] = [a, d]
            st["split"] += 1
            feed_dma()

        for _ in range(RAWN):
            feed_dma()
        feed_split()

        def take(key):
            i = st["use"]
            assert chunks[i][:3] == key, (chunks[i], key)
            w = chunks[i][3]
            while st["split"] <= i:
                feed_split()
            return whi[i % SPL][:, 0:w], wlo[i % SPL][:, 0:w], split_tok[i]

        def done(tok):
            use_tok[st["use"]] = tok
            st["use"] += 1
            if st["split"] <= st["use"]:
                feed_split()

        def mm3(o, wa, wb, xa, xb, first, last, toks, sig=False):
            p.pe(lambda e: e.matmul(o, wa, xa, start=first, stop=False), *toks)
            p.pe(lambda e: e.matmul(o, wa, xb, start=False, stop=False))
            return p.pe(lambda e: e.matmul(o, wb, xa, start=False, stop=last), sig=sig)

        def transpose(o, i, *toks, sig=False, id_=None):
            k = i.shape[0]
            idn = ident if id_ is None else id_
            return p.pe(lambda e: e.transpose(o, i, idn[0:k, 0:k]), *toks, sig=sig)

        def rstd(src, n, width, eps, toks):
            a = p.pool(lambda e: e.tensor_scalar(src, src, 1.0 / width, eps, ALU.mult, ALU.add), toks)
            h = con("half")[:, 0:1]
            hb = h.to_broadcast([128, n])
            return p.pool(lambda e: e.tensor_tensor(src, src, hb, ALU.pow), a, t_c)

        def sumsq(src2, width, scratch, toks):
            ts = []
            for tt in range(2):
                s_, o_, acc = src2[:, tt, :], scratch[:, tt, :], small[:, tt:tt + 1]
                ts.append(p.act(lambda e, s_=s_, o_=o_, acc=acc: e.activation(o_, s_, ACT.Square, accum_out=acc),
                                toks))
            return rstd(small[:, 0:2], 2, width, 1e-6, ts)

        def to_channels(src2, n, gain, hi, lo, toks, k0=0):
            out = []
            for k in range(0, n, 2):
                b, free = R.get()
                ks = list(range(k, min(n, k + 2)))
                for kk in ks:
                    for tt in range(2):
                        o = b[:, (kk - k) * 256 + tt * 128:(kk - k) * 256 + tt * 128 + 128]
                        i = src2[:, tt, kk * 128:(kk + 1) * 128]
                        t = transpose(o, i, toks, free, t_c, sig=(kk == ks[-1] and tt == 1))
                a, ls = None, []
                for kk in ks:
                    o, i = hi[:, k0 + kk, :], b[:, (kk - k) * 256:(kk - k) * 256 + 256]
                    if gain:
                        g = col(gain, kk)
                        a = p.act(lambda e, o=o, i=i, g=g: e.activation(o, i, ACT.Copy, scale=g), t, t_col,
                                  dep=False)
                    else:
                        a = p.act(lambda e, o=o, i=i: e.activation(o, i, ACT.Copy), t, dep=False)
                for kk in ks:
                    o, h, i = lo[:, k0 + kk, :], hi[:, k0 + kk, :].bitcast(F32), b[:, (kk - k) * 256:(kk - k) * 256 + 256]
                    if gain:
                        g = col(gain, kk)
                        d = p.dve(lambda e, o=o, i=i, g=g, h=h: e.scalar_tensor_tensor(o, i, g, h, ALU.mult, ALU.subtract),
                                  a, t_col, dep=False)
                    else:
                        d = p.dve(lambda e, o=o, i=i, h=h: e.tensor_tensor(o, i, h, ALU.subtract), a, dep=False)
                R.put(b, [d])
                out += [a, d]
            return out

        def norm_channels(gain, xtok, free):
            xn = Space().take(2, 1024)
            r = sumsq(X, 1024, xn, [xtok, free])
            ts = []
            for tt in range(2):
                o, i, s_ = xn[:, tt, :], X[:, tt, :], small[:, tt:tt + 1]
                if tt == 0:
                    ts.append(p.act(lambda e, o=o, i=i, s_=s_: e.activation(o, i, ACT.Copy, scale=s_), r))
                else:
                    ts.append(p.dve(lambda e, o=o, i=i, s_=s_: e.tensor_scalar(o, i, s_, None, ALU.mult), r, ts))
            return to_channels(xn, 8, gain, xh, xl, ts)

        def down_like(key_fn, n, lhs, toks_fn, banks, frees, kper=2):
            for j in range(n):
                hi, lo, w = take(key_fn(j))
                h3 = hi.rearrange("p (k n) -> p k n", k=kper)
                l3 = lo.rearrange("p (k n) -> p k n", k=kper)
                for kk in range(kper):
                    k = j * kper + kk
                    for tt in range(2):
                        a, b = lhs(k, tt)
                        for nn in range(2):
                            o = banks[2 * tt + nn]
                            first, last = k == 0, k == n * kper - 1
                            wh_, wl_ = h3[:, kk, nn * 512:nn * 512 + 512], l3[:, kk, nn * 512:nn * 512 + 512]
                            t = mm3(o, a, b, wh_, wl_, first, last, [w, toks_fn(k), frees if k == 0 else None],
                                    sig=(kk == kper - 1 and tt == 1 and nn == 1))
                done(t)
                yield t

        def residual(banks, scale, tok):
            for tt in range(2):
                for nn in range(2):
                    o = X[:, tt, nn * 512:nn * 512 + 512]
                    b = banks[2 * tt + nn]
                    d = p.dve(lambda e, o=o, b=b: e.scalar_tensor_tensor(o, b, scale, o, ALU.mult, ALU.add), tok,
                              dep=(tt == 0 and nn == 0))
                    A.put(b, [d])
            return d

        def ffn(which, gain, xtok):
            xt = norm_channels(gain, xtok, None)
            sg = [small_buf(i) for i in range(2)]
            hring = Ring([(yh[:, i, :], yl[:, i, :]) for i in range(5)])
            sgr = Ring(sg)
            got = [A.get() for _ in range(4)]
            banks, frees = [b for b, _ in got], [f for _, f in got]
            hs = {}

            def gu(m):
                hi, lo, w = take((which, "gu", m))
                b, free = R.get()
                for g in range(2):
                    for k in range(8):
                        c0 = (g * 8 + k) * 128
                        t = mm3(b[:, g * 256:(g + 1) * 256], hi[:, c0:c0 + 128], lo[:, c0:c0 + 128], xh[:, k, :],
                                xl[:, k, :], k == 0, k == 7, [w, xt, free], sig=(k == 7))
                done(t)
                s_, sf = sgr.get()
                a = p.act(lambda e: e.activation(s_, b[:, 0:256], ACT.Silu), t, sf, dep=False)
                d = p.dve(lambda e: e.tensor_tensor(s_, s_, b[:, 256:512], ALU.mult), a, dep=False)
                R.put(b, [d])
                (hh, hl), hf = hring.get()
                a = p.act(lambda e: e.activation(hh, s_, ACT.Copy), d, hf, dep=False)
                d = p.dve(lambda e: e.tensor_tensor(hl, s_, hh.bitcast(F32), ALU.subtract), a, hf, dep=False)
                sgr.put(s_, [a, d])
                hs[m] = (hh, hl, [a, d])

            def lhs(k, tt):
                hh, hl, _ = hs[k]
                return hh[:, tt * 128:(tt + 1) * 128], hl[:, tt * 128:(tt + 1) * 128]

            dn = down_like(lambda j: (which, "down", j), NM // 2, lhs, lambda k: hs[k][2], banks, frees)
            for m in range(NM + 1):
                if m < NM:
                    gu(m)
                if m >= 2 and m % 2 == 0:
                    t = next(dn)
                    for k in (m - 2, m - 1):
                        hring.put(hs[k][:2], [t])
            return residual(banks, 0.5, t)

        smb = [arena[:, 20000 + 256 * i:20256 + 256 * i] for i in range(2)]

        def small_buf(i):
            return smb[i]

        def soften(S, n, toks, nm, den):
            d = p.dve(lambda e: e.tensor_reduce(nm, S, AX, ALU.max, negate=True), toks)
            a = p.act(lambda e: e.activation(S, S, ACT.Exp, bias=nm, accum_out=den), d)
            return a, p.dve(lambda e: e.reciprocal(den, den), a)

        def turn_and_weigh(S, blocks, values, PT, ptfree, a, rden, o, extra, ofree):
            ts = []
            for b0 in range(0, blocks, 4):
                b, free = R.get()
                nb = min(4, blocks - b0)
                for i in range(nb):
                    t = transpose(b[:, i * 128:(i + 1) * 128], S[:, (b0 + i) * 128:(b0 + i + 1) * 128], a, free,
                                  t_c, sig=(i == nb - 1))
                dst = PT[:, b0 * 128:(b0 + nb) * 128]
                c = p.act(lambda e, dst=dst, b=b, nb=nb: e.activation(dst, b[:, 0:nb * 128], ACT.Copy), t, ptfree,
                          dep=False)
                R.put(b, [c])
                ts.append(c)
            yield 1
            b, free = R.get()
            dv = o.shape[1]
            for i in range(blocks):
                t = p.pe(lambda e, i=i: e.matmul(b[:, 0:dv], PT[:, i * 128:(i + 1) * 128], values[i],
                                                 start=(i == 0), stop=(i == blocks - 1)), ts, free, extra,
                         sig=(i == blocks - 1))
            d = p.dve(lambda e: e.tensor_scalar(o, b[:, 0:dv], rden, None, ALU.mult), t, ofree)
            R.put(b, [d])
            self_done.append((t, d))

        self_done = []

        def rope(src, dst, tt, nh, hd, off, half, name, tmp, toks):
            c = con(name + "c")[:, tt * half:(tt + 1) * half].unsqueeze(1).to_broadcast([128, nh, half])
            s_ = con(name + "s")[:, tt * half:(tt + 1) * half].unsqueeze(1).to_broadcast([128, nh, half])
            sv = src.rearrange("p (h d) -> p h d", d=hd)
            dv_ = dst.rearrange("p (h d) -> p h d", d=hd)
            x1, x2 = sv[:, :, off:off + half], sv[:, :, off + half:off + 2 * half]
            o1, o2 = dv_[:, :, off:off + half], dv_[:, :, off + half:off + 2 * half]
            n = nh * half
            tv = [tmp[:, i * n:(i + 1) * n].rearrange("p (h d) -> p h d", d=half) for i in range(4)]
            p.dve(lambda e: e.tensor_tensor(tv[0], x1, c, ALU.mult), toks, t_c)
            p.dve(lambda e: e.tensor_tensor(tv[1], x2, s_, ALU.mult), dep=False)
            p.dve(lambda e: e.tensor_tensor(tv[2], x2, c, ALU.mult), dep=False)
            p.dve(lambda e: e.tensor_tensor(tv[3], x1, s_, ALU.mult), dep=False)
            p.dve(lambda e: e.tensor_tensor(o1, tv[0], tv[1], ALU.subtract))
            return p.dve(lambda e: e.tensor_tensor(o2, tv[2], tv[3], ALU.add), dep=False)

        def proj_b(keys, dsts, xt, evac):
            got = [A.get() for _ in range(2)]
            nk = 8 // len(keys)
            w = 0
            for j, key in enumerate(keys):
                hi, lo, wt = take(key)
                w = hi.shape[1] // nk
                for kk in range(nk):
                    k = j * nk + kk
                    for tt in range(2):
                        b, free = got[tt]
                        t = mm3(b[:, 0:w], xh[:, k, tt * 128:(tt + 1) * 128], xl[:, k, tt * 128:(tt + 1) * 128],
                                hi[:, kk * w:(kk + 1) * w], lo[:, kk * w:(kk + 1) * w], k == 0, k == 7,
                                [wt, xt, free if k == 0 else None], sig=(kk == nk - 1 and tt == 1))
                done(t)
                if j < len(keys) - 1:
                    yield 1
            for tt in range(2):
                b, _ = got[tt]
                A.put(b, [evac(tt, b[:, 0:w], t)])
            yield 1

        def mix1(xtok):
            xt = norm_channels("mix_norm", xtok, None)
            after_norm = [p.last("pe"), p.last("act"), p.last("dve")]
            sp = Space()
            zl = sp.take(3, 256)
            rbase = sp.at
            QKV = sp.take(2, 2304)
            DM = [sp.take(384), sp.take(768)]
            GB = sp.take(2048)
            qT = sp.take(6, 256)
            kz = sp.take(12, 256)
            Sb = [sp.take(768) for _ in range(3)]
            PTb = [sp.take(768) for _ in range(2)]
            AO = sp.take(2, 256)
            rt = sp.take(4 * 24 * 8)
            z = sp.take(2, 257)
            ztmp = sp.take(2, 256)
            sem = p.new_sem()
            for tt in range(2):
                a_, w_ = ctab[f"dil{tt}"]
                t_dm = p.dma(DM[tt], consts[:, a_:a_ + w_], sem, after_norm, eng="pool")
            sem = p.new_sem()
            t_gb = p.dma(GB, rows[0:1, 0:2048].to_broadcast([128, 2048]), sem, after_norm, eng="pool")
            zk = p.pool(lambda e: e.memset(kz, 0.0), after_norm)
            z0 = p.pool(lambda e: e.memset(z[:, :, 0:1], 0.0))

            def shift(key, n, w, dst, mus, zz, zt, zfree, dfree=None):
                hi, lo, wt = take(key)
                b, free = A.get()
                for j in range(n):
                    for k in range(8):
                        c0 = k * n * w + j * w
                        t = mm3(b[0:w, j * 256:(j + 1) * 256], hi[:, c0:c0 + w], lo[:, c0:c0 + w], xh[:, k, :],
                                xl[:, k, :], k == 0, k == 7, [wt, xt, free], sig=(k == 7))
                        if k % 4 == 3 and (j, k) != (n - 1, 7):
                            yield 1
                done(t)
                bb = b.rearrange("p (n t) -> p n t", n=2)[0:w, 0:n, :]
                c = p.act(lambda e: e.activation(zz[0:w, 0:n, 1:257], bb, ACT.Copy), t, zfree, z0, dep=False)
                A.put(b, [c])
                yield 1
                d = p.dve(lambda e: e.tensor_tensor(zt[0:w, 0:n, :], zz[0:w, 0:n, 0:256], zz[0:w, 0:n, 1:257],
                                                    ALU.subtract), c, dfree)
                for j in range(n):
                    m_ = col("mu", mus[j])[0:w]
                    d = p.dve(lambda e: e.scalar_tensor_tensor(
                        dst[0:w, j, :], zt[0:w, j, :], m_, zz[0:w, j, 1:257], ALU.mult, ALU.add), t_col,
                        dep=(j == 0))
                yield 1
                return d

            def run(gen):
                while True:
                    try:
                        next(gen)
                    except StopIteration as s_:
                        return s_.value

            d = run(shift(("mix1", "lora", 0), 2, 128, zl, [0, 1], z, ztmp, None))
            d = run(shift(("mix1", "lora", 1), 1, 128, zl[:, 2:3, :], [2], z, ztmp, d))
            p.act(lambda e: e.activation(zl[0:64, 0, :], zl[0:64, 0, :], ACT.Tanh), d)
            p.act(lambda e: e.activation(zl[:, 1, :], zl[:, 1, :], ACT.Tanh, scale=0.5), d, dep=False)
            a = p.act(lambda e: e.activation(zl[:, 2, :], zl[:, 2, :], ACT.Tanh, scale=0.5), d, dep=False)
            p.dve(lambda e: e.tensor_scalar(zl[:, 1, :], zl[:, 1, :], 0.5, 0.5, ALU.mult, ALU.add), a)
            t_zl = p.dve(lambda e: e.tensor_scalar(zl[:, 2, :], zl[:, 2, :], 0.5, 0.5, ALU.mult, ALU.add),
                         dep=False)

            def qkv_chunks():
                for j in range(5):
                    keys = [("mix1", "qkv", 2 * j), ("mix1", "qkv", 2 * j + 1)] if j < 4 else [("mix1", "qkv", 8)]

                    def evac(tt, b, t, j=j):
                        o = QKV[:, tt, j * 512:j * 512 + b.shape[1]]
                        return p.act(lambda e: e.activation(o, b, ACT.Copy), t, after_norm, dep=False)
                    yield from proj_b(keys, None, xt, evac)

            for _ in qkv_chunks():
                pass
            tq = p.last("act")
            r_ = []
            for tt in range(2):
                r_.append(rope(QKV[:, tt, 0:1536], QKV[:, tt, 0:1536], tt, 24, 64, 0, 8, "r16", rt, [tq]))

            def gates():
                for j in range(4):
                    def evac(tt, b, t, j=j):
                        o = GATE[:, tt, j * 512:(j + 1) * 512]
                        gb = GB[:, j * 512:(j + 1) * 512]
                        d = p.dve(lambda e: e.tensor_tensor(o, b, gb, ALU.add), t, t_gb, dep=False)
                        a = p.act(lambda e: e.activation(o, o, ACT.Tanh, scale=0.5), d, dep=False)
                        p.pool(lambda e: e.tensor_scalar(o, o, 0.5, 0.5, ALU.mult, ALU.add), a, dep=False)
                        return d
                    yield from proj_b([("mix1", "gate", 2 * j), ("mix1", "gate", 2 * j + 1)], None, xt, evac)

            def attention():
                kv = []
                for j in range(12):
                    b, free = R.get()
                    for tt in range(2):
                        t = transpose(b[:, tt * 128:(tt + 1) * 128], QKV[:, tt, j * 128:(j + 1) * 128], r_, free, t_c,
                                      sig=(tt == 1))
                    if j < 6:
                        c = p.act(lambda e, j=j, b=b: e.activation(qT[:, j, :], b[:, 0:256], ACT.Copy), t, dep=False)
                    else:
                        for q in range(2):
                            o = kz[64 * q:64 * q + 64, 2 * (j - 6) + q, :]
                            i_ = b[64 * q:64 * q + 64, 0:256]
                            c = p.act(lambda e, o=o, i_=i_: e.activation(o, i_, ACT.Copy), t, zk, dep=False)
                    R.put(b, [c])
                    kv.append(c)
                    if j % 3 == 2:
                        yield 1
                Sr, Pr = Ring(Sb), Ring(PTb)
                stat = Ring([small[:, 8 + 2 * i:10 + 2 * i] for i in range(4)])

                def unit(hh, tt):
                    S, sfree = Sr.get()
                    sv_, stf = stat.get()
                    nm, den = sv_[:, 0:1], sv_[:, 1:2]
                    W = 128 * (tt + 1)
                    groups = [[0, 1, 2]] if tt == 0 else [[0, 1], [2]]
                    ds = []
                    for gs in groups:
                        b, free = R.get()
                        for i, g in enumerate(gs):
                            q = qT[:, 2 * g + hh // 2, tt * 128:(tt + 1) * 128]
                            k_ = kz[:, 4 * g + hh, 0:W]
                            o = b[:, i * W:(i + 1) * W]
                            t = p.pe(lambda e, o=o, q=q, k_=k_: e.matmul(o, q, k_, start=True, stop=True), kv, free,
                                     sig=(i == len(gs) - 1))
                        n = len(gs) * W
                        o = S[:, gs[0] * W:gs[0] * W + n]
                        m_ = DM[tt][:, gs[0] * W:gs[0] * W + n]
                        d = p.dve(lambda e, o=o, b=b, m_=m_, n=n: e.scalar_tensor_tensor(
                            o, b[:, 0:n], 0.125, m_, ALU.mult, ALU.add), t, sfree, stf, t_dm, dep=False)
                        R.put(b, [d])
                        ds.append(d)
                    a, rd = soften(S[:, 0:3 * W], 3 * W, ds, nm, den)
                    yield 1
                    PT, pf = Pr.get()
                    vals = [QKV[:, s_, 1536 + (4 * g + hh) * 64:1536 + (4 * g + hh) * 64 + 64]
                            for g in range(3) for s_ in range(tt + 1)]
                    yield from turn_and_weigh(S, 3 * (tt + 1), vals, PT, pf, a, den,
                                              AO[:, tt, hh * 64:(hh + 1) * 64], tq, None)
                    t, d = self_done.pop()
                    Sr.put(S, [t])
                    Pr.put(PT, [t])
                    stat.put(sv_, [d])
                    yield 1

                yield from staggered((unit(hh, tt) for hh in range(4) for tt in range(2)), 2)

            interleave(gates(), attention(), 2)
            ao = p.last("dve")
            tc_ = to_channels(AO, 2, None, yh, yl, [ao])
            got = [A.get() for _ in range(4)]
            banks, frees = [b for b, _ in got], [f for _, f in got]
            for t in down_like(lambda j: ("mix1", "up", 0), 1,
                               lambda k, tt: (yh[:, k, tt * 128:(tt + 1) * 128], yl[:, k, tt * 128:(tt + 1) * 128]),
                               lambda k: tc_, banks, frees):
                pass
            tg = p.last("pool")
            for tt in range(2):
                for nn in range(2):
                    o = GATE[:, tt, nn * 512:nn * 512 + 512]
                    b = banks[2 * tt + nn]
                    d = p.dve(lambda e, o=o, b=b: e.tensor_tensor(o, o, b, ALU.mult), t, tg, dep=False)
                    A.put(b, [d])
            attn_done = [p.last("pe"), p.last("act"), p.last("dve"), p.last("pool")]
            rwkv(rbase, zl, t_zl, xt, shift, attn_done)
            got = [A.get() for _ in range(4)]
            banks, frees = [b for b, _ in got], [f for _, f in got]
            ty = [p.last("act"), p.last("dve")]
            for t in down_like(lambda j: ("mix1", "wout", j), 4,
                               lambda k, tt: (yh[:, k, tt * 128:(tt + 1) * 128], yl[:, k, tt * 128:(tt + 1) * 128]),
                               lambda k: ty, banks, frees):
                pass
            for tt in range(2):
                for nn in range(2):
                    o = GATE[:, tt, 1024 + nn * 512:1024 + nn * 512 + 512]
                    g0 = GATE[:, tt, nn * 512:nn * 512 + 512]
                    b = banks[2 * tt + nn]
                    d = p.dve(lambda e, o=o, b=b: e.tensor_tensor(o, o, b, ALU.mult), t)
                    A.put(b, [d])
                    d = p.dve(lambda e, o=o, g0=g0: e.tensor_tensor(g0, g0, o, ALU.add), d)
            tm = to_channels(GATE[:, :, 0:1024], 8, None, yh, yl, [d, t])
            got = [A.get() for _ in range(4)]
            banks, frees = [b for b, _ in got], [f for _, f in got]
            for t in down_like(lambda j: ("mix1", "wo", j), 4,
                               lambda k, tt: (yh[:, k, tt * 128:(tt + 1) * 128], yl[:, k, tt * 128:(tt + 1) * 128]),
                               lambda k: tm, banks, frees):
                pass
            return residual(banks, 1.0, t)

        def rwkv(base, zl, t_zl, xt, shift, start):
            sp = Space(base)
            KZV = [{q: sp.take(2, 256) for q in "kvr"} for _ in range(2)]
            z = [sp.take(2, 257) for _ in range(2)]
            zt = sp.take(2, 256)
            zs = []
            for t_ in z:
                zs.append(p.pool(lambda e: e.memset(t_[:, :, 0:1], 0.0), start))
            kzv_free = [start, start]
            kzv_ready, groups_done = {}, set()

            def projections():
                prev = [None, None]
                for G in range(4):
                    while G >= 2 and not {2 * G - 4, 2 * G - 3} <= groups_done:
                        yield 1
                    for i, q in enumerate("kvr"):
                        d = yield from shift(("mix1", q, G), 2, 128, KZV[G % 2][q],
                                             [3 + 8 * i + 2 * G, 4 + 8 * i + 2 * G], z[i % 2], zt,
                                             [kzv_free[G % 2], prev[i % 2], zs], dfree=kzv_free[G % 2])
                        prev[i % 2] = d
                        kzv_ready[(q, G)] = d

            class Slot:
                def __init__(self):
                    self.LW, self.LG, self.LN = sp.take(128), sp.take(2, 128), sp.take(2, 128)
                    self.wd, self.aa, self.kk, self.kp, self.rn = [sp.take(256) for _ in range(5)]
                    self.Pi, self.Px, self.iP, self.w1 = [sp.take(256) for _ in range(4)]
                    self.BK = sp.take(512)
                    self.ARz = sp.take(2, 4, 2, 64)
                    self.Vt, self.Bt, self.Kt = [sp.take(256) for _ in range(3)]
                    self.Vz = sp.take(4, 128)
                    self.TB, self.TK = sp.take(4, 128), sp.take(4, 128)
                    self.DTb, self.LTb = sp.take(4, 128), sp.take(4, 128)
                    self.Gz, self.Uz = sp.take(2, 128), sp.take(2, 128)
                    self.ST = sp.take(64)
                    self.st = sp.take(32)
                    self.sem = p.new_sem()
                    self.free = start
                    for t_ in (self.ARz, self.Vz, self.Gz, self.Uz, self.w1, self.DTb, self.LTb):
                        self.zero = p.pool(lambda e: e.memset(t_, 0.0), start)

            def halves(o, i, *toks):
                for q in range(2):
                    ps = slice(64 * q, 64 * q + 64)
                    oo, ii = o[ps, :, 64 * q:64 * q + 64], i[ps, :, :]
                    a = p.act(lambda e: e.activation(oo, ii, ACT.Copy), toks, dep=False)
                return a

            def group(g, s):
                G, j = g // 2, g % 2
                prev, z0 = s.free, s.zero
                u4 = lambda t_: t_.rearrange("p (u k) -> p u k", u=4)
                u2 = lambda t_: t_.rearrange("p (a k) -> p a k", a=2)
                wd, aa, kk, kp, rn, Pi, Px, iP, w1 = s.wd, s.aa, s.kk, s.kp, s.rn, s.Pi, s.Px, s.iP, s.w1
                ARz, Vt, Bt, Kt, Vz, TB, TK = s.ARz, s.Vt, s.Bt, s.Kt, s.Vz, s.TB, s.TK
                DTb, LTb, Gz, Uz, ST, st_ = s.DTb, s.LTb, s.Gz, s.Uz, s.ST, s.st
                bt, kt = s.BK[:, 0:256], s.BK[:, 256:512]
                L, Dm, DT, Xc, Xb = u4(aa), u4(wd), u4(kk), u4(kp), s.BK.rearrange("p (u k) -> p u k", u=4)
                Yt, sq = Px, iP
                cs = slice(g * 128, g * 128 + 128)
                p.dma(s.LW, lorap[0, :, cs], s.sem, prev, eng="pool")
                p.dma(s.LG, lorap[1:3, :, cs].rearrange("a p n -> p a n"), s.sem, eng="pool")
                tl = p.dma(s.LN, rows[1:3, cs].unsqueeze(0).to_broadcast([128, 2, 128]), s.sem, eng="pool")
                while ("k", G) not in kzv_ready:
                    yield 1
                tk_ = kzv_ready[("k", G)]
                k3 = KZV[G % 2]["k"][:, j, :]
                b, f = R.get()
                o1, o2, l1, l2 = b[:, 0:256], b[:, 256:512], s.LW[0:64], s.LW[64:128]
                p.pe(lambda e: e.matmul(o1, l1, zl[0:64, 0, :], start=True, stop=True), t_zl, tl, f, sig=True)
                p.wait("pe", [p.last("pe")])
                t1 = p.pe(lambda e: e.matmul(o2, l2, zl[64:128, 0, :], start=True, stop=True), sig=True)
                yield 1
                a = p.dve(lambda e: e.tensor_scalar(wd, o1, col("w0", g), 0.5, ALU.add, ALU.mult), t1, t_col, prev,
                          dep=False)
                a = p.dve(lambda e: e.tensor_scalar(aa, o2, col("a0", g), 0.5, ALU.add, ALU.mult), dep=False)
                R.put(b, [a])
                p.act(lambda e: e.activation(wd, wd, ACT.Tanh), a, dep=False)
                ta = p.act(lambda e: e.activation(aa, aa, ACT.Tanh), dep=False)
                d = p.dve(lambda e: e.tensor_scalar(kk, k3, col("kk", g), None, ALU.mult), tk_, prev, dep=False)
                a = p.act(lambda e: e.activation(rn, kk, ACT.Square), d, prev, dep=False)
                p.dve(lambda e: e.tensor_scalar(wd, wd, 0.5, 0.5, ALU.mult, ALU.add), ta, dep=False)
                d = p.dve(lambda e: e.tensor_scalar(aa, aa, 0.5, 0.5, ALU.mult, ALU.add), dep=False)
                ew = p.act(lambda e: e.activation(wd, wd, ACT.Exp, scale=DECAY), d, dep=False)
                b, f = R.get()
                for tt in range(2):
                    t = p.pe(lambda e: e.matmul(b[:, tt * 2:tt * 2 + 2], rn[:, tt * 128:(tt + 1) * 128],
                                                con("hsel"), start=True, stop=True), a, f, sig=(tt == 1))
                yield 1
                nrm = st_[:, 16:20]
                d = p.dve(lambda e: e.tensor_scalar(nrm, b[:, 0:4], 1e-24, None, ALU.max), t, dep=False)
                R.put(b, [d])
                hb = con("half")[:, 0:1].to_broadcast([128, 4])
                pw = p.pool(lambda e: e.tensor_tensor(nrm, nrm, hb, ALU.pow), d)
                p.dve(lambda e: e.tensor_scalar(kp, aa, 1.0, col("ka", g), ALU.subtract, ALU.mult))
                tkp = p.dve(lambda e: e.scalar_tensor_tensor(kp, kp, 1.0, k3, ALU.add, ALU.mult))
                wv, w1v, Piv, Pxv = u4(wd), u4(w1), u4(Pi), u4(Px)
                p.dve(lambda e: e.tensor_copy(w1v[:, :, 0:1], wv[:, :, 0:1]), ew, z0, dep=False)
                p.dve(lambda e: e.memset(wv[:, :, 0:1], 0.0))
                p.dve(lambda e: e.tensor_tensor_scan(Pi, wd, w1, 0.0, ALU.mult, ALU.add))
                yield 1
                p.dve(lambda e: e.tensor_copy(Pxv[:, :, 1:64], Piv[:, :, 0:63]))
                p.dve(lambda e: e.memset(Pxv[:, :, 0:1], 1.0), dep=False)
                p.dve(lambda e: e.reciprocal(iP, Pi), dep=False)
                p.dve(lambda e: e.tensor_tensor(kt, kp, iP, ALU.mult))
                wide4, nb4 = u4(rn), nrm.unsqueeze(2).to_broadcast([128, 4, 64])
                sp_ = p.dve(lambda e: e.tensor_copy(wide4, nb4), pw, dep=False)
                b, f = R.get()
                for tt in range(2):
                    trn = transpose(b[:, tt * 128:tt * 128 + 128], rn[:, tt * 128:tt * 128 + 128], sp_, f,
                                    sig=(tt == 1))
                yield 1
                while ("r", G) not in kzv_ready:
                    yield 1
                tv_, tr_ = kzv_ready[("v", G)], kzv_ready[("r", G)]
                v3, r3 = KZV[G % 2]["v"][:, j, :], KZV[G % 2]["r"][:, j, :]
                d = p.dve(lambda e: e.tensor_tensor(kk, kk, b[:, 0:256], ALU.mult), trn, dep=False)
                R.put(b, [d])
                p.dve(lambda e: e.tensor_tensor(bt, kk, aa, ALU.mult))
                p.dve(lambda e: e.tensor_tensor(bt, bt, iP, ALU.mult))
                for hh in range(2):
                    ps = slice(64 * hh, 64 * hh + 64)
                    oa, orr = ARz[ps, hh, :, 0, :], ARz[ps, hh, :, 1, :]
                    ka_, px_, r_, pi_ = u4(kk[ps]), u4(Px[ps]), u4(r3[ps]), u4(Pi[ps])
                    p.dve(lambda e: e.scalar_tensor_tensor(oa, ka_, -1.0, px_, ALU.mult, ALU.mult), z0,
                          dep=(hh == 0))
                    tar = p.dve(lambda e: e.tensor_tensor(orr, r_, pi_, ALU.mult), tr_, dep=False)
                tb_ = p.dve(lambda e: e.scalar_tensor_tensor(rn, r3, col("rk", g), kp, ALU.mult, ALU.mult))
                yield 1
                tt_ = {}
                for pair in ((("v", v3, Vt), ("b", bt, Bt)), (("k", kt, Kt),)):
                    b, f = R.get()
                    for i, (nm, src, dst) in enumerate(pair):
                        for tt in range(2):
                            t = transpose(b[:, i * 256 + tt * 128:i * 256 + tt * 128 + 128],
                                          src[:, tt * 128:(tt + 1) * 128], tb_, tv_, f, t_c,
                                          sig=(tt == 1 and i == len(pair) - 1))
                    for i, (nm, src, dst) in enumerate(pair):
                        a = p.act(lambda e: e.activation(dst, b[:, i * 256:i * 256 + 256], ACT.Copy), t, prev,
                                  dep=False)
                        tt_[nm] = a
                    R.put(b, [a])
                Vz5 = Vz.rearrange("p (a c) k -> p a c k", c=2)
                Vt3 = u2(Vt)
                for q in range(2):
                    ps = slice(64 * q, 64 * q + 64)
                    vz = p.pool(lambda e: e.tensor_copy(Vz5[ps, :, q, :], Vt3[ps, :, :]), tt_["v"], prev, z0)
                pend = []
                for nm, src, dst in (("b", bt, TB), ("k", kt, TK)):
                    b, f = R.get()
                    for u in range(4):
                        hh, tt = u // 2, u % 2
                        for q in range(2):
                            c = 2 * tt + q
                            o = b[64 * q:64 * q + 64, u * 128:(u + 1) * 128]
                            l_ = src[:, c * 64:(c + 1) * 64]
                            r_ = ARz[:, hh, c, :, :].rearrange("p a t -> p (a t)")
                            t = p.pe(lambda e: e.matmul(o, l_, r_, start=True, stop=True), f, tb_,
                                     sig=(u == 3 and q == 1))
                    pend.append((b, dst, t))
                b, f = R.get()
                for u in range(4):
                    hh, tt = u // 2, u % 2
                    for q in range(2):
                        c = 2 * tt + q
                        o = b[64 * q:64 * q + 64, u * 64:(u + 1) * 64]
                        l_, r_ = ARz[:, hh, c, 0, :], bt[:, c * 64:(c + 1) * 64]
                        t = p.pe(lambda e: e.matmul(o, l_, r_, start=True, stop=True), f, sig=(u == 3 and q == 1))
                yield 1
                m_ = con("mar").unsqueeze(1).to_broadcast([128, 4, 128])
                toks = []
                for bb, dst, t_ in pend:
                    bv = u4(bb)
                    d = p.dve(lambda e: e.tensor_tensor(dst, bv, m_, ALU.mult), t_, prev, dep=False)
                    R.put(bb, [d])
                    toks.append(d)
                t_tb, t_tk = toks
                bv, ml = u4(b[:, 0:256]), con("mlow").unsqueeze(1).to_broadcast([128, 4, 64])
                d = p.dve(lambda e: e.tensor_tensor(L, bv, ml, ALU.mult), t, dep=False)
                R.put(b, [d])
                xz = p.pool(lambda e: e.memset(Xb, 0.0), t)
                LT = TB[:, :, 0:64]
                bc = lambda n: con(n).unsqueeze(1).to_broadcast([128, 4, 64])
                lt = halves(LTb, LT, t_tb, prev, z0)
                p.dve(lambda e: e.tensor_tensor(Dm, L, bc("m0"), ALU.mult))
                p.dve(lambda e: e.tensor_tensor(DT, LT, bc("m0t"), ALU.mult), dep=False)
                p.dve(lambda e: e.tensor_tensor(Dm, Dm, bc("i64"), ALU.add))
                d = p.dve(lambda e: e.tensor_tensor(DT, DT, bc("i64"), ALU.add), dep=False)
                db = halves(DTb, DT, d, prev, z0)
                dd = d
                for k in range(1, 6):
                    b, f = R.get()
                    for u in range(4):
                        t = p.pe(lambda e: e.matmul(b[:, u * 64:(u + 1) * 64], LTb[:, u, :], Dm[:, u, :],
                                                    start=True, stop=True), f, lt, dd, sig=(u == 3))
                    bv = u4(b[:, 0:256])
                    yield 1
                    xc = p.dve(lambda e: e.tensor_tensor(Xc, bv, bc(f"m{k}"), ALU.mult), t, dep=False)
                    R.put(b, [xc])
                    xb = halves(Xb, Xc, xc, xz, db)
                    if k < 5:
                        b, f = R.get()
                        for u in range(4):
                            t = p.pe(lambda e: e.matmul(b[:, u * 64:(u + 1) * 64], DTb[:, u, :], Xc[:, u, :],
                                                        start=True, stop=True), f, db, xc, sig=(u == 3))
                    b2, f = R.get()
                    for u in range(4):
                        t2 = p.pe(lambda e: e.matmul(b2[:, u * 64:(u + 1) * 64], Xb[:, u, :], DT[:, u, :],
                                                     start=True, stop=True), f, xb, sig=(u == 3))
                    yield 1
                    if k < 5:
                        bv = u4(b[:, 0:256])
                        dd = p.dve(lambda e: e.tensor_tensor(Dm, Dm, bv, ALU.add), t, dep=False)
                        R.put(b, [dd])
                    bv = u4(b2[:, 0:256])
                    d = p.dve(lambda e: e.tensor_tensor(DT, DT, bv, ALU.add), t2, dep=False)
                    R.put(b2, [d])
                    if k < 5:
                        db = halves(DTb, DT, d)
                t_inv = d
                s_tok = None
                for c in range(4):
                    tt, q = c // 2, c % 2
                    ps = slice(64 * q, 64 * q + 64)
                    if q == 0:
                        yb, yf = R.get()
                    b, f = R.get()
                    for hh in range(2):
                        o = b[ps, hh * 64:(hh + 1) * 64]
                        u = hh * 2 + tt
                        if c:
                            p.pe(lambda e: e.matmul(o, ARz[:, hh, c, 0, :], ST, start=True, stop=False), f, s_tok)
                        t = p.pe(lambda e: e.matmul(o, TK[:, u, 0:64], Vz[:, c, hh * 64:(hh + 1) * 64],
                                                    start=(c == 0), stop=True), f, vz, t_tk, sig=(hh == 1))
                    for hh in range(2):
                        o = yb[ps, hh * 64:(hh + 1) * 64]
                        u = hh * 2 + tt
                        if c:
                            p.pe(lambda e: e.matmul(o, ARz[:, hh, c, 1, :], ST, start=(hh == 0), stop=False,
                                                    skip_group_check=True), yf)
                        t_y = p.pe(lambda e: e.matmul(o, TK[:, u, 64:128], Vz[:, c, hh * 64:(hh + 1) * 64],
                                                      start=(c == 0 and hh == 0), stop=False,
                                                      skip_group_check=True), yf, sig=(hh == 1))
                    yield 1
                    gd = p.act(lambda e: e.activation(Gz[ps, q, :], b[ps, 0:128], ACT.Copy), t, z0, prev, dep=False)
                    R.put(b, [gd])
                    b, f = R.get()
                    for hh in range(2):
                        o = b[ps, hh * 64:(hh + 1) * 64]
                        u = hh * 2 + tt
                        t = p.pe(lambda e: e.matmul(o, DT[:, u, :], Gz[:, q, hh * 64:(hh + 1) * 64], start=True,
                                                    stop=True), f, gd, t_inv, sig=(hh == 1))
                    yield 1
                    ud = p.act(lambda e: e.activation(Uz[ps, q, :], b[ps, 0:128], ACT.Copy), t, z0, prev, dep=False)
                    R.put(b, [ud])
                    if c < 3:
                        b, f = R.get()
                        for hh in range(2):
                            o = b[64 * hh:64 * hh + 64, 0:64]
                            hc = slice(tt * 128 + hh * 64, tt * 128 + hh * 64 + 64)
                            p.pe(lambda e: e.matmul(o, Bt[:, hc], Uz[:, q, hh * 64:(hh + 1) * 64], start=True,
                                                    stop=False), f, ud, tt_["b"])
                            t = p.pe(lambda e: e.matmul(o, Kt[:, hc], Vz[:, c, hh * 64:(hh + 1) * 64], start=False,
                                                        stop=True), tt_["k"], sig=(hh == 1))
                    for hh in range(2):
                        o = yb[ps, hh * 64:(hh + 1) * 64]
                        u = hh * 2 + tt
                        ty = p.pe(lambda e: e.matmul(o, TB[:, u, 64:128], Uz[:, q, hh * 64:(hh + 1) * 64],
                                                     start=False, stop=True, skip_group_check=True), ud, t_tb,
                                  sig=(hh == 1))
                    yield 1
                    if c < 3:
                        bv = b[:, 0:64]
                        pc = Pi[:, c * 64 + 63:c * 64 + 64]
                        if c:
                            p.dve(lambda e: e.tensor_tensor(ST, ST, bv, ALU.add), t, t_y, dep=False)
                            s_tok = p.dve(lambda e: e.tensor_scalar(ST, ST, pc, None, ALU.mult))
                        else:
                            s_tok = p.dve(lambda e: e.tensor_scalar(ST, bv, pc, None, ALU.mult), t, prev, dep=False)
                        R.put(b, [s_tok])
                    if q == 1:
                        yd = p.act(lambda e: e.activation(Yt[:, tt * 128:(tt + 1) * 128], yb[:, 0:128], ACT.Copy),
                                   ty, tb_, dep=False)
                        R.put(yb, [yd])
                y4, s4 = u4(Yt), u4(sq)
                mean, var = st_[:, 0:4], st_[:, 4:8]
                mb = mean.unsqueeze(2).to_broadcast([128, 4, 64])
                vb = var.unsqueeze(2).to_broadcast([128, 4, 64])
                p.dve(lambda e: e.tensor_reduce(mean, y4, AX, ALU.add), yd)
                p.dve(lambda e: e.tensor_scalar(mean, mean, 1.0 / 64, None, ALU.mult))
                d = p.dve(lambda e: e.tensor_tensor(y4, y4, mb, ALU.subtract))
                a = p.act(lambda e: e.activation(s4, y4, ACT.Square), d, dep=False)
                b1, f1 = R.get()
                for tt in range(2):
                    o = b1[:, tt * 128:(tt + 1) * 128]
                    p.pe(lambda e: e.matmul(o, zl[:, 1, tt * 128:(tt + 1) * 128], s.LG[:, 0, :], start=True,
                                            stop=False), f1, tl)
                    p.pe(lambda e: e.matmul(o, zl[:, 2, tt * 128:(tt + 1) * 128], s.LG[:, 1, :], start=False,
                                            stop=True))
                for tt in range(2):
                    t2 = p.pe(lambda e: e.matmul(b1[:, 256 + tt * 2:258 + tt * 2], rn[:, tt * 128:(tt + 1) * 128],
                                                 con("hsel"), start=True, stop=True), sig=True)
                yield 1
                d = p.dve(lambda e: e.tensor_reduce(var, s4, AX, ALU.add), a, dep=False)
                p.pool(lambda e: e.tensor_scalar(var, var, 1.0 / 64, 64e-5, ALU.mult, ALU.add), d)
                h8 = con("half")[:, 0:1].to_broadcast([128, 4])
                pw = p.pool(lambda e: e.tensor_tensor(var, var, h8, ALU.pow))
                yield 1
                p.dve(lambda e: e.tensor_tensor(y4, y4, vb, ALU.mult), pw, dep=False)
                bs = b1[:, 256:260].unsqueeze(2).to_broadcast([128, 4, 64])
                v4 = u4(Vt)
                p.dve(lambda e: e.tensor_tensor(s4, v4, bs, ALU.mult), t2, dep=False)
                lw = s.LN[:, 0:1, :].to_broadcast([128, 2, 128])
                lb_ = s.LN[:, 1:2, :].to_broadcast([128, 2, 128])
                y2 = u2(Yt)
                p.dve(lambda e: e.tensor_tensor(y2, y2, lw, ALU.mult), tl)
                p.dve(lambda e: e.tensor_tensor(y2, y2, lb_, ALU.add))
                p.dve(lambda e: e.tensor_tensor(Yt, Yt, sq, ALU.add))
                d = p.dve(lambda e: e.tensor_tensor(Yt, Yt, b1[:, 0:256], ALU.mult))
                R.put(b1, [d])
                to_channels(y2, 1, None, yh, yl, [d], k0=g)
                s.free = [p.last("pe"), p.last("act"), p.last("dve"), p.last("pool")]
                groups_done.add(g)
                if g % 2 or (g + 1) in groups_done:
                    kzv_free[G % 2] = s.free
                yield 1

            slots = [Slot(), Slot()]

            def lane(n):
                for g in range(n, 8, 2):
                    yield from group(g, slots[n])

            live = [projections(), lane(0), lane(1)]
            while live:
                for g_ in list(live):
                    if next(g_, 0) == 0:
                        live.remove(g_)

        def mix2(l, xtok):
            xt = norm_channels(f"mix_norm_2{l}", xtok, None)
            after = [p.last("pe"), p.last("act"), p.last("dve")]
            sp = Space()
            PJ = sp.take(2, NIN2)
            EB = sp.take(6, 256)
            AK = sp.take(6, 256)
            BK = sp.take(5, 256)
            CK = sp.take(5, 256)
            IK = sp.take(4, 256)
            AQ, BQ, CQ, IQ = sp.take(3, 256), sp.take(3, 256), sp.take(5, 256), sp.take(2, 256)
            QF = sp.take(2, 480)
            KVF = sp.take(2, 640)
            KF = sp.take(2, 480)
            IKr = sp.take(2, 512)
            sc2 = sp.take(2, 384)
            rt = GATE[:, 0, 0:2048]
            OUT = rt.rearrange("p (t d) -> p t d", t=2)
            IXW = GATE[:, 1, 0:2048]
            MB = [sp.take(128), sp.take(256)]
            SC = sp.take(256)
            work = SC
            sflat, iflat = sc2.rearrange("p a b -> p (a b)"), IKr.rearrange("p a b -> p (a b)")
            Sb = [sflat[:, 256 * i:256 * i + 256] for i in range(3)]
            PTb = [iflat[:, 256 * i:256 * i + 256] for i in range(3)]
            CM = [sp.take(128), sp.take(256)]
            sem = p.new_sem()
            t_eb = p.dma(EB, bass.AP(ebias.tensor, ebias[l, 0, 0:1].offset, [[1, 128], [384, 6], [1, 256]]), sem, after, eng="pool")
            zz = [p.pool(lambda e, t_=t_: e.memset(t_, 0.0), after) for t_ in (AK, BK, IKr, CM[0], CM[1])]
            zz.append(p.pool(lambda e: e.memset(CM[0][0:64, 64:128], NEG)))
            zz.append(p.pool(lambda e: e.memset(CM[1][0:64, 192:256], NEG)))
            ev = []

            def proj():
                for j in (6, 0, 1, 2, 3, 4, 5):
                    keys = [(l, "in2", 12)] if j == 6 else [(l, "in2", 2 * j), (l, "in2", 2 * j + 1)]

                    def evac(tt, b, t, j=j):
                        o = PJ[:, tt, j * 512:j * 512 + b.shape[1]]
                        a = p.act(lambda e: e.activation(o, b, ACT.Copy), t, after, dep=False)
                        ev.append(a)
                        return a
                    yield from proj_b(keys, None, xt, evac)

            for _ in proj():
                pass
            tp = [p.last("act")]

            lat = []
            for j, (c0, w, nm, k0) in enumerate(((2408, 384, f"cq{l}", 0), (2792, 256, f"ckv{l}", 3))):
                s2 = sc2[:, :, 0:w]
                r = sumsq(PJ[:, :, c0:c0 + w], w, s2, tp)
                for tt in range(2):
                    o, i_, s_ = s2[:, tt, :], PJ[:, tt, c0:c0 + w], small[:, tt:tt + 1]
                    a = p.act(lambda e, o=o, i_=i_, s_=s_: e.activation(o, i_, ACT.Copy, scale=s_), r)
                to_channels(s2, w // 128, nm, yh, yl, [a], k0=k0)
                lat = [p.last("act"), p.last("dve"), p.last("pe")]
            t = None
            for nm, nk, k0, w, dst in (("uq", 3, 0, 480, QF), ("ukv", 2, 3, 640, KVF)):
                hi, lo, wt = take((l, nm, 0))
                for tt in range(2):
                    for c0 in range(0, w, 320):
                        cw = min(320, w - c0)
                        b, f = R.get()
                        for k in range(nk):
                            lh, ll = yh[:, k0 + k, tt * 128:(tt + 1) * 128], yl[:, k0 + k, tt * 128:(tt + 1) * 128]
                            t = mm3(b[:, 0:cw], lh, ll, hi[:, k * w + c0:k * w + c0 + cw],
                                    lo[:, k * w + c0:k * w + c0 + cw], k == 0, k == nk - 1, [wt, lat, f],
                                    sig=(k == nk - 1))
                        o = dst[:, tt, c0:c0 + cw]
                        a = p.act(lambda e, o=o, b=b, cw=cw: e.activation(o, b[:, 0:cw], ACT.Copy), t, after,
                                  dep=False)
                        R.put(b, [a])
                done(t)
            tl = [p.last("act")]
            for tt in range(2):
                P_ = PJ[:, tt, :]
                rope(P_[:, 1152:1792], P_[:, 1152:1792], tt, 10, 64, 0, 32, "r64", rt, tp)
                rope(P_[:, 2112:2400], P_[:, 2112:2400], tt, 9, 32, 0, 16, "r32", rt, tp)
                rope(P_[:, 3048:3080], P_[:, 3048:3080], tt, 1, 32, 0, 16, "r32", rt, tp)
                tr = rope(QF[:, tt, :], QF[:, tt, :], tt, 5, 96, 64, 16, "r32", rt, tl)
                kf = KF[:, tt, :].rearrange("p (h d) -> p h d", d=96)
                kn = KVF[:, tt, :].rearrange("p (h d) -> p h d", d=128)[:, :, 0:64]
                kr = P_[:, 3048:3080].unsqueeze(1).to_broadcast([128, 5, 32])
                p.pool(lambda e, kf=kf, kn=kn: e.tensor_copy(kf[:, :, 0:64], kn), tl, after)
                p.pool(lambda e, kf=kf, kr=kr: e.tensor_copy(kf[:, :, 64:96], kr), tr)
                for j in range(4):
                    o = IKr[:, tt, j * 128 + 32 * j:j * 128 + 32 * j + 32]
                    tk = p.pool(lambda e, o=o, i_=P_[:, 2368:2400]: e.tensor_copy(o, i_), tr)
            ready = [tr, tk, tp, tl]

            def turned(src, w, parts):
                b, f = R.get()
                for tt in range(2):
                    t = transpose(b[0:w, tt * 128:(tt + 1) * 128], src(tt), ready, f, t_c, sig=(tt == 1))
                c = None
                for dst, r0, n in parts:
                    c = p.act(lambda e, dst=dst, r0=r0, n=n: e.activation(dst[r0:r0 + n], b[r0:r0 + n, 0:256],
                                                                          ACT.Copy), t, zz, after, dep=False)
                R.put(b, [c])
                return c

            for j in range(2):
                turned(lambda tt, j=j: PJ[:, tt, 2112 + 128 * j:2240 + 128 * j], 128, [(IQ[:, j, :], 0, 128)])
            for j in range(4):
                ti = turned(lambda tt, j=j: IKr[:, tt, 128 * j:128 * j + 128], 128, [(IK[:, j, :], 0, 128)])

            def heads():
                for j in range(3):
                    turned(lambda tt, j=j: PJ[:, tt, 128 * j:128 * j + 128], 128, [(AQ[:, j, :], 0, 128)])
                    turned(lambda tt, j=j: PJ[:, tt, 384 + 128 * j:512 + 128 * j], 128,
                           [(AK[:, 2 * j, :], 0, 64), (AK[:, 2 * j + 1, :], 64, 64)])
                    yield 1
                for j in range(5):
                    turned(lambda tt, j=j: QF[:, tt, 96 * j:96 * j + 96], 96, [(CQ[:, j, :], 0, 96)])
                    turned(lambda tt, j=j: KF[:, tt, 96 * j:96 * j + 96], 96, [(CK[:, j, :], 0, 96)])
                    yield 1
                for j in range(3):
                    w = 128 if j < 2 else 64
                    turned(lambda tt, j=j, w=w: PJ[:, tt, 1152 + 128 * j:1152 + 128 * j + w], w,
                           [(BQ[:, j, :], 0, w)])
                    turned(lambda tt, j=j, w=w: PJ[:, tt, 1472 + 128 * j:1472 + 128 * j + w], w,
                           [(BK[:, 2 * j, :], 0, 64)] + ([(BK[:, 2 * j + 1, :], 64, 64)] if w == 128 else []))
                    yield 1

            mtok = {}

            def index(tt):
                W = 128 * (tt + 1)
                sl = slice(tt * 128, (tt + 1) * 128)
                iv = IXW[:, 0:8 * W].rearrange("p (h w) -> p h w", h=8)
                nb = 512 // W
                for h0 in range(0, 8, nb):
                    b, f = R.get()
                    for i in range(nb):
                        h = h0 + i
                        o = b[:, i * W:(i + 1) * W]
                        q, k_ = IQ[:, h // 4, sl], IK[:, h % 4, 0:W]
                        t = p.pe(lambda e, o=o, q=q, k_=k_: e.matmul(o, q, k_, start=True, stop=True), f, ti,
                                 sig=(i == nb - 1))
                    o = IXW[:, h0 * W:h0 * W + 512]
                    a = p.act(lambda e, o=o, b=b: e.activation(o, b, ACT.Relu, scale=32 ** -0.5), t, p.last("dve"),
                              dep=False)
                    R.put(b, [a])
                    yield 1
                iw = PJ[:, tt, 2400:2408]
                ws = small[:, 32:40]
                p.dve(lambda e: e.tensor_scalar(ws, iw, 8 ** -0.5, None, ALU.mult), tp)
                wb = ws.unsqueeze(2).to_broadcast([128, 8, W])
                p.dve(lambda e: e.tensor_tensor(iv, iv, wb, ALU.mult), a)
                p.dve(lambda e: e.tensor_tensor(iv[:, 0:4, :], iv[:, 0:4, :], iv[:, 4:8, :], ALU.add))
                p.dve(lambda e: e.tensor_tensor(iv[:, 0:2, :], iv[:, 0:2, :], iv[:, 2:4, :], ALU.add))
                s_, w_ = SC[:, 0:W], work[:, 0:W]
                p.dve(lambda e: e.tensor_tensor(s_, iv[:, 0, :], iv[:, 1, :], ALU.add))
                p.dve(lambda e: e.memset(SC[0:64, W - 64:W], NEG))
                yield 1
                m8 = small[:, 40:48]
                for r in range(8):
                    p.dve(lambda e: e.max(m8, s_))
                    p.dve(lambda e: e.match_replace(s_, m8, s_, -3e38))
                    if r % 2:
                        yield 1
                p.dve(lambda e: e.tensor_scalar(w_, s_, -2e38, NEG, ALU.is_ge, ALU.mult))
                mb = MB[tt]
                cm = CM[tt]
                mtok[tt] = p.dve(lambda e: e.tensor_tensor(mb, w_, cm, ALU.add), zz)
                yield 1

            Sr, Pr = Ring(Sb), Ring(PTb)
            stat = Ring([small[:, 8 + 2 * i:10 + 2 * i] for i in range(4)])

            def unit(kind, h, tt):
                S, sfree = Sr.get()
                sv_, stf = stat.get()
                nm, den = sv_[:, 0:1], sv_[:, 1:2]
                W = 128 * (tt + 1)
                sl = slice(tt * 128, (tt + 1) * 128)
                b, f = R.get()
                sw = S[:, 0:W]
                tk_ = p.last("act") if (kind, h) not in kt_ else kt_[(kind, h)]
                if kind == "a":
                    p.pe(lambda e: e.matmul(b[:, 0:W], AQ[:, h // 2, sl], AK[:, h, 0:W], start=True, stop=True),
                         f, tk_)
                    for kt2 in range(tt + 1):
                        lh = EB[:, h, 128 * (tt - kt2):128 * (tt - kt2) + 128]
                        t = p.pe(lambda e, kt2=kt2, lh=lh: e.matmul(
                            b[:, 256 + kt2 * 128:384 + kt2 * 128], lh, con("anti"), start=True, stop=True), t_eb,
                            sig=(kt2 == tt))
                    cm = CM[tt]
                    d0 = p.dve(lambda e: e.scalar_tensor_tensor(sw, b[:, 0:W], 0.125, cm, ALU.mult, ALU.add), t,
                               sfree, stf, zz, dep=False)
                    d = p.dve(lambda e: e.tensor_tensor(sw, sw, b[:, 256:256 + W], ALU.add), d0)
                    v = [PJ[:, s_, 768 + h * 64:768 + (h + 1) * 64] for s_ in range(tt + 1)]
                    oc = h * 64
                elif kind == "b":
                    t = p.pe(lambda e: e.matmul(b[:, 0:W], BQ[0:bk(h), h // 2, sl], BK[0:bk(h), h, 0:W], start=True,
                                                stop=True), f, tk_, sig=True)
                    mb = MB[tt]
                    d = p.dve(lambda e: e.scalar_tensor_tensor(sw, b[:, 0:W], 0.125, mb, ALU.mult, ALU.add), t,
                              sfree, stf, mtok[tt], dep=False)
                    v = [PJ[:, s_, 1792 + h * 64:1792 + (h + 1) * 64] for s_ in range(tt + 1)]
                    oc = 384 + h * 64
                else:
                    t = p.pe(lambda e: e.matmul(b[:, 0:W], CQ[0:96, h, sl], CK[0:96, h, 0:W], start=True, stop=True),
                             f, tk_, sig=True)
                    cm = CM[tt]
                    d = p.dve(lambda e: e.scalar_tensor_tensor(sw, b[:, 0:W], 96 ** -0.5, cm, ALU.mult, ALU.add), t,
                              sfree, stf, zz, dep=False)
                    v = [KVF[:, s_, h * 128 + 64:h * 128 + 128] for s_ in range(tt + 1)]
                    oc = 704 + h * 64
                R.put(b, [d])
                a, rd = soften(sw, W, [d], nm, den)
                yield 1
                PT, pf = Pr.get()
                yield from turn_and_weigh(S, tt + 1, v, PT, pf, a, den, OUT[:, tt, oc:oc + 64], [tp, tl], after)
                t, d = self_done.pop()
                Sr.put(S, [t])
                Pr.put(PT, [t])
                stat.put(sv_, [d])
                yield 1

            kt_ = {}

            def bk(h):
                return 64 if h == 4 else 128

            for _ in heads():
                pass
            units = [(k, h, tt) for k, n in (("a", 6), ("c", 5)) for h in range(n) for tt in range(2)]

            def idx_all():
                yield from index(0)
                yield from index(1)
            interleave(staggered((unit(*u) for u in units), 2), idx_all(), 1)
            for _ in staggered((unit("b", h, tt) for tt in range(2) for h in range(5)), 2):
                pass
            to_ = to_channels(OUT, 8, None, xh, xl, [p.last("dve"), p.last("pe")])
            got = [A.get() for _ in range(4)]
            banks, frees = [b for b, _ in got], [f for _, f in got]
            for t in down_like(lambda j: (l, "wout2", j), 4,
                               lambda k, tt: (xh[:, k, tt * 128:(tt + 1) * 128], xl[:, k, tt * 128:(tt + 1) * 128]),
                               lambda k: to_, banks, frees):
                pass
            return residual(banks, 1.0, t)

        def final(row, xtok, inplace=True):
            sp = Space()
            xn = sp.take(2, 1024)
            gr = sp.take(1024)
            g = p.dma(gr, rows[row:row + 1, 0:1024].to_broadcast([128, 1024]), p.new_sem(), xtok, eng="pool")
            r = sumsq(X, 1024, xn, [xtok])
            d = None
            for tt in range(2):
                o, s_ = X[:, tt, :], small[:, tt:tt + 1]
                d = p.dve(lambda e, o=o, s_=s_: e.scalar_tensor_tensor(o, o, s_, gr, ALU.mult, ALU.mult), r, g,
                          dep=False)
            return [d, xtok] if isinstance(xtok, tuple) else [d]

        xtok = [t_x]
        for s in stages:
            if s[0] == "ffn":
                xtok = [ffn(s[1], s[2], xtok)]
            elif s[0] == "mix1":
                xtok = [mix1(xtok)]
            elif s[0] == "mix2":
                xtok = [mix2(s[1], xtok)]
            else:
                xtok = final(s[1], xtok)
        s_out = p.new_sem()
        t = p.dma(out.rearrange("(t p) d -> p t d", p=128), X[:], s_out, xtok)
        p.wait("sp", [t])

        block = ctx.enter_context(nc.Block())

        @block.sync
        def _(e):
            for f in p.q["sp"]:
                f(e)

        @block.tensor
        def _(e):
            for f in p.q["pe"]:
                f(e)

        @block.scalar
        def _(e):
            for f in p.q["act"]:
                f(e)

        @block.vector
        def _(e):
            for f in p.q["dve"]:
                f(e)

        @block.gpsimd
        def _(e):
            for f in p.q["pool"]:
                f(e)


STAGES = [("ffn", "f1", "ffn1_norm"), ("mix1",), ("ffn", "f2", "ffn2_norm"), ("final", 3),
          ("ffn", "f3", "ffn1_norm_20"), ("mix2", 0), ("ffn", "f4", "ffn2_norm_20"),
          ("ffn", "f5", "ffn1_norm_21"), ("mix2", 1), ("ffn", "f6", "ffn2_norm_21"), ("final", 4)]


def kernel(**inputs):
    import concourse.bacc as bacc
    from concourse.bass_utils import run_bass_kernel_spmd

    I = {k: np.asarray(v) for k, v in inputs.items()}
    w_in = I["w_in"][0]
    ffns = {"f1": ("ffn1", "", 0), "f2": ("ffn2", "", 0), "f3": ("ffn1", "_2", 0), "f4": ("ffn2", "_2", 0),
            "f5": ("ffn1", "_2", 1), "f6": ("ffn2", "_2", 1)}
    AW, RS = 2304, 3360

    def rows_of(w):
        return w.reshape(w.shape[0] // 128, 128, w.shape[1]).transpose(1, 0, 2)

    def block(c):
        who, what, j, w = c
        if what in ("gu", "down"):
            n, sfx, l = ffns[who]
            if what == "gu":
                a = [rows_of(I[f"{n}_w_{g}{sfx}"][l][:, j * 128:(j + 1) * 128]) for g in ("gate", "up")]
                return np.stack(a, 1)
            return rows_of(I[f"{n}_w_down{sfx}"][l][j * 256:(j + 1) * 256])
        if who == "mix1":
            if what == "lora":
                c0 = AW + 3072 + 256 * j
                if j == 1:
                    return rows_of(np.pad(w_in[:, c0:c0 + 32], ((0, 0), (0, 96))))
                return rows_of(w_in[:, c0:c0 + 256])
            if what == "qkv":
                if j == 8:
                    return rows_of(w_in[:, 2048:2304])
                return rows_of(w_in[(j % 2) * 512:(j % 2) * 512 + 512, (j // 2) * 512:(j // 2) * 512 + 512])
            if what == "gate":
                c0 = AW + RS + (j // 2) * 512
                return rows_of(w_in[(j % 2) * 512:(j % 2) * 512 + 512, c0:c0 + 512])
            if what == "up":
                return rows_of(I["attn_w_up"][0])
            if what in "kvr":
                c0 = AW + {"r": 0, "k": 1024, "v": 2048}[what] + 256 * j
                return rows_of(w_in[:, c0:c0 + 256])
            return rows_of(I["rwkv_w_out" if what == "wout" else "w_o"][0][j * 256:(j + 1) * 256])
        if what == "in2":
            wi = I["w_in_2"][who]
            if j == 12:
                return rows_of(wi[:, 3072:3080])
            return rows_of(wi[(j % 2) * 512:(j % 2) * 512 + 512, (j // 2) * 512:(j // 2) * 512 + 512])
        if what == "uq":
            return rows_of(I["c_w_uq_2"][who])
        if what == "ukv":
            return rows_of(I["c_w_ukv_2"][who])
        return rows_of(I["w_out_2"][who][j * 256:(j + 1) * 256])

    chunks = plan(STAGES)
    wall = np.empty(sum(128 * c[3] for c in chunks), np.float32)
    at = 0
    for c in chunks:
        n = 128 * c[3]
        wall[at:at + n].reshape(128, -1)[:] = block(c).reshape(128, -1)
        at += n

    clay, NCOL = col_layout()
    cols = np.zeros((128, NCOL), np.float32)

    def put(name, v, at=0):
        a, w = clay[name]
        n = v.size // 128
        cols[:, a + at:a + at + n] = v.reshape(n, 128).T

    for n in ("ffn1_norm", "mix_norm", "ffn2_norm"):
        put(n, I[n][0])
        for l in range(2):
            put(f"{n}_2{l}", I[n + "_2"][l])
    mu = I["rwkv_mu"][0]
    put("mu", mu[3072:3328], 0)
    cols[0:32, clay["mu"][0] + 2] = mu[3328:3360]
    for i, o in enumerate((1024, 2048, 0)):
        put("mu", mu[o:o + 1024], 3 + 8 * i)
    for n, k in (("w0", "rwkv_w0"), ("a0", "rwkv_a0"), ("kk", "rwkv_k_k"), ("ka", "rwkv_k_a"), ("rk", "rwkv_r_k")):
        put(n, I[k][0].reshape(-1))
    for l in range(2):
        put(f"cq{l}", I["c_q_norm_2"][l])
        put(f"ckv{l}", I["c_kv_norm_2"][l])
    rows = np.zeros((5, 2048), np.float32)
    rows[0] = I["gate_bias"][0]
    rows[1, :1024], rows[2, :1024] = I["rwkv_ln_w"][0], I["rwkv_ln_b"][0]
    rows[3, :1024], rows[4, :1024] = I["final_norm"], I["final_norm_2"]
    lorap = np.zeros((3, 128, 1024), np.float32)
    lorap[0, :64], lorap[0, 64:] = I["rwkv_w2"][0], I["rwkv_a2"][0]
    lorap[1], lorap[2, :32] = I["rwkv_g2"][0][:128], I["rwkv_g2"][0][128:]
    ebias = I["a_rel_bias_2"][:, :, np.clip(np.arange(384) - 127, -63, 128) + 63]

    arrays = {"x": np.ascontiguousarray(I["x"][0]), "wall": wall, "consts": const_table()[1], "cols": cols,
              "rows": rows, "lorap": lorap, "ebias": np.ascontiguousarray(ebias)}
    nc = bacc.Bacc("TRN2", target_bir_lowering=False, num_devices=1)
    aps = [nc.dram_tensor(n, a.shape, mybir.dt.from_np(a.dtype), kind="ExternalInput").ap() for n, a in arrays.items()]
    o = nc.dram_tensor("out", (256, 1024), F32, kind="ExternalOutput").ap()
    build(nc, STAGES, *aps, o)
    r = run_bass_kernel_spmd(nc, [arrays], core_ids=[0])
    return r.results[0]["out"].reshape(1, 256, 1024)
```

```python
from contextlib import ExitStack
import math

import numpy as np

import concourse.bass as bass
from concourse import mybir

F32 = mybir.dt.float32
F32R = mybir.dt.float32r
ALU = mybir.AluOpType
ACT = mybir.ActivationFunctionType
AX = mybir.AxisListType.X

D = 1024
FF = 2816
NM = FF // 128
NIN2 = 3080
NEG = -1e30
DECAY = -math.exp(-0.5)
CW = 2048


def plan(stages):
    out = []

    def ffn(w):
        for m in range(NM + 1):
            if m < NM:
                out.append((w, "gu", m, 2048))
            if m >= 2 and m % 2 == 0:
                out.append((w, "down", m // 2 - 1, 2048))

    for s in stages:
        if s[0] == "ffn":
            ffn(s[1])
        elif s[0] == "mix1":
            out.append(("mix1", "lora", 0, 2048))
            out.append(("mix1", "lora", 1, 1024))
            for j in range(4):
                out += [("mix1", "qkv", 2 * j, 2048), ("mix1", "qkv", 2 * j + 1, 2048)]
            out.append(("mix1", "qkv", 8, 2048))
            for j in range(8):
                out.append(("mix1", "gate", j, 2048))
            out.append(("mix1", "up", 0, 2048))
            for g in range(4):
                for q in "kvr":
                    out.append(("mix1", q, g, 2048))
            for j in range(4):
                out.append(("mix1", "wout", j, 2048))
            for j in range(4):
                out.append(("mix1", "wo", j, 2048))
        elif s[0] == "mix2":
            l = s[1]
            out.append((l, "in2", 12, 64))
            for j in (8, 9, 10, 11, 6, 7):
                out.append((l, "in2", j, 2048))
            out.append((l, "uq", 0, 1440))
            out.append((l, "ukv", 0, 1280))
            for j in (4, 5, 2, 3, 0, 1):
                out.append((l, "in2", j, 2048))
            for j in (2, 3, 1, 0):
                out.append((l, "wout2", j, 2048))
    return out


def const_table():
    p = np.arange(128)
    cols = {}
    parts = []
    at = 0

    def put(name, a):
        nonlocal at
        a = np.asarray(a, np.float32).reshape(128, -1)
        cols[name] = (at, a.shape[1])
        parts.append(a)
        at += a.shape[1]

    put("ident", np.eye(128))
    put("anti", np.eye(128)[:, ::-1])
    put("hsel", (p[:, None] // 64 == np.arange(2)[None, :]))
    s = p[:, None] % 64
    t = np.arange(64)[None, :]
    put("mar", np.stack([s < t, s <= t], 1))
    put("mlow", t < s)
    put("i64", t == s)

    def lower(k):
        return (s >> (k + 1) == t >> (k + 1)) & ((s >> k) % 2 == 1) & ((t >> k) % 2 == 0)

    def upper(k):
        return (s >> (k + 1) == t >> (k + 1)) & ((s >> k) % 2 == 0) & ((t >> k) % 2 == 1)

    put("m0", lower(0))
    put("m0t", upper(0))
    for k in range(1, 6):
        put(f"m{k}", lower(k))
    put("half", np.full((128, 2), -0.5))
    f = np.float32

    def tables(theta, d):
        half = d // 2
        inv = np.power(f(theta), -(np.arange(half, dtype=f) * f(2.0 / d))).astype(f)
        ang = (np.arange(256, dtype=f)[:, None] * inv[None, :]).astype(f)
        sh = lambda a: a.reshape(2, 128, half).transpose(1, 0, 2)
        return sh(np.cos(ang)), sh(np.sin(ang))

    for name, th, d in (("r16", 500000.0, 16), ("r64", 10000.0, 64), ("r32", 10000.0, 32)):
        c, sn = tables(th, d)
        put(name + "c", c)
        put(name + "s", sn)
    base = at
    for tt in range(2):
        tq = (128 * tt + p)[:, None]
        sk = np.arange(128 * (tt + 1))[None, :]
        ok = [(sk <= tq) & (tq - sk <= 128), (sk <= tq) & ((tq - sk) % 4 == 0), (sk <= tq) & ((tq - sk) % 16 == 0)]
        put(f"dil{tt}", np.where(np.stack(ok, 1), 0.0, NEG))
    return cols, np.concatenate(parts, 1), base


def col_layout():
    names = [("ffn1_norm", 8), ("mix_norm", 8), ("ffn2_norm", 8), ("mu", 27), ("w0", 8), ("a0", 8), ("kk", 8),
             ("ka", 8), ("rk", 8)]
    for l in range(2):
        names += [(f"ffn1_norm_2{l}", 8), (f"mix_norm_2{l}", 8), (f"ffn2_norm_2{l}", 8), (f"cq{l}", 3), (f"ckv{l}", 2)]
    at, out = 0, {}
    for n, w in names:
        out[n] = (at, w)
        at += w
    return out, at


class Call:

    def matmul(self, *a, **k):
        return lambda e: e.matmul(*a, **k)

    def transpose(self, *a, **k):
        return lambda e: e.transpose(*a, **k)

    def activation(self, *a, **k):
        return lambda e: e.activation(*a, **k)

    def tensor_tensor(self, *a, **k):
        return lambda e: e.tensor_tensor(*a, **k)

    def tensor_scalar(self, *a, **k):
        return lambda e: e.tensor_scalar(*a, **k)

    def scalar_tensor_tensor(self, *a, **k):
        return lambda e: e.scalar_tensor_tensor(*a, **k)

    def tensor_reduce(self, *a, **k):
        return lambda e: e.tensor_reduce(*a, **k)

    def tensor_copy(self, *a, **k):
        return lambda e: e.tensor_copy(*a, **k)

    def memset(self, *a, **k):
        return lambda e: e.memset(*a, **k)

    def reciprocal(self, *a, **k):
        return lambda e: e.reciprocal(*a, **k)

    def tensor_tensor_scan(self, *a, **k):
        return lambda e: e.tensor_tensor_scan(*a, **k)

    def max(self, *a, **k):
        return lambda e: e.max(*a, **k)

    def match_replace(self, *a, **k):
        return lambda e: e.match_replace(*a, **k)


CALL = Call()


class Prog:

    def __init__(self, nc, ctx):
        self.nc, self.ctx = nc, ctx
        self.q = {e: [] for e in ("pe", "act", "dve", "pool", "sp")}
        self.sem = {e: ctx.enter_context(nc.semaphore(f"s_{e}")) for e in ("pe", "act", "dve", "pool")}
        self.n = {e: 0 for e in self.sem}
        self.seen = {}
        self.nsem = 0

    def wait(self, eng, toks):
        for t in toks:
            if t is None:
                continue
            if not (len(t) == 2 and isinstance(t[1], int)):
                self.wait(eng, t)
                continue
            s, v = t
            key = (eng, id(s))
            if self.seen.get(key, 0) < v:
                self.seen[key] = v
                self.q[eng].append(lambda e, s=s, v=v: e.wait_ge(s, v))

    def last(self, eng):
        return (self.sem[eng], self.n[eng]) if self.n[eng] else None

    def op(self, eng, fn, *toks, dep=True, sig=True):
        fn = fn(CALL)
        self.wait(eng, toks)
        if dep and eng != "pe":
            self.wait(eng, [self.last(eng)])
        if not sig:
            self.q[eng].append(fn)
            return None
        s = self.sem[eng]
        self.q[eng].append(lambda e: fn(e).then_inc(s, 1))
        self.n[eng] += 1
        return (s, self.n[eng])

    def pe(self, fn, *t, sig=False):
        return self.op("pe", fn, *t, sig=sig)

    def act(self, fn, *t, dep=True):
        return self.op("act", fn, *t, dep=dep)

    def dve(self, fn, *t, dep=True):
        return self.op("dve", fn, *t, dep=dep)

    def pool(self, fn, *t, dep=True):
        return self.op("pool", fn, *t, dep=dep)

    def new_sem(self):
        self.nsem += 1
        return [self.ctx.enter_context(self.nc.semaphore(f"d{self.nsem}")), 0]

    def dma(self, dst, src, sem, *toks, eng="sp"):
        self.wait(eng, toks)
        sem[1] += 16
        s = sem[0]
        self.q[eng].append(lambda e: e.dma_start(dst, src).then_inc(s, 16))
        return (s, sem[1])


class Ring:

    def __init__(self, aps):
        self.free = [(a, []) for a in aps]

    def get(self):
        assert self.free, "no slot free"
        return self.free.pop(0)

    def put(self, ap, toks):
        self.free.append((ap, list(toks)))


def interleave(main, side, ratio=1):
    side_on = True
    for _ in main:
        for _ in range(ratio):
            if side_on and next(side, 0) == 0:
                side_on = False
    for _ in side:
        pass


def staggered(gens, depth):
    gens = iter(gens)
    live = []
    while True:
        if len(live) < depth:
            g = next(gens, None)
            if g is not None:
                live.append(g)
        if not live:
            return
        for g in list(live):
            if next(g, 0) == 0:
                live.remove(g)
        yield 1


def together(*gens):
    live = list(gens)
    while live:
        for g in list(live):
            if next(g, 0) == 0:
                live.remove(g)


def build(nc, stages, x_in, wall, consts, cols, rows, lorap, ebias, out):
    ctab, carr, cbase = const_table()
    NCON = carr.shape[1]
    clay, NCOL = col_layout()
    with ExitStack() as ctx:
        p = Prog(nc, ctx)

        def sb(name, shape, dt=F32):
            return ctx.enter_context(nc.sbuf_tensor(name, shape, dt))

        X = sb("X", [128, 2, 1024])
        raw = [sb(f"raw{i}", [128, CW]) for i in range(3)]
        whi = [sb(f"whi{i}", [128, CW], F32R) for i in range(2)]
        wlo = [sb(f"wlo{i}", [128, CW], F32R) for i in range(2)]
        xh, xl = sb("xh", [128, 8, 256], F32R), sb("xl", [128, 8, 256], F32R)
        yh, yl = sb("yh", [128, 8, 256], F32R), sb("yl", [128, 8, 256], F32R)
        C = sb("C", [128, cbase])
        COL = sb("COL", [128, NCOL])
        small = sb("small", [128, 256])
        GATE = sb("GATE", [128, 2, 2048])
        NA = 22300
        arena = sb("arena", [128, NA])
        PS = ctx.enter_context(nc.psum_tensor("PS", [128, 8, 512], F32))
        bank = [PS[:, i, :] for i in range(8)]
        R = A = Ring(bank)

        def con(name):
            a, w = ctab[name]
            return C[:, a:a + w]

        def col(name, j):
            a, _ = clay[name]
            return COL[:, a + j:a + j + 1]

        class Space:
            def __init__(self, at=0):
                self.at = at

            def take(self, *shape):
                n = int(np.prod(shape))
                a = arena[:, self.at:self.at + n]
                self.at += n
                assert self.at <= NA, self.at
                if len(shape) == 1:
                    return a
                names = "abcde"[:len(shape)]
                return a.rearrange(f"p ({' '.join(names)}) -> p {' '.join(names)}",
                                   **{n_: s_ for n_, s_ in zip(names, shape)})

        ident = con("ident")
        sem_c, sem_x, sem_col = p.new_sem(), p.new_sem(), p.new_sem()
        t_x = p.dma(X[:], x_in.rearrange("(t p) d -> p t d", p=128), sem_x)
        t_c = p.dma(C[:], consts[:, 0:cbase], sem_c)
        t_col = p.dma(COL[:], cols, sem_col)

        chunks = plan(stages)
        offs = np.cumsum([0] + [128 * c[3] for c in chunks])
        raw_sem = [p.new_sem() for _ in range(3)]
        RAWN, SPL = 3, 2
        st = {"dma": 0, "split": 0, "use": 0}
        land, split_tok, use_tok, info = {}, {}, {}, {}

        def feed_dma():
            i = st["dma"]
            if i >= len(chunks):
                return
            w = chunks[i][3]
            src = wall[int(offs[i]):int(offs[i + 1])].rearrange("(p w) -> p w", p=128)
            land[i] = p.dma(raw[i % RAWN][:, 0:w], src, raw_sem[i % RAWN],
                            split_tok[i - RAWN] if i >= RAWN else [])
            st["dma"] += 1

        def pieces(n):
            i = st["split"]
            if i >= len(chunks):
                return
            w = chunks[i][3]
            free = use_tok[i - SPL] if i >= SPL else None
            toks = []
            cuts = [w * q // n for q in range(n + 1)]
            for q in range(n + 1):
                if q:
                    c = slice(cuts[q - 1], cuts[q])
                    r, hi, lo = raw[i % RAWN][:, c], whi[i % SPL][:, c].bitcast(F32), wlo[i % SPL][:, c]
                    toks.append(p.dve(lambda e: e.tensor_tensor(lo, r, hi, ALU.subtract), land[i], toks[-1], free,
                                      dep=False))
                if q < n:
                    c = slice(cuts[q], cuts[q + 1])
                    r, hi = raw[i % RAWN][:, c], whi[i % SPL][:, c]
                    toks.append(p.act(lambda e: e.activation(hi, r, ACT.Copy), land[i], free, dep=False))
                    yield 1
            split_tok[i] = toks
            st["split"] += 1
            feed_dma()
            yield 1

        under_way = []

        def feed_split():
            for g_ in under_way or [pieces(2)]:
                for _ in g_:
                    pass
            under_way.clear()

        def pump():
            if not under_way and st["split"] == st["use"] + 1:
                under_way.append(pieces(4))
            if under_way and next(under_way[0], 0) == 0:
                under_way.clear()

        for _ in range(RAWN):
            feed_dma()
        feed_split()

        def take(key):
            i = st["use"]
            assert chunks[i][:3] == key, (chunks[i], key)
            w = chunks[i][3]
            while st["split"] <= i:
                feed_split()
            return whi[i % SPL][:, 0:w], wlo[i % SPL][:, 0:w], split_tok[i]

        def done(tok):
            use_tok[st["use"]] = tok
            st["use"] += 1
            if st["split"] <= st["use"]:
                feed_split()

        def mm3(o, wa, wb, xa, xb, first, last, toks, sig=False):
            p.pe(lambda e: e.matmul(o, wa, xa, start=first, stop=False), *toks)
            p.pe(lambda e: e.matmul(o, wa, xb, start=False, stop=False))
            return p.pe(lambda e: e.matmul(o, wb, xa, start=False, stop=last), sig=sig)

        def transpose(o, i, *toks, sig=False, id_=None):
            k = i.shape[0]
            idn = ident if id_ is None else id_
            return p.pe(lambda e: e.transpose(o, i, idn[0:k, 0:k]), *toks, sig=sig)

        def rstd(src, n, width, eps, toks):
            a = p.pool(lambda e: e.tensor_scalar(src, src, 1.0 / width, eps, ALU.mult, ALU.add), toks)
            h = con("half")[:, 0:1]
            hb = h.to_broadcast([128, n])
            return p.pool(lambda e: e.tensor_tensor(src, src, hb, ALU.pow), a, t_c)

        def sumsq(src2, width, scratch, toks):
            ts = []
            for tt in range(2):
                s_, o_, acc = src2[:, tt, :], scratch[:, tt, :], small[:, tt:tt + 1]
                a = p.act(lambda e: e.activation(o_, s_, ACT.Square, accum_out=acc), toks[tt], dep=(tt == 0))
                ts.append(rstd(acc, 1, width, 1e-6, a))
            return ts

        def to_channels(src2, n, gain, hi, lo, toks, k0=0):
            out = []
            for k in range(0, n, 2):
                b, free = R.get()
                ks = list(range(k, min(n, k + 2)))
                for kk in ks:
                    for tt in range(2):
                        o = b[:, (kk - k) * 256 + tt * 128:(kk - k) * 256 + tt * 128 + 128]
                        i = src2[:, tt, kk * 128:(kk + 1) * 128]
                        t = transpose(o, i, toks, free, t_c, sig=(kk == ks[-1] and tt == 1))
                a, ls = None, []
                for kk in ks:
                    o, i = hi[:, k0 + kk, :], b[:, (kk - k) * 256:(kk - k) * 256 + 256]
                    if gain:
                        g = col(gain, kk)
                        a = p.act(lambda e, o=o, i=i, g=g: e.activation(o, i, ACT.Copy, scale=g), t, t_col,
                                  dep=False)
                    else:
                        a = p.act(lambda e, o=o, i=i: e.activation(o, i, ACT.Copy), t, dep=False)
                for kk in ks:
                    o, h, i = lo[:, k0 + kk, :], hi[:, k0 + kk, :].bitcast(F32), b[:, (kk - k) * 256:(kk - k) * 256 + 256]
                    if gain:
                        g = col(gain, kk)
                        d = p.dve(lambda e, o=o, i=i, g=g, h=h: e.scalar_tensor_tensor(o, i, g, h, ALU.mult, ALU.subtract),
                                  a, t_col, dep=False)
                    else:
                        d = p.dve(lambda e, o=o, i=i, h=h: e.tensor_tensor(o, i, h, ALU.subtract), a, dep=False)
                R.put(b, [d])
                out += [a, d]
            return out

        def norm_channels(gain, xtok, free):
            xn = Space().take(2, 1024)
            r = sumsq(X, 1024, xn, xtok)
            ts = []
            for tt in range(2):
                for half in range(2):
                    c = slice(half * 512, half * 512 + 512)
                    o, i, s_ = xn[:, tt, c], X[:, tt, c], small[:, tt:tt + 1]
                    if half:
                        ts.append(p.act(lambda e: e.activation(o, i, ACT.Copy, scale=s_), r[tt], dep=False))
                    else:
                        ts.append(p.dve(lambda e: e.tensor_scalar(o, i, s_, None, ALU.mult), r[tt], dep=False))
            out = to_channels(xn, 8, gain, xh, xl, ts)
            return [out[k - k % 2:k - k % 2 + 2] for k in range(8)]

        def down_like(key_fn, n, lhs, toks_fn, banks, frees, kper=2, order=None, fine=False):
            order = order or list(range(n))
            for j in order:
                hi, lo, w = take(key_fn(j))
                h3 = hi.rearrange("p (k n) -> p k n", k=kper)
                l3 = lo.rearrange("p (k n) -> p k n", k=kper)
                end = []
                steps = [(kk, tt) for kk in range(kper) for tt in range(2)]
                if j == order[-1]:
                    steps.sort(key=lambda s_: s_[1])
                for kk, tt in steps:
                    k = j * kper + kk
                    a, b = lhs(k, tt)
                    for nn in range(2):
                        o = banks[2 * tt + nn]
                        first, last = (j, kk) == (order[0], 0), (j, kk) == (order[-1], kper - 1)
                        wh_, wl_ = h3[:, kk, nn * 512:nn * 512 + 512], l3[:, kk, nn * 512:nn * 512 + 512]
                        t = mm3(o, a, b, wh_, wl_, first, last, [w, toks_fn(k), frees if first else None],
                                sig=(kk == kper - 1 and nn == 1))
                    if kk == kper - 1:
                        end.append(t)
                    if fine:
                        pump()
                    if fine and (kk, tt) != (kper - 1, 1):
                        yield None
                done(t)
                yield end

        def residual(banks, scale, tok):
            ds = []
            for tt in range(2):
                for nn in range(2):
                    o = X[:, tt, nn * 512:nn * 512 + 512]
                    b = banks[2 * tt + nn]
                    d = p.dve(lambda e: e.scalar_tensor_tensor(o, b, scale, o, ALU.mult, ALU.add), tok[tt],
                              dep=False)
                    A.put(b, [d])
                ds.append(d)
            return ds

        def ffn(which, gain, xtok):
            xt = norm_channels(gain, xtok, None)
            sg = [small_buf(i) for i in range(2)]
            hring = Ring([(yh[:, i, :], yl[:, i, :]) for i in range(5)])
            sgr = Ring(sg)
            got = [A.get() for _ in range(4)]
            banks, frees = [b for b, _ in got], [f for _, f in got]
            hs = {}

            def gu(m):
                hi, lo, w = take((which, "gu", m))
                b, free = R.get()
                for g in range(2):
                    for k in range(8):
                        c0 = (g * 8 + k) * 128
                        t = mm3(b[:, g * 256:(g + 1) * 256], hi[:, c0:c0 + 128], lo[:, c0:c0 + 128], xh[:, k, :],
                                xl[:, k, :], k == 0, k == 7, [w, xt[k], free], sig=(k == 7))
                done(t)
                s_, sf = sgr.get()
                a = p.act(lambda e: e.activation(s_, b[:, 0:256], ACT.Silu), t, sf, dep=False)
                d = p.dve(lambda e: e.tensor_tensor(s_, s_, b[:, 256:512], ALU.mult), a, dep=False)
                R.put(b, [d])
                (hh, hl), hf = hring.get()
                a = p.act(lambda e: e.activation(hh, s_, ACT.Copy), d, hf, dep=False)
                d = p.dve(lambda e: e.tensor_tensor(hl, s_, hh.bitcast(F32), ALU.subtract), a, hf, dep=False)
                sgr.put(s_, [a, d])
                hs[m] = (hh, hl, [a, d])

            def lhs(k, tt):
                hh, hl, _ = hs[k]
                return hh[:, tt * 128:(tt + 1) * 128], hl[:, tt * 128:(tt + 1) * 128]

            dn = down_like(lambda j: (which, "down", j), NM // 2, lhs, lambda k: hs[k][2], banks, frees)
            for m in range(NM + 1):
                if m < NM:
                    gu(m)
                if m >= 2 and m % 2 == 0:
                    t = next(dn)
                    for k in (m - 2, m - 1):
                        hring.put(hs[k][:2], [t])
            return residual(banks, 0.5, t)

        smb = [arena[:, 20000 + 256 * i:20256 + 256 * i] for i in range(2)]

        def small_buf(i):
            return smb[i]

        def soften(S, n, toks, nm, den):
            d = p.dve(lambda e: e.tensor_reduce(nm, S, AX, ALU.max, negate=True), toks)
            return p.act(lambda e: e.activation(S, S, ACT.Exp, bias=nm, accum_out=den), d)

        def turn_and_weigh(S, blocks, values, PT, ptfree, a, rden, o, extra, ofree):
            ts = []
            for b0 in range(0, blocks, 4):
                b, free = R.get()
                nb = min(4, blocks - b0)
                for i in range(nb):
                    t = transpose(b[:, i * 128:(i + 1) * 128], S[:, (b0 + i) * 128:(b0 + i + 1) * 128], a, free,
                                  t_c, sig=(i == nb - 1))
                dst = PT[:, b0 * 128:(b0 + nb) * 128]
                c = p.act(lambda e, dst=dst, b=b, nb=nb: e.activation(dst, b[:, 0:nb * 128], ACT.Copy), t, ptfree,
                          dep=False)
                R.put(b, [c])
                ts.append(c)
            yield 1
            p.dve(lambda e: e.reciprocal(rden, rden), a, dep=False)
            b, free = R.get()
            dv = o.shape[1]
            for i in range(blocks):
                t = p.pe(lambda e, i=i: e.matmul(b[:, 0:dv], PT[:, i * 128:(i + 1) * 128], values[i],
                                                 start=(i == 0), stop=(i == blocks - 1)), ts, free, extra,
                         sig=(i == blocks - 1))
            d = p.dve(lambda e: e.tensor_scalar(o, b[:, 0:dv], rden, None, ALU.mult), t, ofree)
            R.put(b, [d])
            self_done.append((t, d))

        self_done = []

        def rope(src, dst, tt, nh, hd, off, half, name, tmp, toks):
            c = con(name + "c")[:, tt * half:(tt + 1) * half].unsqueeze(1).to_broadcast([128, nh, half])
            s_ = con(name + "s")[:, tt * half:(tt + 1) * half].unsqueeze(1).to_broadcast([128, nh, half])
            sv = src.rearrange("p (h d) -> p h d", d=hd)
            dv_ = dst.rearrange("p (h d) -> p h d", d=hd)
            x1, x2 = sv[:, :, off:off + half], sv[:, :, off + half:off + 2 * half]
            o1, o2 = dv_[:, :, off:off + half], dv_[:, :, off + half:off + 2 * half]
            n = nh * half
            tv = [tmp[:, i * n:(i + 1) * n].rearrange("p (h d) -> p h d", d=half) for i in range(4)]
            p.dve(lambda e: e.tensor_tensor(tv[0], x1, c, ALU.mult), toks, t_c)
            p.dve(lambda e: e.tensor_tensor(tv[1], x2, s_, ALU.mult), dep=False)
            p.dve(lambda e: e.tensor_tensor(tv[2], x2, c, ALU.mult), dep=False)
            p.dve(lambda e: e.tensor_tensor(tv[3], x1, s_, ALU.mult), dep=False)
            p.dve(lambda e: e.tensor_tensor(o1, tv[0], tv[1], ALU.subtract))
            return p.dve(lambda e: e.tensor_tensor(o2, tv[2], tv[3], ALU.add), dep=False)

        def proj_b(keys, xt, evac, fine=False):
            got = [A.get() for _ in range(2)]
            nk = 8 // len(keys)
            w = 0
            for j, key in enumerate(keys):
                hi, lo, wt = take(key)
                w = hi.shape[1] // nk
                for kk in range(nk):
                    k = j * nk + kk
                    for tt in range(2):
                        b, free = got[tt]
                        t = mm3(b[:, 0:w], xh[:, k, tt * 128:(tt + 1) * 128], xl[:, k, tt * 128:(tt + 1) * 128],
                                hi[:, kk * w:(kk + 1) * w], lo[:, kk * w:(kk + 1) * w], k == 0, k == 7,
                                [wt, xt[k], free if k == 0 else None], sig=(kk == nk - 1 and tt == 1))
                        if fine and tt == 0:
                            yield 1
                    if len(keys) > 1:
                        pump()
                    if kk < nk - 1:
                        yield 1
                done(t)
                if j < len(keys) - 1:
                    yield 1
            for tt in range(2):
                b, _ = got[tt]
                A.put(b, [evac(tt, b[:, 0:w], t)])
            yield 1

        def mix1(xtok):
            xt = norm_channels("mix_norm", xtok, None)
            after_norm = [p.last("pe"), p.last("act"), p.last("dve")]
            sp = Space()
            zl = sp.take(3, 256)
            rbase = sp.at
            QKV = sp.take(2, 2304)
            DM = [sp.take(384), sp.take(768)]
            GB = sp.take(2048)
            qT = sp.take(6, 256)
            kz = sp.take(12, 256)
            Sb = [sp.take(768) for _ in range(3)]
            PTb = [sp.take(768) for _ in range(3)]
            AO = sp.take(2, 256)
            rt = sp.take(4 * 24 * 8)
            z = sp.take(2, 257)
            sem = p.new_sem()
            for tt in range(2):
                a_, w_ = ctab[f"dil{tt}"]
                t_dm = p.dma(DM[tt], consts[:, a_:a_ + w_], sem, after_norm, eng="pool")
            sem = p.new_sem()
            t_gb = p.dma(GB, rows[0:1, 0:2048].to_broadcast([128, 2048]), sem, after_norm, eng="pool")
            zk = p.pool(lambda e: e.memset(kz, 0.0), after_norm)
            z0 = p.pool(lambda e: e.memset(z[:, :, 0:1], 0.0))

            def shift(key, n, w, dst, mus, zz, zfree, dfree=None):
                while not A.free:
                    yield 1
                b, free = A.get()
                hi, lo, wt = take(key)
                for j in range(n):
                    for k in range(8):
                        c0 = k * n * w + j * w
                        t = mm3(b[0:w, j * 256:(j + 1) * 256], hi[:, c0:c0 + w], lo[:, c0:c0 + w], xh[:, k, :],
                                xl[:, k, :], k == 0, k == 7, [wt, xt[k], free], sig=(k == 7))
                        if k % 4 == 3:
                            pump()
                        if k % 4 == 3 and (j, k) != (n - 1, 7):
                            yield 1
                done(t)
                bb = b.rearrange("p (n t) -> p n t", n=2)[0:w, 0:n, :]
                c = p.act(lambda e: e.activation(zz[0:w, 0:n, 1:257], bb, ACT.Copy), t, zfree, z0, dep=False)
                A.put(b, [c])
                yield 1
                p.dve(lambda e: e.tensor_tensor(dst[0:w, 0:n, :], zz[0:w, 0:n, 0:256], zz[0:w, 0:n, 1:257],
                                                ALU.subtract), c, dfree, dep=False)
                for j in range(n):
                    m_ = col("mu", mus[j])[0:w]
                    d = p.dve(lambda e: e.scalar_tensor_tensor(
                        dst[0:w, j, :], dst[0:w, j, :], m_, zz[0:w, j, 1:257], ALU.mult, ALU.add), t_col,
                        dep=(j == 0))
                yield 1
                return d

            def run(gen):
                while True:
                    try:
                        next(gen)
                    except StopIteration as s_:
                        return s_.value

            d = run(shift(("mix1", "lora", 0), 2, 128, zl, [0, 1], z, None))
            d = run(shift(("mix1", "lora", 1), 1, 128, zl[:, 2:3, :], [2], z, d))
            p.act(lambda e: e.activation(zl[0:64, 0, :], zl[0:64, 0, :], ACT.Tanh), d)
            p.act(lambda e: e.activation(zl[:, 1, :], zl[:, 1, :], ACT.Tanh, scale=0.5), d, dep=False)
            a = p.act(lambda e: e.activation(zl[:, 2, :], zl[:, 2, :], ACT.Tanh, scale=0.5), d, dep=False)
            p.dve(lambda e: e.tensor_scalar(zl[:, 1, :], zl[:, 1, :], 0.5, 0.5, ALU.mult, ALU.add), a)
            t_zl = p.dve(lambda e: e.tensor_scalar(zl[:, 2, :], zl[:, 2, :], 0.5, 0.5, ALU.mult, ALU.add),
                         dep=False)

            def qkv_chunks():
                for j in range(5):
                    keys = [("mix1", "qkv", 2 * j), ("mix1", "qkv", 2 * j + 1)] if j < 4 else [("mix1", "qkv", 8)]

                    def evac(tt, b, t, j=j):
                        o = QKV[:, tt, j * 512:j * 512 + b.shape[1]]
                        return p.act(lambda e: e.activation(o, b, ACT.Copy), t, after_norm, dep=False)
                    yield from proj_b(keys, xt, evac)

            for _ in qkv_chunks():
                pass
            tq = p.last("act")
            r_ = []
            for tt in range(2):
                r_.append(rope(QKV[:, tt, 0:1536], QKV[:, tt, 0:1536], tt, 24, 64, 0, 8, "r16", rt, [tq]))

            def gates():
                for j in range(4):
                    def evac(tt, b, t, j=j):
                        o = GATE[:, tt, j * 512:(j + 1) * 512]
                        gb = GB[:, j * 512:(j + 1) * 512]
                        d = p.dve(lambda e: e.tensor_tensor(o, b, gb, ALU.add), t, t_gb, dep=False)
                        a = p.act(lambda e: e.activation(o, o, ACT.Tanh, scale=0.5), d, dep=False)
                        p.pool(lambda e: e.tensor_scalar(o, o, 0.5, 0.5, ALU.mult, ALU.add), a, dep=False)
                        return d
                    yield from proj_b([("mix1", "gate", 2 * j), ("mix1", "gate", 2 * j + 1)], xt, evac)

            def attention():
                kv = []
                for j in range(12):
                    b, free = R.get()
                    for tt in range(2):
                        t = transpose(b[:, tt * 128:(tt + 1) * 128], QKV[:, tt, j * 128:(j + 1) * 128], r_, free, t_c,
                                      sig=(tt == 1))
                    if j < 6:
                        c = p.act(lambda e, j=j, b=b: e.activation(qT[:, j, :], b[:, 0:256], ACT.Copy), t, dep=False)
                    else:
                        for q in range(2):
                            o = kz[64 * q:64 * q + 64, 2 * (j - 6) + q, :]
                            i_ = b[64 * q:64 * q + 64, 0:256]
                            c = p.act(lambda e, o=o, i_=i_: e.activation(o, i_, ACT.Copy), t, zk, dep=False)
                    R.put(b, [c])
                    kv.append(c)
                    if j % 3 == 2:
                        yield 1
                Sr, Pr = Ring(Sb), Ring(PTb)
                stat = Ring([small[:, 8 + 2 * i:10 + 2 * i] for i in range(4)])

                def unit(hh, tt):
                    S, sfree = Sr.get()
                    sv_, stf = stat.get()
                    nm, den = sv_[:, 0:1], sv_[:, 1:2]
                    W = 128 * (tt + 1)
                    groups = [[0, 1, 2]] if tt == 0 else [[0, 1], [2]]
                    ds = []
                    for gs in groups:
                        b, free = R.get()
                        for i, g in enumerate(gs):
                            q = qT[:, 2 * g + hh // 2, tt * 128:(tt + 1) * 128]
                            k_ = kz[:, 4 * g + hh, 0:W]
                            o = b[:, i * W:(i + 1) * W]
                            t = p.pe(lambda e, o=o, q=q, k_=k_: e.matmul(o, q, k_, start=True, stop=True), kv, free,
                                     sig=(i == len(gs) - 1))
                        n = len(gs) * W
                        o = S[:, gs[0] * W:gs[0] * W + n]
                        m_ = DM[tt][:, gs[0] * W:gs[0] * W + n]
                        d = p.dve(lambda e, o=o, b=b, m_=m_, n=n: e.scalar_tensor_tensor(
                            o, b[:, 0:n], 0.125, m_, ALU.mult, ALU.add), t, sfree, stf, t_dm, dep=False)
                        R.put(b, [d])
                        ds.append(d)
                    a = soften(S[:, 0:3 * W], 3 * W, ds, nm, den)
                    yield 1
                    PT, pf = Pr.get()
                    vals = [QKV[:, s_, 1536 + (4 * g + hh) * 64:1536 + (4 * g + hh) * 64 + 64]
                            for g in range(3) for s_ in range(tt + 1)]
                    yield from turn_and_weigh(S, 3 * (tt + 1), vals, PT, pf, a, den,
                                              AO[:, tt, hh * 64:(hh + 1) * 64], tq, None)
                    t, d = self_done.pop()
                    Sr.put(S, [t])
                    Pr.put(PT, [t])
                    stat.put(sv_, [d])
                    yield 1

                yield from staggered((unit(hh, tt) for hh in range(4) for tt in range(2)), 3)

            interleave(gates(), attention(), 1)
            ao = p.last("dve")
            tc_ = to_channels(AO, 2, None, yh, yl, [ao])
            tg = p.last("pool")
            attn_done = [p.last("pe"), p.last("act"), p.last("dve"), tg]
            got = [A.get() for _ in range(4)]
            banks, frees = [b for b, _ in got], [f for _, f in got]
            for t in down_like(lambda j: ("mix1", "up", 0), 1,
                               lambda k, tt: (yh[:, k, tt * 128:(tt + 1) * 128], yl[:, k, tt * 128:(tt + 1) * 128]),
                               lambda k: tc_, banks, frees):
                pass
            for tt in range(2):
                for nn in range(2):
                    o = GATE[:, tt, nn * 512:nn * 512 + 512]
                    b = banks[2 * tt + nn]
                    d = p.dve(lambda e, o=o, b=b: e.tensor_tensor(o, o, b, ALU.mult), t[tt], tg, dep=False)
                    A.put(b, [d])
            banks, t = rwkv(rbase, zl, t_zl, xt, shift, attn_done)
            dt_ = [[], []]
            for tt in range(2):
                for nn in range(2):
                    o = GATE[:, tt, 1024 + nn * 512:1024 + nn * 512 + 512]
                    g0 = GATE[:, tt, nn * 512:nn * 512 + 512]
                    b = banks[2 * tt + nn]
                    d = p.dve(lambda e: e.tensor_tensor(o, o, b, ALU.mult), t[tt], tg)
                    A.put(b, [d])
                    dt_[nn].append(p.dve(lambda e: e.tensor_tensor(g0, g0, o, ALU.add), d))
            tm = []
            for nn in range(2):
                tm += to_channels(GATE[:, :, nn * 512:nn * 512 + 512], 4, None, yh, yl, dt_[nn], k0=4 * nn)
            got = [A.get() for _ in range(4)]
            banks, frees = [b for b, _ in got], [f for _, f in got]
            for t in down_like(lambda j: ("mix1", "wo", j), 4,
                               lambda k, tt: (yh[:, k, tt * 128:(tt + 1) * 128], yl[:, k, tt * 128:(tt + 1) * 128]),
                               lambda k: tm[k - k % 2:k - k % 2 + 2], banks, frees):
                pass
            return residual(banks, 1.0, t)

        def rwkv(base, zl, t_zl, xt, shift, start):
            sp = Space(base)
            KZV = [{q: sp.take(2, 256) for q in "kvr"} for _ in range(2)]
            z = [sp.take(2, 257) for _ in range(2)]
            zs = []
            for t_ in z:
                zs.append(p.pool(lambda e: e.memset(t_[:, :, 0:1], 0.0), start))
            kzv_free = [start, start]
            kzv_ready, used, ytok, end = {}, set(), {}, {}

            def projections():
                prev = [None, None]
                for G in range(4):
                    while G >= 2 and not {2 * G - 4, 2 * G - 3} <= used:
                        yield 1
                    for i, q in enumerate("kvr"):
                        d = yield from shift(("mix1", q, G), 2, 128, KZV[G % 2][q],
                                             [3 + 8 * i + 2 * G, 4 + 8 * i + 2 * G], z[i % 2],
                                             [kzv_free[G % 2], prev[i % 2], zs], dfree=kzv_free[G % 2])
                        prev[i % 2] = d
                        kzv_ready[(q, G)] = d

            class Front:

                def __init__(self):
                    self.LW, self.wd, self.aa, self.kp, self.Pi = [sp.take(w_) for w_ in (128, 256, 256, 256, 256)]
                    self.kr, self.wp = sp.take(512), sp.take(512)
                    self.BK = sp.take(512)
                    self.sem = p.new_sem()

            class Whole:

                def __init__(self, n):
                    self.ARz = sp.take(2, 4, 2, 64)
                    self.Bt, self.Kt = sp.take(256), sp.take(256)
                    self.Vz = sp.take(4, 128)
                    self.TB, self.TK = sp.take(4, 128), sp.take(4, 128)
                    self.Gz, self.Uz = sp.take(2, 128), sp.take(2, 128)
                    self.ST = small[:, 48 + 64 * n:112 + 64 * n]
                    self.st = sp.take(32)
                    for t_ in (self.ARz, self.Vz, self.Gz, self.Uz):
                        self.zero = p.pool(lambda e: e.memset(t_, 0.0), start)

            class Rows:

                def __init__(self):
                    self.LG, self.LN = sp.take(2, 128), sp.take(2, 128)
                    self.sem = p.new_sem()

            def everyone():
                return [p.last("pe"), p.last("act"), p.last("dve"), p.last("pool")]

            def room(n):
                while len(R.free) < n:
                    yield 1

            def halves(o, i, *toks):
                for q in range(2):
                    ps = slice(64 * q, 64 * q + 64)
                    oo, ii = o[ps, :, 64 * q:64 * q + 64], i[ps, :, :]
                    a = p.act(lambda e: e.activation(oo, ii, ACT.Copy), toks, dep=False)
                return a

            def group(g):
                while not (fronts.free and wholes.free):
                    yield 1
                F_, prev_f = fronts.get()
                s, prev_s = wholes.get()
                prev = [prev_f, prev_s]
                G, j = g // 2, g % 2
                z0 = s.zero
                u4 = lambda t_: t_.rearrange("p (u k) -> p u k", u=4)
                u2 = lambda t_: t_.rearrange("p (a k) -> p a k", a=2)
                wd, aa, kp, Pi = F_.wd, F_.aa, F_.kp, F_.Pi
                kk, rn, w1, iP = F_.kr[:, 0:256], F_.kr[:, 256:512], F_.wp[:, 0:256], F_.wp[:, 256:512]
                Px = w1
                ARz, Bt, Kt, Vz, TB, TK = s.ARz, s.Bt, s.Kt, s.Vz, s.TB, s.TK
                Gz, Uz, ST, st_ = s.Gz, s.Uz, s.ST, s.st
                bt, kt = F_.BK[:, 0:256], F_.BK[:, 256:512]
                L, Dm, DT, Xc, Xb = u4(aa), u4(wd), TB[:, :, 0:64], u4(kp), u4(F_.BK)
                DTb, LTb = u4(F_.kr), u4(F_.wp)
                Yt, sq = Kt, Bt
                cs = slice(g * 128, g * 128 + 128)
                z1 = p.pool(lambda e: e.memset(w1, 0.0), prev)
                tl = p.dma(F_.LW, lorap[0, :, cs], F_.sem, prev, eng="pool")
                while ("k", G) not in kzv_ready:
                    yield 1
                tk_ = kzv_ready[("k", G)]
                k3 = KZV[G % 2]["k"][:, j, :]
                yield from room(1)
                b, f = R.get()
                o1, o2, l1, l2 = b[:, 0:256], b[:, 256:512], F_.LW[0:64], F_.LW[64:128]
                p.pe(lambda e: e.matmul(o1, l1, zl[0:64, 0, :], start=True, stop=True), t_zl, tl, f, sig=True)
                p.wait("pe", [p.last("pe")])
                t1 = p.pe(lambda e: e.matmul(o2, l2, zl[64:128, 0, :], start=True, stop=True), sig=True)
                yield 1
                a = p.dve(lambda e: e.tensor_scalar(wd, o1, col("w0", g), 0.5, ALU.add, ALU.mult), t1, t_col, prev,
                          dep=False)
                a = p.dve(lambda e: e.tensor_scalar(aa, o2, col("a0", g), 0.5, ALU.add, ALU.mult), dep=False)
                R.put(b, [a])
                p.act(lambda e: e.activation(wd, wd, ACT.Tanh), a, dep=False)
                ta = p.act(lambda e: e.activation(aa, aa, ACT.Tanh), dep=False)
                d = p.dve(lambda e: e.tensor_scalar(kk, k3, col("kk", g), None, ALU.mult), tk_, prev, dep=False)
                a = p.act(lambda e: e.activation(rn, kk, ACT.Square), d, prev, dep=False)
                p.dve(lambda e: e.tensor_scalar(wd, wd, 0.5, 0.5, ALU.mult, ALU.add), ta, dep=False)
                d = p.dve(lambda e: e.tensor_scalar(aa, aa, 0.5, 0.5, ALU.mult, ALU.add), dep=False)
                ew = p.act(lambda e: e.activation(wd, wd, ACT.Exp, scale=DECAY), d, dep=False)
                yield from room(1)
                b, f = R.get()
                for tt in range(2):
                    t = p.pe(lambda e: e.matmul(b[:, tt * 2:tt * 2 + 2], rn[:, tt * 128:(tt + 1) * 128],
                                                con("hsel"), start=True, stop=True), a, f, sig=(tt == 1))
                yield 1
                nrm = st_[:, 16:20]
                d = p.dve(lambda e: e.tensor_scalar(nrm, b[:, 0:4], 1e-24, None, ALU.max), t, dep=False)
                R.put(b, [d])
                hb = con("half")[:, 0:1].to_broadcast([128, 4])
                pw = p.pool(lambda e: e.tensor_tensor(nrm, nrm, hb, ALU.pow), d)
                p.dve(lambda e: e.tensor_scalar(kp, aa, 1.0, col("ka", g), ALU.subtract, ALU.mult))
                tkp = p.dve(lambda e: e.scalar_tensor_tensor(kp, kp, 1.0, k3, ALU.add, ALU.mult))
                wv, w1v, Piv, Pxv = u4(wd), u4(w1), u4(Pi), u4(Px)
                p.dve(lambda e: e.tensor_copy(w1v[:, :, 0:1], wv[:, :, 0:1]), ew, z1, dep=False)
                p.dve(lambda e: e.memset(wv[:, :, 0:1], 0.0))
                p.dve(lambda e: e.tensor_tensor_scan(Pi, wd, w1, 0.0, ALU.mult, ALU.add))
                yield 1
                p.dve(lambda e: e.tensor_copy(Pxv[:, :, 1:64], Piv[:, :, 0:63]))
                p.dve(lambda e: e.memset(Pxv[:, :, 0:1], 1.0), dep=False)
                p.dve(lambda e: e.reciprocal(iP, Pi), dep=False)
                p.dve(lambda e: e.tensor_tensor(kt, kp, iP, ALU.mult))
                wide4, nb4 = u4(rn), nrm.unsqueeze(2).to_broadcast([128, 4, 64])
                sp_ = p.dve(lambda e: e.tensor_copy(wide4, nb4), pw, dep=False)
                pcs = st_[:, 24:28]
                p.dve(lambda e: e.tensor_copy(pcs.unsqueeze(2), Piv[:, :, 63:64]), dep=False)
                yield from room(1)
                b, f = R.get()
                for tt in range(2):
                    trn = transpose(b[:, tt * 128:tt * 128 + 128], rn[:, tt * 128:tt * 128 + 128], sp_, f,
                                    sig=(tt == 1))
                yield 1
                while ("r", G) not in kzv_ready:
                    yield 1
                tv_, tr_ = kzv_ready[("v", G)], kzv_ready[("r", G)]
                v3, r3 = KZV[G % 2]["v"][:, j, :], KZV[G % 2]["r"][:, j, :]
                d = p.dve(lambda e: e.tensor_tensor(kk, kk, b[:, 0:256], ALU.mult), trn, dep=False)
                R.put(b, [d])
                p.dve(lambda e: e.tensor_tensor(bt, kk, aa, ALU.mult))
                p.dve(lambda e: e.tensor_tensor(bt, bt, iP, ALU.mult))
                for hh in range(2):
                    ps = slice(64 * hh, 64 * hh + 64)
                    oa, orr = ARz[ps, hh, :, 0, :], ARz[ps, hh, :, 1, :]
                    ka_, px_, r_, pi_ = u4(kk[ps]), u4(Px[ps]), u4(r3[ps]), u4(Pi[ps])
                    p.dve(lambda e: e.scalar_tensor_tensor(oa, ka_, -1.0, px_, ALU.mult, ALU.mult), z0,
                          dep=(hh == 0))
                    tar = p.dve(lambda e: e.tensor_tensor(orr, r_, pi_, ALU.mult), tr_, dep=False)
                tb_ = p.dve(lambda e: e.scalar_tensor_tensor(rn, r3, col("rk", g), kp, ALU.mult, ALU.mult))
                yield 1
                yield from room(2)
                tt_ = {}
                bonus = st_[:, 20:24]
                for pair in ((("v", v3), ("b", bt)), (("k", kt),)):
                    b, f = R.get()
                    for i, (nm, src) in enumerate(pair):
                        for tt in range(2):
                            t = transpose(b[:, i * 256 + tt * 128:i * 256 + tt * 128 + 128],
                                          src[:, tt * 128:(tt + 1) * 128], tb_, tv_, f, t_c,
                                          sig=(tt == 1 and i == len(pair) - 1))
                    if len(pair) == 2:
                        b4 = b[:, 0:256].rearrange("p (a k) -> p a k", a=2)
                        Vz5 = Vz.rearrange("p (a c) k -> p a c k", c=2)
                        for q in range(2):
                            ps = slice(64 * q, 64 * q + 64)
                            vz = p.act(lambda e: e.activation(Vz5[ps, :, q, :], b4[ps, :, :], ACT.Copy), t, prev, z0,
                                       dep=False)
                        a = p.act(lambda e: e.activation(Bt, b[:, 256:512], ACT.Copy), dep=False)
                        tt_["b"] = a
                    else:
                        for tt in range(2):
                            t = p.pe(lambda e: e.matmul(b[:, 256 + tt * 2:258 + tt * 2], rn[:, tt * 128:(tt + 1) * 128],
                                                        con("hsel"), start=True, stop=True), sig=True)
                        a = p.act(lambda e: e.activation(Kt, b[:, 0:256], ACT.Copy), t, prev, dep=False)
                        tt_["k"] = a
                        a = p.act(lambda e: e.activation(bonus, b[:, 256:260], ACT.Copy), dep=False)
                    R.put(b, [a])
                dbz = p.pool(lambda e: e.memset(F_.kr, 0.0), t)
                ltz = p.pool(lambda e: e.memset(F_.wp, 0.0), tb_)
                used.add(g)
                if used >= {2 * G, 2 * G + 1}:
                    kzv_free[G % 2] = everyone()
                yield from room(3)
                pend = []
                for nm, src, dst in (("b", bt, TB), ("k", kt, TK)):
                    b, f = R.get()
                    for u in range(4):
                        hh, tt = u // 2, u % 2
                        for q in range(2):
                            c = 2 * tt + q
                            o = b[64 * q:64 * q + 64, u * 128:(u + 1) * 128]
                            l_ = src[:, c * 64:(c + 1) * 64]
                            r_ = ARz[:, hh, c, :, :].rearrange("p a t -> p (a t)")
                            t = p.pe(lambda e: e.matmul(o, l_, r_, start=True, stop=True), f, tb_,
                                     sig=(u == 3 and q == 1))
                    pend.append((b, dst, t))
                b, f = R.get()
                for u in range(4):
                    hh, tt = u // 2, u % 2
                    for q in range(2):
                        c = 2 * tt + q
                        o = b[64 * q:64 * q + 64, u * 64:(u + 1) * 64]
                        l_, r_ = ARz[:, hh, c, 0, :], bt[:, c * 64:(c + 1) * 64]
                        t = p.pe(lambda e: e.matmul(o, l_, r_, start=True, stop=True), f, sig=(u == 3 and q == 1))
                yield 1
                m_ = con("mar").unsqueeze(1).to_broadcast([128, 4, 128])
                toks = []
                for bb, dst, t_ in pend:
                    bv = u4(bb)
                    d = p.dve(lambda e: e.tensor_tensor(dst, bv, m_, ALU.mult), t_, prev, dep=False)
                    R.put(bb, [d])
                    toks.append(d)
                t_tb, t_tk = toks
                bv, ml = u4(b[:, 0:256]), con("mlow").unsqueeze(1).to_broadcast([128, 4, 64])
                d = p.dve(lambda e: e.tensor_tensor(L, bv, ml, ALU.mult), t, dep=False)
                R.put(b, [d])
                xz = p.pool(lambda e: e.memset(Xb, 0.0), t)
                LT = TB[:, :, 0:64]
                bc = lambda n: con(n).unsqueeze(1).to_broadcast([128, 4, 64])
                lt = halves(LTb, LT, t_tb, ltz)
                p.dve(lambda e: e.tensor_tensor(Dm, L, bc("m0"), ALU.mult))
                p.dve(lambda e: e.tensor_tensor(DT, LT, bc("m0t"), ALU.mult), lt, dep=False)
                p.dve(lambda e: e.tensor_tensor(Dm, Dm, bc("i64"), ALU.add))
                d = p.dve(lambda e: e.tensor_tensor(DT, DT, bc("i64"), ALU.add), dep=False)
                db = halves(DTb, DT, d, dbz)
                dd = d
                for k in range(1, 6):
                    yield from room(1)
                    b, f = R.get()
                    for u in range(4):
                        t = p.pe(lambda e: e.matmul(b[:, u * 64:(u + 1) * 64], LTb[:, u, :], Dm[:, u, :],
                                                    start=True, stop=True), f, lt, dd, sig=(u == 3))
                    bv = u4(b[:, 0:256])
                    yield 1
                    xc = p.dve(lambda e: e.tensor_tensor(Xc, bv, bc(f"m{k}"), ALU.mult), t, dep=False)
                    R.put(b, [xc])
                    xb = halves(Xb, Xc, xc, xz, db)
                    yield from room(2)
                    if k < 5:
                        b, f = R.get()
                        for u in range(4):
                            t = p.pe(lambda e: e.matmul(b[:, u * 64:(u + 1) * 64], DTb[:, u, :], Xc[:, u, :],
                                                        start=True, stop=True), f, db, xc, sig=(u == 3))
                    b2, f = R.get()
                    for u in range(4):
                        t2 = p.pe(lambda e: e.matmul(b2[:, u * 64:(u + 1) * 64], Xb[:, u, :], DT[:, u, :],
                                                     start=True, stop=True), f, xb, sig=(u == 3))
                    yield 1
                    if k < 5:
                        bv = u4(b[:, 0:256])
                        dd = p.dve(lambda e: e.tensor_tensor(Dm, Dm, bv, ALU.add), t, dep=False)
                        R.put(b, [dd])
                    bv = u4(b2[:, 0:256])
                    d = p.dve(lambda e: e.tensor_tensor(DT, DT, bv, ALU.add), t2, dep=False)
                    R.put(b2, [d])
                    if k < 5:
                        db = halves(DTb, DT, d)
                t_inv = d
                fronts.put(F_, everyone())
                while not rowsets.free:
                    yield 1
                W_, prev_w = rowsets.get()
                p.dma(W_.LG, lorap[1:3, :, cs].rearrange("a p n -> p a n"), W_.sem, prev_w, eng="pool")
                tl = p.dma(W_.LN, rows[1:3, cs].unsqueeze(0).to_broadcast([128, 2, 128]), W_.sem, eng="pool")
                s_tok = None
                for c in range(4):
                    tt, q = c // 2, c % 2
                    ps = slice(64 * q, 64 * q + 64)
                    yield from room(2 - q)
                    if q == 0:
                        yb, yf = R.get()
                    b, f = R.get()
                    for hh in range(2):
                        o = b[ps, hh * 64:(hh + 1) * 64]
                        u = hh * 2 + tt
                        if c:
                            p.pe(lambda e: e.matmul(o, ARz[:, hh, c, 0, :], ST, start=True, stop=False), f, s_tok)
                        t = p.pe(lambda e: e.matmul(o, TK[:, u, 0:64], Vz[:, c, hh * 64:(hh + 1) * 64],
                                                    start=(c == 0), stop=True), f, vz, t_tk, sig=(hh == 1))
                    for hh in range(2):
                        o = yb[ps, hh * 64:(hh + 1) * 64]
                        u = hh * 2 + tt
                        if c:
                            p.pe(lambda e: e.matmul(o, ARz[:, hh, c, 1, :], ST, start=(hh == 0), stop=False,
                                                    skip_group_check=True), yf)
                        t_y = p.pe(lambda e: e.matmul(o, TK[:, u, 64:128], Vz[:, c, hh * 64:(hh + 1) * 64],
                                                      start=(c == 0 and hh == 0), stop=False,
                                                      skip_group_check=True), yf, sig=(hh == 1))
                    yield 1
                    gd = p.act(lambda e: e.activation(Gz[ps, q, :], b[ps, 0:128], ACT.Copy), t, z0, prev, dep=False)
                    R.put(b, [gd])
                    yield from room(1)
                    b, f = R.get()
                    for hh in range(2):
                        o = b[ps, hh * 64:(hh + 1) * 64]
                        u = hh * 2 + tt
                        t = p.pe(lambda e: e.matmul(o, DT[:, u, :], Gz[:, q, hh * 64:(hh + 1) * 64], start=True,
                                                    stop=True), f, gd, t_inv, sig=(hh == 1))
                    yield 1
                    ud = p.act(lambda e: e.activation(Uz[ps, q, :], b[ps, 0:128], ACT.Copy), t, z0, prev, dep=False)
                    R.put(b, [ud])
                    yield from room(1)
                    if c < 3:
                        b, f = R.get()
                        for hh in range(2):
                            o = b[64 * hh:64 * hh + 64, 0:64]
                            hc = slice(tt * 128 + hh * 64, tt * 128 + hh * 64 + 64)
                            p.pe(lambda e: e.matmul(o, Bt[:, hc], Uz[:, q, hh * 64:(hh + 1) * 64], start=True,
                                                    stop=False), f, ud, tt_["b"])
                            t = p.pe(lambda e: e.matmul(o, Kt[:, hc], Vz[:, c, hh * 64:(hh + 1) * 64], start=False,
                                                        stop=True), tt_["k"], sig=(hh == 1))
                    for hh in range(2):
                        o = yb[ps, hh * 64:(hh + 1) * 64]
                        u = hh * 2 + tt
                        ty = p.pe(lambda e: e.matmul(o, TB[:, u, 64:128], Uz[:, q, hh * 64:(hh + 1) * 64],
                                                     start=False, stop=True, skip_group_check=True), ud, t_tb,
                                  sig=(hh == 1))
                    yield 1
                    if c < 3:
                        bv = b[:, 0:64]
                        pc = st_[:, 24 + c:25 + c]
                        if c:
                            p.dve(lambda e: e.tensor_tensor(ST, ST, bv, ALU.add), t, t_y, dep=False)
                            s_tok = p.dve(lambda e: e.tensor_scalar(ST, ST, pc, None, ALU.mult))
                        else:
                            s_tok = p.dve(lambda e: e.tensor_scalar(ST, bv, pc, None, ALU.mult), t, prev, dep=False)
                        R.put(b, [s_tok])
                    if q == 1:
                        yd = p.act(lambda e: e.activation(Yt[:, tt * 128:(tt + 1) * 128], yb[:, 0:128], ACT.Copy),
                                   ty, tt_["k"], dep=False)
                        R.put(yb, [yd])
                y4, s4 = u4(Yt), u4(sq)
                mean, var = st_[:, 0:4], st_[:, 4:8]
                mb = mean.unsqueeze(2).to_broadcast([128, 4, 64])
                vb = var.unsqueeze(2).to_broadcast([128, 4, 64])
                p.dve(lambda e: e.tensor_reduce(mean, y4, AX, ALU.add), yd)
                p.dve(lambda e: e.tensor_scalar(mean, mean, 1.0 / 64, None, ALU.mult))
                d = p.dve(lambda e: e.tensor_tensor(y4, y4, mb, ALU.subtract))
                a = p.act(lambda e: e.activation(s4, y4, ACT.Square), d, dep=False)
                yield from room(1)
                b1, f1 = R.get()
                for tt in range(2):
                    o = b1[:, tt * 128:(tt + 1) * 128]
                    p.pe(lambda e: e.matmul(o, zl[:, 1, tt * 128:(tt + 1) * 128], W_.LG[:, 0, :], start=True,
                                            stop=False), f1, tl)
                    t2 = p.pe(lambda e: e.matmul(o, zl[:, 2, tt * 128:(tt + 1) * 128], W_.LG[:, 1, :], start=False,
                                                 stop=True), sig=(tt == 1))
                yield 1
                d = p.dve(lambda e: e.tensor_reduce(var, s4, AX, ALU.add), a, dep=False)
                p.pool(lambda e: e.tensor_scalar(var, var, 1.0 / 64, 64e-5, ALU.mult, ALU.add), d)
                h8 = con("half")[:, 0:1].to_broadcast([128, 4])
                pw = p.pool(lambda e: e.tensor_tensor(var, var, h8, ALU.pow))
                yield 1
                p.dve(lambda e: e.tensor_tensor(y4, y4, vb, ALU.mult), pw, dep=False)
                for q in range(2):
                    ps = slice(64 * q, 64 * q + 64)
                    for tt in range(2):
                        o = sq[ps, tt * 128:(tt + 1) * 128].rearrange("p (h k) -> p h k", h=2)
                        v_ = Vz[ps, 2 * tt + q, :].rearrange("p (h k) -> p h k", h=2)
                        bs = bonus[ps, 2 * tt:2 * tt + 2].unsqueeze(2).to_broadcast([64, 2, 64])
                        p.dve(lambda e: e.tensor_tensor(o, v_, bs, ALU.mult), dep=False)
                lw = W_.LN[:, 0:1, :].to_broadcast([128, 2, 128])
                lb_ = W_.LN[:, 1:2, :].to_broadcast([128, 2, 128])
                y2 = u2(Yt)
                p.dve(lambda e: e.tensor_tensor(y2, y2, lw, ALU.mult), tl)
                p.dve(lambda e: e.tensor_tensor(y2, y2, lb_, ALU.add))
                p.dve(lambda e: e.tensor_tensor(Yt, Yt, sq, ALU.add))
                d = p.dve(lambda e: e.tensor_tensor(Yt, Yt, b1[:, 0:256], ALU.mult), t2)
                R.put(b1, [d])
                ytok[g] = to_channels(y2, 1, None, yh, yl, [d], k0=g)
                wholes.put(s, everyone())
                rowsets.put(W_, everyone())
                yield 1

            fronts, wholes = Ring([Front(), Front()]), Ring([Whole(n) for n in range(3)])
            rowsets = Ring([Rows(), Rows()])
            for r_ in (fronts, wholes, rowsets):
                r_.free = [(m, [start]) for m, _ in r_.free]

            def outward():
                while not all(g in ytok for g in range(6)):
                    yield 1
                yield from room(5)
                got = [A.get() for _ in range(4)]
                end["banks"], frees = [b for b, _ in got], [f for _, f in got]
                dn = down_like(lambda j: ("mix1", "wout", j), 4,
                               lambda k, tt: (yh[:, k, tt * 128:(tt + 1) * 128], yl[:, k, tt * 128:(tt + 1) * 128]),
                               lambda k: ytok[k], end["banks"], frees, fine=True)
                for _ in range(3):
                    while next(dn) is None:
                        yield 1
                    yield 1
                while not all(g in ytok for g in range(8)):
                    yield 1
                for t in dn:
                    end["t"] = t

            together(projections(), staggered((group(g) for g in range(8)), 3), outward())
            return end["banks"], end["t"]

        def mix2(l, xtok):
            xt = norm_channels(f"mix_norm_2{l}", xtok, None)
            after = [p.last("pe"), p.last("act"), p.last("dve")]
            sp = Space()
            PJ = sp.take(2, NIN2)
            EB = sp.take(6, 256)
            AK = sp.take(6, 256)
            BK = sp.take(5, 256)
            CK = sp.take(5, 256)
            IK = sp.take(4, 256)
            AQ, BQ, CQ, IQ = sp.take(3, 256), sp.take(3, 256), sp.take(5, 256), sp.take(2, 256)
            QF = sp.take(2, 480)
            KVF = sp.take(2, 640)
            KF = sp.take(2, 480)
            IKr = sp.take(2, 512)
            sc2 = sp.take(2, 384)
            OUT = GATE[:, 0, 0:2048].rearrange("p (t d) -> p t d", t=2)
            IXW = GATE[:, 1, 0:2048]
            MB = [sp.take(128), sp.take(256)]
            SC = sp.take(256)
            lots = []
            for t_ in (sc2, QF, KF):
                flat = t_.rearrange("p a b -> p (a b)")
                lots += [flat[:, 256 * i:256 * i + 256] for i in range(3)]
            flat = IKr.rearrange("p a b -> p (a b)")
            more = [flat[:, 256 * i:256 * i + 256] for i in range(4)]
            CM = [sp.take(128), sp.take(256)]
            sem = p.new_sem()
            t_eb = p.dma(EB, bass.AP(ebias.tensor, ebias[l, 0, 0:1].offset, [[1, 128], [384, 6], [1, 256]]), sem, after, eng="pool")
            zz = [p.pool(lambda e, t_=t_: e.memset(t_, 0.0), after) for t_ in (IKr, CM[0], CM[1], BK)]
            zz.append(p.pool(lambda e: e.memset(CM[0][0:64, 64:128], NEG)))
            zz.append(p.pool(lambda e: e.memset(CM[1][0:64, 192:256], NEG)))

            ptok, end = {}, {}

            def proj(j):
                keys = [(l, "in2", 12)] if j == 6 else [(l, "in2", 2 * j), (l, "in2", 2 * j + 1)]

                def evac(tt, b, t):
                    o = PJ[:, tt, j * 512:j * 512 + b.shape[1]]
                    end["x"] = t
                    ptok[j] = p.act(lambda e: e.activation(o, b, ACT.Copy), t, after, dep=False)
                    return ptok[j]
                yield from proj_b(keys, xt, evac)
                assert j in ptok

            for j in (6, 4, 5):
                for _ in proj(j):
                    pass

            lat = {}

            def latents():
                kff = KF.rearrange("p a b -> p (a b)")[:, 0:512].rearrange("p (a b) -> p a b", a=2)
                got = []
                for i, (c0, w, buf) in enumerate(((2408, 384, sc2), (2792, 256, kff))):
                    ss = small[:, 2 * i:2 * i + 2]
                    ts = []
                    for tt in range(2):
                        src, o, acc = PJ[:, tt, c0:c0 + w], buf[:, tt, :], small[:, 2 * i + tt:2 * i + tt + 1]
                        ts.append(p.act(lambda e: e.activation(o, src, ACT.Square, accum_out=acc), ptok[5], ptok[4],
                                        ptok[6], after))
                    got.append(rstd(ss, 2, w, 1e-6, ts))
                yield 1
                yield 1
                nrm = []
                for i, (c0, w, buf) in enumerate(((2408, 384, sc2), (2792, 256, kff))):
                    for tt in range(2):
                        o, src, s_ = buf[:, tt, :], PJ[:, tt, c0:c0 + w], small[:, 2 * i + tt:2 * i + tt + 1]
                        if tt:
                            a = p.act(lambda e: e.activation(o, src, ACT.Copy, scale=s_), got[i], dep=False)
                        else:
                            d = p.dve(lambda e: e.tensor_scalar(o, src, s_, None, ALU.mult), got[i], dep=False)
                    nrm.append([a, d])
                yield 1
                yield 1
                lat["uq"] = to_channels(sc2, 3, f"cq{l}", yh, yl, nrm[0], k0=0)
                yield 1
                lat["ukv"] = to_channels(kff, 2, f"ckv{l}", yh, yl, nrm[1], k0=3)
                yield 1

            together(latents(), proj(3))
            t = None
            up = {}
            for nm, nk, k0, w, dst in (("uq", 3, 0, 480, QF), ("ukv", 2, 3, 640, KVF)):
                hi, lo, wt = take((l, nm, 0))
                for tt in range(2):
                    cw = w if w <= 512 else w // 2
                    for c0 in range(0, w, cw):
                        b, f = R.get()
                        for k in range(nk):
                            lh, ll = yh[:, k0 + k, tt * 128:(tt + 1) * 128], yl[:, k0 + k, tt * 128:(tt + 1) * 128]
                            t = mm3(b[:, 0:cw], lh, ll, hi[:, k * w + c0:k * w + c0 + cw],
                                    lo[:, k * w + c0:k * w + c0 + cw], k == 0, k == nk - 1, [wt, lat[nm], f],
                                    sig=(k == nk - 1))
                        o = dst[:, tt, c0:c0 + cw]
                        a = p.act(lambda e: e.activation(o, b[:, 0:cw], ACT.Copy), t, after, dep=False)
                        R.put(b, [a])
                done(t)
                up[nm] = a
            def turned(src, w, parts, toks, eng="act"):
                b, f = R.get()
                for tt in range(2):
                    t = transpose(b[0:w, tt * 128:(tt + 1) * 128], src(tt), toks, f, t_c, sig=(tt == 1))
                c = None
                for dst, r0, n in parts:
                    o, i_ = dst[r0:r0 + n], b[r0:r0 + n, 0:256]
                    if eng == "act":
                        c = p.act(lambda e: e.activation(o, i_, ACT.Copy), t, zz, after, dep=False)
                    else:
                        c = p.dve(lambda e: e.tensor_copy(o, i_), t, zz, after, dep=False)
                R.put(b, [c])
                return c

            Sr, Pr = Ring([]), Ring([])
            stat = Ring([small[:, 8 + 2 * i:10 + 2 * i] for i in range(8)])
            kt_, mtok = {}, {}

            def unit(kind, h, tt):
                S, sfree = Sr.get()
                sv_, stf = stat.get()
                nm, den = sv_[:, 0:1], sv_[:, 1:2]
                W = 128 * (tt + 1)
                sl = slice(tt * 128, (tt + 1) * 128)
                b, f = R.get()
                sw = S[:, 0:W]
                tk_ = kt_[(kind, h)]
                if kind == "a":
                    p.pe(lambda e: e.matmul(b[:, 0:W], AQ[:, h // 2, sl], AK[:, h, 0:W], start=True, stop=True),
                         f, tk_)
                    for kt2 in range(tt + 1):
                        lh = EB[:, h, 128 * (tt - kt2):128 * (tt - kt2) + 128]
                        t = p.pe(lambda e: e.matmul(b[:, 256 + kt2 * 128:384 + kt2 * 128], lh, con("anti"),
                                                    start=True, stop=True), t_eb, sig=(kt2 == tt))
                    cm = CM[tt]
                    d0 = p.dve(lambda e: e.scalar_tensor_tensor(sw, b[:, 0:W], 0.125, cm, ALU.mult, ALU.add), t,
                               sfree, stf, zz, dep=False)
                    d = p.dve(lambda e: e.tensor_tensor(sw, sw, b[:, 256:256 + W], ALU.add), d0)
                    v = [PJ[:, s_, 768 + h * 64:768 + (h + 1) * 64] for s_ in range(tt + 1)]
                    vt = [ptok[1], ptok[2]]
                    oc = h * 64
                elif kind == "b":
                    t = p.pe(lambda e: e.matmul(b[:, 0:W], BQ[0:bk(h), h // 2, sl], BK[0:bk(h), h, 0:W], start=True,
                                                stop=True), f, tk_, sig=True)
                    mb = MB[tt]
                    d = p.dve(lambda e: e.scalar_tensor_tensor(sw, b[:, 0:W], 0.125, mb, ALU.mult, ALU.add), t,
                              sfree, stf, mtok[tt], dep=False)
                    v = [PJ[:, s_, 1792 + h * 64:1792 + (h + 1) * 64] for s_ in range(tt + 1)]
                    vt = [ptok[3], ptok[4]]
                    oc = 384 + h * 64
                else:
                    t = p.pe(lambda e: e.matmul(b[:, 0:W], CQ[0:96, h, sl], CK[0:96, h, 0:W], start=True, stop=True),
                             f, tk_, sig=True)
                    cm = CM[tt]
                    d = p.dve(lambda e: e.scalar_tensor_tensor(sw, b[:, 0:W], 96 ** -0.5, cm, ALU.mult, ALU.add), t,
                              sfree, stf, zz, dep=False)
                    v = [KVF[:, s_, h * 128 + 64:h * 128 + 128] for s_ in range(tt + 1)]
                    vt = [up["ukv"]]
                    oc = 704 + h * 64
                R.put(b, [d])
                a = soften(sw, W, [d], nm, den)
                yield 1
                PT, pf = Pr.get()
                yield from turn_and_weigh(S, tt + 1, v, PT, pf, a, den, OUT[:, tt, oc:oc + 64], vt, after)
                t, d = self_done.pop()
                Sr.put(S, [t])
                Pr.put(PT, [t])
                stat.put(sv_, [d])
                yield 1

            def bk(h):
                return 64 if h == 4 else 128

            head_done, ak = {}, {}

            def latent_heads():
                kr_ = []
                for tt in range(2):
                    P_ = PJ[:, tt, :]
                    tmp = AQ.rearrange("p a b -> p (a b)")
                    tk = rope(P_[:, 3048:3080], P_[:, 3048:3080], tt, 1, 32, 0, 16, "r32", tmp,
                              [ptok[5], ptok[6], after])
                    tq = rope(QF[:, tt, :], QF[:, tt, :], tt, 5, 96, 64, 16, "r32", tmp, [up["uq"]])
                    kf = KF[:, tt, :].rearrange("p (h d) -> p h d", d=96)
                    kn = KVF[:, tt, :].rearrange("p (h d) -> p h d", d=128)[:, :, 0:64]
                    kr = P_[:, 3048:3080].unsqueeze(1).to_broadcast([128, 5, 32])
                    p.pool(lambda e: e.tensor_copy(kf[:, :, 0:64], kn), up["ukv"], after)
                    kr_.append(p.pool(lambda e: e.tensor_copy(kf[:, :, 64:96], kr), tk))
                    yield 1
                for j in range(5):
                    turned(lambda tt: QF[:, tt, 96 * j:96 * j + 96], 96, [(CQ[:, j, :], 0, 96)], [tq, up["uq"]])
                    kt_[("c", j)] = turned(lambda tt: KF[:, tt, 96 * j:96 * j + 96], 96, [(CK[:, j, :], 0, 96)], kr_)
                    yield 1
                for i, a_ in enumerate(lots):
                    (Sr if i < 5 else Pr).put(a_, [kt_[("c", 4)]])
                yield from staggered((unit("c", h, tt) for h in range(5) for tt in range(2)), 3)
                head_done["c"] = p.last("dve")
                while not (0 in ptok and "z" in ak):
                    yield 1
                for j in range(3):
                    turned(lambda tt: PJ[:, tt, 128 * j:128 * j + 128], 128, [(AQ[:, j, :], 0, 128)], [ptok[0]])
                    c = turned(lambda tt: PJ[:, tt, 384 + 128 * j:512 + 128 * j], 128,
                               [(AK[:, 2 * j, :], 0, 64), (AK[:, 2 * j + 1, :], 64, 64)],
                               [ptok[0], ptok[1], ak["z"]])
                    kt_[("a", 2 * j)] = kt_[("a", 2 * j + 1)] = c
                    yield 1
                yield from staggered((unit("a", h, tt) for h in (5, 4, 3, 2, 1, 0) for tt in range(2)), 4)
                head_done["a"] = p.last("dve")

            def indexed_heads():
                for tt in range(2):
                    P_ = PJ[:, tt, :]
                    tr = rope(P_[:, 2112:2400], P_[:, 2112:2400], tt, 9, 32, 0, 16, "r32", IXW, [ptok[4], after])
                    for j in range(4):
                        o = IKr[:, tt, j * 128 + 32 * j:j * 128 + 32 * j + 32]
                        tk = p.pool(lambda e: e.tensor_copy(o, P_[:, 2368:2400]), tr)
                    yield 1
                for j in range(2):
                    turned(lambda tt: PJ[:, tt, 2112 + 128 * j:2240 + 128 * j], 128, [(IQ[:, j, :], 0, 128)], [tr])
                for j in range(4):
                    ti = turned(lambda tt: IKr[:, tt, 128 * j:128 * j + 128], 128, [(IK[:, j, :], 0, 128)], [tk])
                    yield 1
                free = [tr]
                for tt in range(2):
                    free = yield from index(tt, ti, free)
                while not (("b", 4) in kt_ and ("c", 4) in kt_):
                    yield 1
                for i, a_ in enumerate(more):
                    (Sr if i < 1 else Pr).put(a_, [ti])
                yield from staggered((unit("b", h, tt) for h in range(5) for tt in range(2)), 3)
                head_done["b"] = p.last("dve")

            def sparse_rows():
                while not (2 in ptok and 3 in ptok):
                    yield 1
                for tt in range(2):
                    P_ = PJ[:, tt, :]
                    tr = rope(P_[:, 1152:1792], P_[:, 1152:1792], tt, 10, 64, 0, 32, "r64", AK.rearrange("p a b -> p (a b)"),
                              [ptok[2], ptok[3], after])
                    yield 1
                ak["z"] = p.pool(lambda e: e.memset(AK, 0.0), tr)
                for j in range(3):
                    w = 128 if j < 2 else 64
                    turned(lambda tt: PJ[:, tt, 1152 + 128 * j:1152 + 128 * j + w], w, [(BQ[:, j, :], 0, w)], [tr])
                    c = turned(lambda tt: PJ[:, tt, 1472 + 128 * j:1472 + 128 * j + w], w,
                               [(BK[:, 2 * j, :], 0, 64)] + ([(BK[:, 2 * j + 1, :], 64, 64)] if w == 128 else []),
                               [tr])
                    kt_[("b", 2 * j)] = kt_[("b", 2 * j + 1)] = c
                    yield 1

            def index(tt, ti, free):
                W = 128 * (tt + 1)
                sl = slice(tt * 128, (tt + 1) * 128)
                iv = IXW[:, 0:8 * W].rearrange("p (h w) -> p h w", h=8)
                nb = 512 // W
                for h0 in range(0, 8, nb):
                    b, f = R.get()
                    for i in range(nb):
                        h = h0 + i
                        o = b[:, i * W:(i + 1) * W]
                        q, k_ = IQ[:, h // 4, sl], IK[:, h % 4, 0:W]
                        t = p.pe(lambda e: e.matmul(o, q, k_, start=True, stop=True), f, ti, sig=(i == nb - 1))
                    o = IXW[:, h0 * W:h0 * W + 512]
                    a = p.act(lambda e: e.activation(o, b, ACT.Relu, scale=32 ** -0.5), t, free, dep=False)
                    R.put(b, [a])
                    yield 1
                iw = PJ[:, tt, 2400:2408]
                ws = small[:, 32:40]
                p.dve(lambda e: e.tensor_scalar(ws, iw, 8 ** -0.5, None, ALU.mult), ptok[4])
                wb = ws.unsqueeze(2).to_broadcast([128, 8, W])
                p.dve(lambda e: e.tensor_tensor(iv, iv, wb, ALU.mult), a)
                p.dve(lambda e: e.tensor_tensor(iv[:, 0:4, :], iv[:, 0:4, :], iv[:, 4:8, :], ALU.add))
                yield 1
                p.dve(lambda e: e.tensor_tensor(iv[:, 0:2, :], iv[:, 0:2, :], iv[:, 2:4, :], ALU.add))
                s_ = SC[:, 0:W]
                free = [p.dve(lambda e: e.tensor_tensor(s_, iv[:, 0, :], iv[:, 1, :], ALU.add), after)]
                p.dve(lambda e: e.memset(SC[0:64, W - 64:W], NEG))
                yield 1
                m8 = small[:, 40:48]
                for r in range(8):
                    p.dve(lambda e: e.max(m8, s_))
                    p.dve(lambda e: e.match_replace(s_, m8, s_, -3e38))
                    if r % 2:
                        yield 1
                p.dve(lambda e: e.tensor_scalar(s_, s_, -2e38, NEG, ALU.is_ge, ALU.mult))
                mb, cm = MB[tt], CM[tt]
                mtok[tt] = p.dve(lambda e: e.tensor_tensor(mb, s_, cm, ALU.add), zz)
                yield 1
                return free

            def products():
                for j in (2, 1, 0):
                    yield from proj(j)
                while not ("b" in head_done and "c" in head_done):
                    yield 1
                to = {}
                for k0 in (4, 6):
                    c = to_channels(OUT[:, :, k0 * 128:k0 * 128 + 256], 2, None, xh, xl,
                                    [head_done["b"], head_done["c"], end["x"]], k0=k0)
                    to[k0] = to[k0 + 1] = c
                got = [A.get() for _ in range(4)]
                banks, frees = [b for b, _ in got], [f for _, f in got]
                dn = down_like(lambda j: (l, "wout2", j), 4,
                               lambda k, tt: (xh[:, k, tt * 128:(tt + 1) * 128], xl[:, k, tt * 128:(tt + 1) * 128]),
                               lambda k: to[k], banks, frees, order=[2, 3, 1, 0], fine=True)
                n = 0
                while n < 2:
                    if next(dn) is not None:
                        n += 1
                    yield 1
                while "a" not in head_done:
                    yield 1
                for k0 in (2, 0):
                    c = to_channels(OUT[:, :, k0 * 128:k0 * 128 + 256], 2, None, xh, xl, [head_done["a"]], k0=k0)
                    to[k0] = to[k0 + 1] = c
                for t in dn:
                    if t is not None:
                        end["t"] = t
                end["banks"] = banks

            together(products(), latent_heads(), indexed_heads(), sparse_rows())
            return residual(end["banks"], 1.0, end["t"])

        def final(row, xtok, inplace=True):
            sp = Space()
            xn = sp.take(2, 1024)
            gr = sp.take(1024)
            g = p.dma(gr, rows[row:row + 1, 0:1024].to_broadcast([128, 1024]), p.new_sem(), xtok, eng="pool")
            r = sumsq(X, 1024, xn, xtok)
            ds = []
            for tt in range(2):
                o, s_ = X[:, tt, :], small[:, tt:tt + 1]
                d = p.dve(lambda e, o=o, s_=s_: e.scalar_tensor_tensor(o, o, s_, gr, ALU.mult, ALU.mult), r[tt],
                          g, dep=False)
                ds.append(d)
            return ds

        xtok = [t_x, t_x]
        for s in stages:
            if s[0] == "ffn":
                xtok = ffn(s[1], s[2], xtok)
            elif s[0] == "mix1":
                xtok = mix1(xtok)
            elif s[0] == "mix2":
                xtok = mix2(s[1], xtok)
            else:
                xtok = final(s[1], xtok)
        s_out = p.new_sem()
        for tt in range(2):
            t = p.dma(out[tt * 128:(tt + 1) * 128], X[:, tt, :], s_out, xtok[tt])
        p.wait("sp", [t])

        block = ctx.enter_context(nc.Block())

        @block.sync
        def _(e):
            for f in p.q["sp"]:
                f(e)

        @block.tensor
        def _(e):
            for f in p.q["pe"]:
                f(e)

        @block.scalar
        def _(e):
            for f in p.q["act"]:
                f(e)

        @block.vector
        def _(e):
            for f in p.q["dve"]:
                f(e)

        @block.gpsimd
        def _(e):
            for f in p.q["pool"]:
                f(e)


STAGES = [("ffn", "f1", "ffn1_norm"), ("mix1",), ("ffn", "f2", "ffn2_norm"), ("final", 3),
          ("ffn", "f3", "ffn1_norm_20"), ("mix2", 0), ("ffn", "f4", "ffn2_norm_20"),
          ("ffn", "f5", "ffn1_norm_21"), ("mix2", 1), ("ffn", "f6", "ffn2_norm_21"), ("final", 4)]


def kernel(**inputs):
    import concourse.bacc as bacc
    from concourse.bass_utils import run_bass_kernel_spmd

    I = {k: np.asarray(v) for k, v in inputs.items()}
    w_in = I["w_in"][0]
    ffns = {"f1": ("ffn1", "", 0), "f2": ("ffn2", "", 0), "f3": ("ffn1", "_2", 0), "f4": ("ffn2", "_2", 0),
            "f5": ("ffn1", "_2", 1), "f6": ("ffn2", "_2", 1)}
    AW, RS = 2304, 3360

    def rows_of(w):
        return w.reshape(w.shape[0] // 128, 128, w.shape[1]).transpose(1, 0, 2)

    def block(c):
        who, what, j, w = c
        if what in ("gu", "down"):
            n, sfx, l = ffns[who]
            if what == "gu":
                a = [rows_of(I[f"{n}_w_{g}{sfx}"][l][:, j * 128:(j + 1) * 128]) for g in ("gate", "up")]
                return np.stack(a, 1)
            return rows_of(I[f"{n}_w_down{sfx}"][l][j * 256:(j + 1) * 256])
        if who == "mix1":
            if what == "lora":
                c0 = AW + 3072 + 256 * j
                if j == 1:
                    return rows_of(np.pad(w_in[:, c0:c0 + 32], ((0, 0), (0, 96))))
                return rows_of(w_in[:, c0:c0 + 256])
            if what == "qkv":
                if j == 8:
                    return rows_of(w_in[:, 2048:2304])
                return rows_of(w_in[(j % 2) * 512:(j % 2) * 512 + 512, (j // 2) * 512:(j // 2) * 512 + 512])
            if what == "gate":
                c0 = AW + RS + (j // 2) * 512
                return rows_of(w_in[(j % 2) * 512:(j % 2) * 512 + 512, c0:c0 + 512])
            if what == "up":
                return rows_of(I["attn_w_up"][0])
            if what in "kvr":
                c0 = AW + {"r": 0, "k": 1024, "v": 2048}[what] + 256 * j
                return rows_of(w_in[:, c0:c0 + 256])
            return rows_of(I["rwkv_w_out" if what == "wout" else "w_o"][0][j * 256:(j + 1) * 256])
        if what == "in2":
            wi = I["w_in_2"][who]
            if j == 12:
                return rows_of(wi[:, 3072:3080])
            return rows_of(wi[(j % 2) * 512:(j % 2) * 512 + 512, (j // 2) * 512:(j // 2) * 512 + 512])
        if what == "uq":
            return rows_of(I["c_w_uq_2"][who])
        if what == "ukv":
            return rows_of(I["c_w_ukv_2"][who])
        return rows_of(I["w_out_2"][who][j * 256:(j + 1) * 256])

    chunks = plan(STAGES)
    wall = np.empty(sum(128 * c[3] for c in chunks), np.float32)
    at = 0
    for c in chunks:
        n = 128 * c[3]
        wall[at:at + n].reshape(128, -1)[:] = block(c).reshape(128, -1)
        at += n

    clay, NCOL = col_layout()
    cols = np.zeros((128, NCOL), np.float32)

    def put(name, v, at=0):
        a, w = clay[name]
        n = v.size // 128
        cols[:, a + at:a + at + n] = v.reshape(n, 128).T

    for n in ("ffn1_norm", "mix_norm", "ffn2_norm"):
        put(n, I[n][0])
        for l in range(2):
            put(f"{n}_2{l}", I[n + "_2"][l])
    mu = I["rwkv_mu"][0]
    put("mu", mu[3072:3328], 0)
    cols[0:32, clay["mu"][0] + 2] = mu[3328:3360]
    for i, o in enumerate((1024, 2048, 0)):
        put("mu", mu[o:o + 1024], 3 + 8 * i)
    for n, k in (("w0", "rwkv_w0"), ("a0", "rwkv_a0"), ("kk", "rwkv_k_k"), ("ka", "rwkv_k_a"), ("rk", "rwkv_r_k")):
        put(n, I[k][0].reshape(-1))
    for l in range(2):
        put(f"cq{l}", I["c_q_norm_2"][l])
        put(f"ckv{l}", I["c_kv_norm_2"][l])
    rows = np.zeros((5, 2048), np.float32)
    rows[0] = I["gate_bias"][0]
    rows[1, :1024], rows[2, :1024] = I["rwkv_ln_w"][0], I["rwkv_ln_b"][0]
    rows[3, :1024], rows[4, :1024] = I["final_norm"], I["final_norm_2"]
    lorap = np.zeros((3, 128, 1024), np.float32)
    lorap[0, :64], lorap[0, 64:] = I["rwkv_w2"][0], I["rwkv_a2"][0]
    lorap[1], lorap[2, :32] = I["rwkv_g2"][0][:128], I["rwkv_g2"][0][128:]
    ebias = I["a_rel_bias_2"][:, :, np.clip(np.arange(384) - 127, -63, 128) + 63]

    arrays = {"x": np.ascontiguousarray(I["x"][0]), "wall": wall, "consts": const_table()[1], "cols": cols,
              "rows": rows, "lorap": lorap, "ebias": np.ascontiguousarray(ebias)}
    nc = bacc.Bacc("TRN2", target_bir_lowering=False, num_devices=1)
    aps = [nc.dram_tensor(n, a.shape, mybir.dt.from_np(a.dtype), kind="ExternalInput").ap() for n, a in arrays.items()]
    o = nc.dram_tensor("out", (256, 1024), F32, kind="ExternalOutput").ap()
    build(nc, STAGES, *aps, o)
    r = run_bass_kernel_spmd(nc, [arrays], core_ids=[0])
    return r.results[0]["out"].reshape(1, 256, 1024)
```
